# Optimizing a Trainium2 kernel written in Bass

```python
import math
import jax, jax.numpy as jnp
from jax import lax
import numpy as np

D_MODEL = 1024
BATCH = 1
SEQ = 256
DEPTH = 2
DEC_BATCH = 8
DEC_SEQ = 1
PAST_LEN = 2048
PAGE_SIZE = 128

S5_WIDTH = D_MODEL // 2
S5_GROUP = 16
S5_GROUPS = S5_WIDTH // S5_GROUP
S5_STATE = 64
GDN_HEAD_DIM = 128
GDN_WIDTH = D_MODEL // 2
GDN_HEADS = GDN_WIDTH // GDN_HEAD_DIM
GDN_CONV = 4
GDN_CHUNK = 64
QKV_WIDTH = 3 * GDN_WIDTH
D_FF = (7 * D_MODEL) // 2
N_EXPERTS = 8
TOP_K = 2
N_DENSE = (DEPTH + 1) // 2
N_MOE = DEPTH // 2
N_MOD = 6
NORM_EPS = 1e-6
L2_EPS = 1e-6
IN_SIZES = (S5_WIDTH, QKV_WIDTH, GDN_WIDTH, GDN_HEADS, GDN_HEADS, D_MODEL, D_MODEL)
IN_COLS = S5_WIDTH + QKV_WIDTH + GDN_WIDTH + 2 * GDN_HEADS + 2 * D_MODEL

kernel_name = 'hybrid_s5_gdn_adaln_moe_step'

def rmsnorm(x, g):
    xf = x.astype(jnp.float32)
    y = xf * lax.rsqrt(jnp.mean(xf * xf, axis=-1, keepdims=True) + NORM_EPS)
    return (y * g.astype(jnp.float32)).astype(x.dtype)

def l2norm(x):
    return x * lax.rsqrt(jnp.sum(x * x, axis=-1, keepdims=True) + L2_EPS)

def _cplx_combine(e1, e2):
    a1r, a1i, b1r, b1i = e1
    a2r, a2i, b2r, b2i = e2
    return (a2r * a1r - a2i * a1i, a2r * a1i + a2i * a1r,
            a2r * b1r - a2i * b1i + b2r, a2r * b1i + a2i * b1r + b2i)

def s5_ssm(u, lam_re, lam_im, log_dt, b_re, b_im, c_re, c_im, d_skip, s0_re, s0_im):
    f32 = jnp.float32
    nb, L, _ = u.shape
    uf = u.astype(f32).reshape(nb, L, S5_GROUPS, S5_GROUP)
    lr = lam_re.astype(f32)
    li = lam_im.astype(f32)
    dt = jnp.exp(log_dt.astype(f32))[:, None]
    mag = jnp.exp(lr * dt)
    ab_re = mag * jnp.cos(li * dt)
    ab_im = mag * jnp.sin(li * dt)
    den = lr * lr + li * li
    nr = ab_re - 1.0
    k_re = (nr * lr + ab_im * li) / den
    k_im = (ab_im * lr - nr * li) / den
    br = b_re.astype(f32)
    bi = b_im.astype(f32)
    bb_re = k_re[..., None] * br - k_im[..., None] * bi
    bb_im = k_re[..., None] * bi + k_im[..., None] * br
    bu_re = jnp.einsum('blgc,gpc->blgp', uf, bb_re)
    bu_im = jnp.einsum('blgc,gpc->blgp', uf, bb_im)
    a_re = jnp.broadcast_to(ab_re, bu_re.shape)
    a_im = jnp.broadcast_to(ab_im, bu_im.shape)
    p_re, p_im, s_re, s_im = lax.associative_scan(_cplx_combine, (a_re, a_im, bu_re, bu_im), axis=1)
    s0r = s0_re.astype(f32)[:, None]
    s0i = s0_im.astype(f32)[:, None]
    s_re = s_re + p_re * s0r - p_im * s0i
    s_im = s_im + p_re * s0i + p_im * s0r
    y = (jnp.einsum('blgp,gcp->blgc', s_re, c_re.astype(f32))
         - jnp.einsum('blgp,gcp->blgc', s_im, c_im.astype(f32)))
    y = y.reshape(nb, L, S5_WIDTH) + d_skip.astype(f32) * uf.reshape(nb, L, S5_WIDTH)
    return y, s_re[:, -1], s_im[:, -1]

def causal_conv(x, buf, w):
    xp = jnp.concatenate([buf.astype(x.dtype), x], axis=1)
    L = x.shape[1]
    out = xp[:, 0:L] * w[0]
    for j in range(1, GDN_CONV):
        out = out + xp[:, j:j + L] * w[j]
    return jax.nn.silu(out), xp[:, -(GDN_CONV - 1):]

def gated_delta_chunked(q, k, v, g, beta, s0):
    nb, L, H, dk = q.shape
    dv = v.shape[-1]
    C = min(GDN_CHUNK, L)
    pad = (-L) % C
    if pad:
        pw = ((0, 0), (0, pad), (0, 0), (0, 0))
        q, k, v = jnp.pad(q, pw), jnp.pad(k, pw), jnp.pad(v, pw)
        g, beta = jnp.pad(g, pw[:3]), jnp.pad(beta, pw[:3])
    n = (L + pad) // C

    def chunks(t):
        t = t.reshape((nb, n, C, H) + t.shape[3:])
        return jnp.moveaxis(t, (1, 3), (0, 2))

    q = chunks(q) * (dk ** -0.5)
    k, v, g, beta = chunks(k), chunks(v), chunks(g), chunks(beta)
    gc = jnp.cumsum(g, axis=-1)
    tril = jnp.tril(jnp.ones((C, C), bool))
    strict = jnp.tril(jnp.ones((C, C), bool), -1)
    diff = gc[..., :, None] - gc[..., None, :]
    decay = jnp.where(tril, jnp.exp(jnp.where(tril, diff, 0.0)), 0.0)
    kb = k * beta[..., None]
    lower = jnp.where(strict, jnp.einsum('nbhcd,nbhmd->nbhcm', kb, k) * decay, 0.0)
    a_mat = lower + jnp.eye(C, dtype=q.dtype)
    rhs = jnp.concatenate([v * beta[..., None], kb * jnp.exp(gc)[..., None]], axis=-1)
    sol = lax.linalg.triangular_solve(a_mat, rhs, left_side=True, lower=True)
    u_c, w_c = sol[..., :dv], sol[..., dv:]
    attn = jnp.where(tril, jnp.einsum('nbhcd,nbhmd->nbhcm', q, k) * decay, 0.0)
    qg = q * jnp.exp(gc)[..., None]
    kg = k * jnp.exp(gc[..., -1:] - gc)[..., None]
    glast = jnp.exp(gc[..., -1])

    def step(S, xs):
        qg_i, kg_i, u_i, w_i, attn_i, gl_i = xs
        v_new = u_i - jnp.einsum('bhcd,bhde->bhce', w_i, S)
        o = jnp.einsum('bhcd,bhde->bhce', qg_i, S) + jnp.einsum('bhcm,bhme->bhce', attn_i, v_new)
        S = S * gl_i[..., None, None] + jnp.einsum('bhcd,bhce->bhde', kg_i, v_new)
        return S, o

    S, o = lax.scan(step, s0, (qg, kg, u_c, w_c, attn, glast))
    o = jnp.moveaxis(o, (0, 2), (1, 3)).reshape(nb, n * C, H, dv)[:, :L]
    return o, S

def mixer(h, s5r0, s5i0, S0, conv0, p, l):
    f32 = jnp.float32
    nb, L, _ = h.shape
    proj = h @ p['w_in'][l]
    split_at = np.cumsum(IN_SIZES)[:-1].tolist()
    u, qkv, z, a_lg, b_lg, gate_a, gate_b = jnp.split(proj, split_at, axis=-1)
    y_s5, s5r, s5i = s5_ssm(u, p['s5_lambda_re'][l], p['s5_lambda_im'][l], p['s5_log_dt'][l],
                            p['s5_b_re'][l], p['s5_b_im'][l], p['s5_c_re'][l], p['s5_c_im'][l],
                            p['s5_d'][l], s5r0, s5i0)
    y_s5 = jax.nn.gelu(y_s5).astype(h.dtype)
    glu_a, glu_b = jnp.split(y_s5 @ p['w_s5_glu'][l], 2, axis=-1)
    branch_a = glu_a * jax.nn.sigmoid(glu_b)
    qkv_c, conv_new = causal_conv(qkv, conv0, p['gdn_conv_w'][l])
    q, k, v = jnp.split(qkv_c.astype(f32), 3, axis=-1)
    q = l2norm(q.reshape(nb, L, GDN_HEADS, GDN_HEAD_DIM))
    k = l2norm(k.reshape(nb, L, GDN_HEADS, GDN_HEAD_DIM))
    v = v.reshape(nb, L, GDN_HEADS, GDN_HEAD_DIM)
    g = -jnp.exp(p['gdn_a_log'][l].astype(f32)) * jax.nn.softplus(a_lg.astype(f32) + p['gdn_dt_bias'][l].astype(f32))
    beta = jax.nn.sigmoid(b_lg.astype(f32))
    o, S = gated_delta_chunked(q, k, v, g, beta, S0.astype(f32))
    o = rmsnorm(o, p['gdn_norm_w'][l]) * jax.nn.silu(z.astype(f32).reshape(nb, L, GDN_HEADS, GDN_HEAD_DIM))
    branch_b = o.reshape(nb, L, GDN_WIDTH).astype(h.dtype) @ p['w_gdn_out'][l]
    merged = jax.nn.sigmoid(gate_a) * branch_a + jax.nn.sigmoid(gate_b) * branch_b
    out = merged @ p['w_out'][l]
    return (out, s5r.astype(s5r0.dtype), s5i.astype(s5i0.dtype), S.astype(S0.dtype),
            conv_new.astype(conv0.dtype))

def swiglu(h, w_gu, w_down):
    gt, up = jnp.split(h @ w_gu, 2, axis=-1)
    return (jax.nn.silu(gt) * up) @ w_down

def moe(h, w_r, b_r, w_gu, w_down):
    shp = h.shape
    t = h.reshape(-1, shp[-1])
    logits = (t @ w_r).astype(jnp.float32) + b_r.astype(jnp.float32)
    top_v, top_i = lax.top_k(logits, TOP_K)
    wts = jax.nn.softmax(top_v, axis=-1)
    comb = jnp.sum(jax.nn.one_hot(top_i, N_EXPERTS, dtype=jnp.float32) * wts[..., None], axis=1)
    comb = comb.astype(t.dtype)
    out = jnp.zeros_like(t)
    for e in range(N_EXPERTS):
        out = out + comb[:, e:e + 1] * swiglu(t, w_gu[e], w_down[e])
    return out.reshape(shp)

def trunk(x, c, s5r0, s5i0, S0, conv0, p):
    cs = jax.nn.silu(c)
    sr_l, si_l, sg_l, sc_l = [], [], [], []
    for l in range(DEPTH):
        mod = cs @ p['w_ada'][l] + p['b_ada'][l]
        sh_m, sc_m, gt_m, sh_f, sc_f, gt_f = jnp.split(mod[:, None, :], N_MOD, axis=-1)
        h = rmsnorm(x, p['g_mix'][l]) * (1.0 + sc_m) + sh_m
        out, sr, si, sg, cb = mixer(h, s5r0[l], s5i0[l], S0[l], conv0[l], p, l)
        x = x + gt_m * out
        h = rmsnorm(x, p['g_ffn'][l]) * (1.0 + sc_f) + sh_f
        if l % 2 == 0:
            f = swiglu(h, p['w_ffn_gate_up'][l // 2], p['w_ffn_down'][l // 2])
        else:
            f = moe(h, p['w_router'][l // 2], p['b_router'][l // 2],
                    p['w_exp_gate_up'][l // 2], p['w_exp_down'][l // 2])
        x = x + gt_f * f
        sr_l.append(sr)
        si_l.append(si)
        sg_l.append(sg)
        sc_l.append(cb)
    y = rmsnorm(x, p['g_final'])
    return y, jnp.stack(sr_l), jnp.stack(si_l), jnp.stack(sg_l), jnp.stack(sc_l)

def setup_inputs(seed: int = 0) -> dict:
    key = jax.random.key(seed)
    ks = iter(jax.random.split(key, 64))
    f32 = jnp.float32

    def nrm(shape, scale):
        return scale * jax.random.normal(next(ks), shape, f32)

    n_idx = jnp.arange(S5_STATE, dtype=f32)
    gdn_dt = jnp.exp(jax.random.uniform(next(ks), (DEPTH, GDN_HEADS), f32, math.log(1e-3), math.log(1e-1)))
    return {
        'x_prompt': nrm((BATCH, SEQ, D_MODEL), 1.0),
        'x_sample': nrm((DEC_BATCH, DEC_SEQ, D_MODEL), 1.0),
        'c_prompt': nrm((BATCH, D_MODEL), 1.0),
        'c_sample': nrm((DEC_BATCH, D_MODEL), 1.0),
        'state_s5_re': nrm((DEPTH, DEC_BATCH, S5_GROUPS, S5_STATE), 0.5),
        'state_s5_im': nrm((DEPTH, DEC_BATCH, S5_GROUPS, S5_STATE), 0.5),
        'state_gdn': nrm((DEPTH, DEC_BATCH, GDN_HEADS, GDN_HEAD_DIM, GDN_HEAD_DIM), 0.5),
        'state_conv': nrm((DEPTH, DEC_BATCH, GDN_CONV - 1, QKV_WIDTH), 1.0),
        'g_mix': 1.0 + nrm((DEPTH, D_MODEL), 0.02),
        'g_ffn': 1.0 + nrm((DEPTH, D_MODEL), 0.02),
        'g_final': 1.0 + nrm((D_MODEL,), 0.02),
        'w_ada': nrm((DEPTH, D_MODEL, N_MOD * D_MODEL), 0.5 * D_MODEL ** -0.5),
        'b_ada': nrm((DEPTH, N_MOD * D_MODEL), 0.02),
        'w_in': nrm((DEPTH, D_MODEL, IN_COLS), D_MODEL ** -0.5),
        's5_lambda_re': -0.5 + nrm((DEPTH, S5_GROUPS, S5_STATE), 0.01),
        's5_lambda_im': math.pi * n_idx + nrm((DEPTH, S5_GROUPS, S5_STATE), 0.01),
        's5_log_dt': jax.random.uniform(next(ks), (DEPTH, S5_GROUPS), f32, math.log(1e-3), math.log(1e-1)),
        's5_b_re': nrm((DEPTH, S5_GROUPS, S5_STATE, S5_GROUP), (2 * S5_GROUP) ** -0.5),
        's5_b_im': nrm((DEPTH, S5_GROUPS, S5_STATE, S5_GROUP), (2 * S5_GROUP) ** -0.5),
        's5_c_re': nrm((DEPTH, S5_GROUPS, S5_GROUP, S5_STATE), (2 * S5_STATE) ** -0.5),
        's5_c_im': nrm((DEPTH, S5_GROUPS, S5_GROUP, S5_STATE), (2 * S5_STATE) ** -0.5),
        's5_d': nrm((DEPTH, S5_WIDTH), 1.0),
        'w_s5_glu': nrm((DEPTH, S5_WIDTH, 2 * D_MODEL), S5_WIDTH ** -0.5),
        'gdn_conv_w': nrm((DEPTH, GDN_CONV, QKV_WIDTH), GDN_CONV ** -0.5),
        'gdn_a_log': jnp.log(jax.random.uniform(next(ks), (DEPTH, GDN_HEADS), f32, 1.0, 16.0)),
        'gdn_dt_bias': gdn_dt + jnp.log(-jnp.expm1(-gdn_dt)),
        'gdn_norm_w': 1.0 + nrm((DEPTH, GDN_HEAD_DIM), 0.02),
        'w_gdn_out': nrm((DEPTH, GDN_WIDTH, D_MODEL), GDN_WIDTH ** -0.5),
        'w_out': nrm((DEPTH, D_MODEL, D_MODEL), D_MODEL ** -0.5),
        'w_ffn_gate_up': nrm((N_DENSE, D_MODEL, 2 * D_FF), D_MODEL ** -0.5),
        'w_ffn_down': nrm((N_DENSE, D_FF, D_MODEL), D_FF ** -0.5),
        'w_router': nrm((N_MOE, D_MODEL, N_EXPERTS), D_MODEL ** -0.5),
        'b_router': nrm((N_MOE, N_EXPERTS), 0.01),
        'w_exp_gate_up': nrm((N_MOE, N_EXPERTS, D_MODEL, 2 * D_FF), D_MODEL ** -0.5),
        'w_exp_down': nrm((N_MOE, N_EXPERTS, D_FF, D_MODEL), D_FF ** -0.5),
    }

def reference(x_prompt, x_sample, c_prompt, c_sample, state_s5_re, state_s5_im, state_gdn, state_conv,
              g_mix, g_ffn, g_final, w_ada, b_ada, w_in, s5_lambda_re, s5_lambda_im, s5_log_dt,
              s5_b_re, s5_b_im, s5_c_re, s5_c_im, s5_d, w_s5_glu, gdn_conv_w, gdn_a_log, gdn_dt_bias,
              gdn_norm_w, w_gdn_out, w_out, w_ffn_gate_up, w_ffn_down, w_router, b_router,
              w_exp_gate_up, w_exp_down):
    p = dict(g_mix=g_mix, g_ffn=g_ffn, g_final=g_final, w_ada=w_ada, b_ada=b_ada, w_in=w_in,
             s5_lambda_re=s5_lambda_re, s5_lambda_im=s5_lambda_im, s5_log_dt=s5_log_dt,
             s5_b_re=s5_b_re, s5_b_im=s5_b_im, s5_c_re=s5_c_re, s5_c_im=s5_c_im, s5_d=s5_d,
             w_s5_glu=w_s5_glu, gdn_conv_w=gdn_conv_w, gdn_a_log=gdn_a_log, gdn_dt_bias=gdn_dt_bias,
             gdn_norm_w=gdn_norm_w, w_gdn_out=w_gdn_out, w_out=w_out, w_ffn_gate_up=w_ffn_gate_up,
             w_ffn_down=w_ffn_down, w_router=w_router, b_router=b_router,
             w_exp_gate_up=w_exp_gate_up, w_exp_down=w_exp_down)
    nbp = x_prompt.shape[0]
    z_sr = jnp.zeros((DEPTH, nbp, S5_GROUPS, S5_STATE), state_s5_re.dtype)
    z_si = jnp.zeros((DEPTH, nbp, S5_GROUPS, S5_STATE), state_s5_im.dtype)
    z_sg = jnp.zeros((DEPTH, nbp, GDN_HEADS, GDN_HEAD_DIM, GDN_HEAD_DIM), state_gdn.dtype)
    z_sc = jnp.zeros((DEPTH, nbp, GDN_CONV - 1, QKV_WIDTH), state_conv.dtype)
    y_prompt, sr_p, si_p, sg_p, sc_p = trunk(x_prompt, c_prompt, z_sr, z_si, z_sg, z_sc, p)
    y_sample, sr_s, si_s, sg_s, sc_s = trunk(x_sample, c_sample, state_s5_re, state_s5_im,
                                             state_gdn, state_conv, p)
    return (y_prompt, y_sample, sr_p, si_p, sg_p, sc_p, sr_s, si_s, sg_s, sc_s)


_drawn_inputs = setup_inputs


def setup_inputs(seed=0):
    import zlib

    import numpy as np

    out = dict(_drawn_inputs(seed))
    spreads = {}
    factors = {'g_ffn': 3.318,
     'g_final': 7.84,
     's5_lambda_re': 14.804,
     'gdn_norm_w': 7.702,
     'b_router': 14.533}
    for name, (base, spread) in spreads.items():
        noise = np.random.default_rng([zlib.crc32(name.encode()), seed]).standard_normal(out[name].shape)
        drawn = base * np.exp(spread * noise) if base else spread * noise
        out[name] = __import__('jax').numpy.asarray(drawn.astype(out[name].dtype))
    for name, factor in factors.items():
        out[name] = (out[name] * factor).astype(out[name].dtype)
    return out
```

```python
import math
from contextlib import ExitStack

import numpy as np

import concourse.bass as bass
from concourse import mybir

ALU = mybir.AluOpType
ACT = mybir.ActivationFunctionType
AX = mybir.AxisListType
F32 = mybir.dt.float32
I32 = mybir.dt.int32

P = 128
D = 1024
SEQ = 256
NB = 8
N = SEQ + NB
KD = D // P
DEPTH = 2
S5W = D // 2
G5, C5, ST = 32, 16, 64
UT = S5W // P
JT = G5 * ST // P
HD = 128
NH = 4
QT = 3 * NH
TAPS = 4
HALF = SEQ // 2
NC = SEQ // HALF
FF = 7 * D // 2
FT = FF // P
NE = 8
CAP = 96
PASSES = -(-N // CAP)
EPS = 1e-6

SLOT = 16
RING = 7
ADA_T, IN_T = 6 * D // P, 36
ADA_S, IN_S, GLU_S, GO_S, WO_S = ADA_T * KD // SLOT, IN_T * KD // SLOT, 16 * UT // SLOT, KD * NH // SLOT, KD * KD // SLOT
MIX_S = ADA_S + IN_S + GLU_S + GO_S + WO_S
UP_S, DOWN_S = 2 * FT * KD // SLOT, FT * KD // SLOT
FFN_S = UP_S + DOWN_S
BEFORE_EXPERTS = 2 * MIX_S + FFN_S
SLOTS = BEFORE_EXPERTS + NE * FFN_S

COLS = {}
_at = 0
for _n, _w in (("g_mix", KD), ("g_ffn", KD), ("b_ada", ADA_T), ("s5_d", UT), ("conv_w", TAPS * QT), ("gdn_w", 1),
               ("lam_re", JT), ("lam_im", JT), ("log_dt", JT), ("a_log", NH), ("dt_bias", NH), ("g_final", KD),
               ("b_router", NE)):
    COLS[_n] = (_at, _w)
    _at += _w
NCOL = _at
MASKS = ["ident", "upper", "strict", "blk", "blkT", "lev0", "lev1", "lev2"]
BASE = 16


def trunk_program(nc, x_in, c_in, cols_in, masks_in, iota_in, sel_in, bpk_in, cpk_in, s5s_in, gdn_in, conv_in,
                  wab_in, wr_in, w_in, y_out, s5_out, gdnp_out, gdns_out, conv_out):
    with ExitStack() as ctx:
        def sb(name, shape, dt=F32):
            return ctx.enter_context(nc.sbuf_tensor(name, shape, dt))

        sems = {}

        def sem(name):
            if name not in sems:
                sems[name] = ctx.enter_context(nc.semaphore(name))
            return sems[name]

        xT = sb("xT", [P, KD, N])
        hT = sb("hT", [P, KD, N])
        uT = sb("uT", [P, UT, N])
        raw = sb("raw", [P, QT, 3 + N])
        cv = sb("cv", [P, QT, N])
        zs = sb("zs", [P, NH, N])
        gates = sb("gates", [P, 2 * KD, N])
        arena = sb("arena", [P, 12 * 1024])
        ring = sb("ring", [P, RING, SLOT * P])
        bpk = sb("bpk", [P, UT, 2, P])
        cpk = sb("cpk", [P, JT, 2, 32])
        ckk = sb("ckk", [P, JT, 2, 32])
        cols = sb("cols", [P, DEPTH, NCOL])
        masks = sb("masks", [P, len(MASKS), P])
        selw = sb("selw", [P, NE, NE])
        ones = sb("ones", [P, P])
        cT = sb("cT", [P, KD, 1 + NB])
        mod = sb("mod", [P, ADA_T, 1 + NB])
        s5s = sb("s5s", [P, DEPTH, JT, 2, NB])
        conv0 = sb("conv0", [P, DEPTH, QT, NB, 3])
        wab = sb("wab", [P, DEPTH, KD, 2 * NH])
        wr = sb("wr", [P, KD, NE])
        s5o = sb("s5o", [P, JT, 2, 1 + NB])
        cvo = sb("cvo", [P, QT, 1 + NB, 3])
        rstd = sb("rstd", [P, N])
        tmp = sb("tmp", [P, 2, N])
        ssb = tmp[:, 1, :]
        iota = gates[:, :, :].rearrange("p a b -> p (a b)")[:, 0:PASSES * CAP]
        sm = sb("sm", [P, 19, JT])
        pw = sb("pw", [P, 6, JT])
        smi = sb("smi", [P, JT], I32)
        sx = sb("sx", [P, 4, JT * NB])
        gd = sb("gd", [P, 12, 3 * NH])
        dg = sb("dg", [NB, 2, NH, NB])
        rowb = sb("rowb", [P, 2, NH * NB])
        ktk = sb("ktk", [NH * NB, P])
        ini = sb("ini", [P, 4])
        rt = sb("rt", [P, 3, NE])
        rtx = sb("rtx", [P, 12, NE])
        cnt = sb("cnt", [1, 1], I32)
        bank = [ctx.enter_context(nc.psum_tensor(f"bank{b}", [P, 512], F32)) for b in range(8)]
        ident, upper, strict, blk, blkT = (masks[:, i, :] for i in range(5))

        def ar(at, *shape):
            n = int(np.prod(shape))
            v = arena[:, at:at + n]
            if len(shape) == 2:
                return v.rearrange("p (a b) -> p a b", b=shape[1])
            if len(shape) == 3:
                return v.rearrange("p (a b c) -> p a b c", b=shape[1], c=shape[2])
            return v

        B1 = 1024
        cosT = ar(0, JT, HALF)
        sinT = ar(2 * B1, JT, 2, HALF)
        st = ar(6 * B1, 8, 2, SEQ)
        wrot = ar(10 * B1, 2, SEQ)
        trot = ar(10 * B1 + 512, 2, SEQ)
        trot2 = ar(11 * B1, 2, SEQ)
        sq = ar(6 * B1, KD, N)
        nrm = hT
        mats = {}
        for i, names in enumerate(("decT vn", "dec y", "ln vb", "lnT", "att", "e", "eT", "p", "pT", "kbg nwT", "kg", "qg")):
            for n in names.split():
                mats[n] = [ar(i * B1 + c * 512, NH, P) for c in range(NC)]
        s_pr = ar(5 * B1, NH, P)
        s0 = ar(5 * B1, NH * NB, P)
        vm = ar(0, NH * NB, P)
        oT = raw[:, 0:NH, 3:3 + N]
        osq = hT[:, NH:2 * NH, :]
        act0 = ar(0, FT, N)
        sg = tmp
        htok = raw[:, :, :].rearrange("p a b -> p (a b)")[:, 0:3 * D].rearrange("p (a b) -> p a b", b=D)
        acc = cv[:, 0:KD, :]
        actE = ar(0, FT, CAP)
        hg = ar(3 * B1, KD, CAP)
        ye = ar(4 * B1, D)
        dcT = ar(5 * B1, N)
        dsel = ar(5 * B1 + 512, 3, CAP)
        dw = ar(6 * B1, 3, CAP)
        sgE = ar(6 * B1 + 512, 2, CAP)

        def col(l, name, i=0, w=None):
            at, width = COLS[name]
            return cols[:, l, at + i:at + i + (width - i if w is None else w)]

        full = [sem(f"full{b}") for b in range(8)]
        free = [sem(f"free{b}") for b in range(8)]
        group, order, reads = {}, [], [0] * 8

        def open_bank(pe, name, readers=1):
            b = len(order) % 8
            if reads[b]:
                pe.wait_ge(free[b], reads[b])
            reads[b] += readers
            group[name] = (b, len(order) // 8 + 1, reads[b])
            order.append(name)
            return bank[b]

        def filled(eng, name):
            b, n, _ = group[name]
            eng.wait_ge(full[b], n)
            return bank[b]

        def gives(ins, name):
            ins.then_inc(free[group[name][0]], 1)

        def taken(eng, name):
            b, _, n = group[name]
            eng.wait_ge(free[b], n)

        landed = [sem(f"landed{r}") for r in range(RING)]
        used = sem("slots_used")

        class Stream:
            pos, blk, owed = 0, 0, False

        stream = Stream()

        def weights(pe):
            r = stream.pos % RING
            if stream.blk == 0:
                pe.wait_ge(landed[r], 16 * (stream.pos // RING + 1))
            b = stream.blk
            stream.blk += 1
            if stream.blk == SLOT:
                stream.pos, stream.blk = stream.pos + 1, 0
            return ring[:, r, b * P:(b + 1) * P]

        def mm(pe, out, rhs, start, stop):
            first = stream.blk == 0
            w = weights(pe)
            ins = pe.matmul(out, w, rhs, start=start, stop=stop)
            if first and stream.owed:
                ins.then_inc(used, 1)
            if first:
                stream.owed = True
            return ins

        count = {}

        def then(eng, ins, name):
            count[name] = count.get(name, 0) + 1
            ins.then_inc(sem(name), 1)
            eng.wait_ge(sem(name), count[name])

        def takes(eng, ins, name):
            gives(ins, name)
            b, _, n = group[name]
            eng.wait_ge(free[b], n)

        LOADS = ("x", "c", "cols", "masks", "iota", "sel", "s5s", "conv0", "wab", "wr")
        for b in range(8):
            sem(f"full{b}")
        ld = {n: sem(f"in_{n}") for n in LOADS}
        block = ctx.enter_context(nc.Block())

        def count_rms(tag):
            return {("mix", 0): 1, ("ffn", 0): 2, ("mix", 1): 3, ("ffn", 1): 4, ("end", 0): 5}[tag]

        @block.tensor
        def _(pe):
            def rms(tag):
                pe.wait_ge(sem("sq_done"), count_rms(tag))
                ps = open_bank(pe, ("rms",) + tag)
                for k in range(KD):
                    ins = pe.matmul(ps[:, 0:N], ones[:, :], sq[:, k, :], start=k == 0, stop=k == KD - 1)
                ins.then_inc(full[group[("rms",) + tag][0]], 1)

            def close(ins, name):
                ins.then_inc(full[group[name][0]], 1)

            def project(name, rhs, kt, readers=1):
                ps = open_bank(pe, name, readers)
                for k in range(kt):
                    ins = mm(pe, ps[:, 0:N], rhs(k), k == 0, k == kt - 1)
                close(ins, name)

            def tok_logits(name, w):
                ps = open_bank(pe, name)
                for g in range(3):
                    m = P if g < 2 else NB
                    for k in range(KD):
                        ins = pe.matmul(ps[0:m, 8 * g:8 * g + 8], hT[:, k, P * g:P * g + m], w[:, k, :],
                                        start=k == 0, stop=k == KD - 1)
                close(ins, name)

            def bu(l, j):
                ps = open_bank(pe, ("bu", l, j))
                a = 32 * (j % 4)
                for c in range(2):
                    ins = pe.matmul(ps[:, c * SEQ:(c + 1) * SEQ], bpk[a:a + 32, j // 4, c, :],
                                    uT[a:a + 32, j // 4, 0:SEQ], start=True, stop=True)
                close(ins, ("bu", l, j))

            def batch4(name, fn, readers=1):
                ps = open_bank(pe, name, readers)
                for h in range(NH):
                    ins = fn(ps[:, h * P:(h + 1) * P], h)
                close(ins, name)

            def one(a, b):
                return lambda o, h: pe.matmul(o, a(h), b(h), start=True, stop=True)

            def mixer(l):
                pe.wait_ge(sem("cs_done"), 1)
                ps = open_bank(pe, ("ada", l))
                for m in range(ADA_T):
                    for k in range(KD):
                        ins = mm(pe, ps[:, 9 * m:9 * m + 9], cT[:, k, :], k == 0, k == KD - 1)
                close(ins, ("ada", l))
                rms(("mix", l))
                if l == 0:
                    pe.wait_ge(ld["wab"], 16)
                pe.wait_ge(sem("h_act"), KD * (2 * l + 1))
                pe.wait_ge(sem("h_smp"), 2 * l + 1)
                tok_logits(("ab", l), wab[:, l])
                for m in range(UT):
                    project(("in", l, m), lambda k: hT[:, k, :], KD)
                pe.wait_ge(sem("b_in"), 16 * (l + 1))
                for m in range(UT):
                    taken(pe, ("in", l, m))
                ps = open_bank(pe, ("bus", l))
                for a in range(4):
                    if a:
                        pe.wait_ge(sem("bus_rows"), 3 * l + a)
                    for j in range(a, JT, 4):
                        for c in range(2):
                            o = NB * (2 * j + c)
                            ins = pe.matmul(ps[:, o:o + NB], bpk[32 * a:32 * a + 32, j // 4, c, :],
                                            uT[32 * a:32 * a + 32, j // 4, SEQ:N], start=True, stop=True)
                    if a < 3:
                        ins.then_inc(sem("bus_rows"), 1)
                close(ins, ("bus", l))
                for m in range(UT, IN_T):
                    project(("in", l, m), lambda k: hT[:, k, :], KD)
                    if (m - UT) % 2 == 1:
                        bu(l, (m - UT) // 2)
                    if (m - UT) % 8 == 7 and m - UT > 8:
                        s5_y(l, (m - UT) // 8 - 1)
                s5_y(l, UT - 1)
                for m in range(UT):
                    pe.wait_ge(sem("gelu_done"), UT * l + m + 1)
                for m in range(2 * KD):
                    project(("glu", l, m), lambda k: uT[:, k, :], UT)
                pe.wait_ge(sem("qk_sq"), l + 1)
                for i in range(2 * NH):
                    ps = open_bank(pe, ("qkn", l, i))
                    close(pe.matmul(ps[:, 0:N], ones[:, :], sq[:, i, :], start=True, stop=True), ("qkn", l, i))
                gdn(l)
                gdn_samples(l)
                pe.wait_ge(sem("o_sq"), l + 1)
                for h in range(NH):
                    ps = open_bank(pe, ("on", l, h))
                    close(pe.matmul(ps[:, 0:N], ones[:, :], osq[:, h, :], start=True, stop=True), ("on", l, h))
                pe.wait_ge(sem("o_done"), l + 1)
                for m in range(KD):
                    project(("go", l, m), lambda k: oT[:, k, :], NH)
                for m in range(KD):
                    pe.wait_ge(sem("merged"), KD * l + m + 1)
                for m in range(KD):
                    project(("wo", l, m), lambda k: hT[:, k, :], KD)

            def s5_y(l, i):
                pe.wait_ge(sem("s_back"), JT * l + 4 * i + 4)
                pe.wait_ge(sem("s_smp"), l + 1)
                ps = open_bank(pe, ("y", l, i))
                for jj in range(4):
                    j = 4 * i + jj
                    o = ps[32 * jj:32 * jj + 32, :]
                    for c in range(2):
                        pe.matmul(o[:, 0:SEQ], ckk[:, j, c, :], st[:, j % 8, c, :], start=c == 0, stop=c == 1)
                    for c in range(2):
                        ins = pe.matmul(o[:, SEQ:N], cpk[:, j, c, :], s5s[:, l, j, c, :], start=c == 0, stop=c == 1)
                close(ins, ("y", l, i))

            def gdn(l):
                def q(c):
                    return lambda h: cv[:, h, P * c:P * c + P]

                def k(c):
                    return lambda h: cv[:, NH + h, P * c:P * c + P]

                pe.wait_ge(sem("g_done"), l + 1)
                name = ("gcc", l)
                ps = open_bank(pe, name)
                close(pe.matmul(ps[:, 0:8], upper, gd[:, 0, 0:8], start=True, stop=True), name)
                for c in range(NC):
                    batch4(("gcb", l, c), one(lambda h: gd[:, 0, 4 * c + h:4 * c + h + 1].broadcast_to([P, P]),
                                              lambda h: upper))
                pe.wait_ge(sem("qk_done"), l + 1)
                for c in range(NC):
                    batch4(("ktok", l, c), lambda o, h: pe.transpose(o, k(c)(h), ident))
                for c in range(NC):
                    batch4(("kk", l, c), one(k(c), k(c)))
                    batch4(("qk", l, c), one(k(c), q(c)))
                for c in range(NC):
                    pe.wait_ge(sem("ln_done"), NC * l + c + 1)
                    batch4(("lt", l, c), lambda o, h: pe.transpose(o, mats["ln"][c][:, h, :], ident))
                    batch4(("vtok", l, c), lambda o, h: pe.transpose(o, cv[:, 2 * NH + h, P * c:P * c + P], ident))
                at = lambda n, c: (lambda h: mats[n][c][:, h, :])
                for s in range(3):
                    for c in range(NC):
                        if s == 0:
                            pe.wait_ge(sem("e_done"), NC * l + c + 1)
                        else:
                            taken(pe, ("e", l, s - 1, c))
                            taken(pe, ("eT", l, s - 1, c))
                        batch4(("e", l, s, c), one(at("eT", c), at("e", c)))
                        batch4(("eT", l, s, c), one(at("e", c), at("eT", c)))
                    for c in range(NC):
                        taken(pe, ("e", l, s, c))
                        taken(pe, ("eT", l, s, c))
                        if s:
                            taken(pe, ("pT", l, s - 1, c))
                        batch4(("p", l, s, c), one(at("eT", c), at("p", c)))
                        batch4(("pT", l, s, c), one(at("e", c), at("pT", c)))
                for s in range(3):
                    for c in range(NC):
                        taken(pe, ("pT", l, 2, c) if s == 0 else ("xT", l, s - 1, c))
                        pe.wait_ge(sem("lev_done"), NC * (3 * l + s) + c + 1)
                        batch4(("yl", l, s, c), one(at("eT", c), at("p", c)))
                    for c in range(NC):
                        taken(pe, ("yl", l, s, c))
                        if s < 2:
                            batch4(("x", l, s, c), one(at("pT", c), at("y", c)))
                        batch4(("xT", l, s, c), one(at("y", c), at("pT", c)))
                for c in range(NC):
                    taken(pe, ("xT", l, 2, c))
                    taken(pe, ("ktok", l, c))
                    batch4(("wt", l, c), one(at("kbg", c), at("pT", c)))
                for c in range(NC):
                    taken(pe, ("vtok", l, c))
                    if c:
                        taken(pe, ("wt", l, c))
                        taken(pe, ("s", l, c - 1))
                    name = ("vn", l, c)
                    ps = open_bank(pe, name)
                    for h in range(NH):
                        o = ps[:, h * P:(h + 1) * P]
                        ins = pe.matmul(o, mats["pT"][c][:, h, :], mats["vb"][c][:, h, :], start=True, stop=c == 0)
                        if c:
                            ins = pe.matmul(o, mats["nwT"][c][:, h, :], s_pr[:, h, :], start=False, stop=True)
                    close(ins, name)
                    taken(pe, name)
                    taken(pe, ("qk", l, c))
                    pe.wait_ge(sem("qg_done"), NC * l + c + 1)
                    name = ("o", l, c)
                    ps = open_bank(pe, name)
                    for h in range(NH):
                        o = ps[:, h * P:(h + 1) * P]
                        ins = pe.matmul(o, mats["vn"][c][:, h, :], mats["att"][c][:, h, :], start=True, stop=c == 0)
                        if c:
                            ins = pe.matmul(o, s_pr[:, h, :], mats["qg"][c][:, h, :], start=False, stop=True)
                    close(ins, name)
                    batch4(("s", l, c), one(at("kg", c), at("vn", c)))

            def gdn_samples(l):
                hb = NH * NB
                pe.wait_ge(sem("qkp_done"), l + 1)
                name = ("skt", l)
                ps = open_bank(pe, name)
                close(pe.transpose(ps[0:hb, 0:P], sx[:, 2, 0:hb], ident), name)
                pe.wait_ge(sem("dg_done"), l + 1)
                name = ("sgb", l)
                ps = open_bank(pe, name)
                close(pe.matmul(ps[:, 0:2 * hb], ones[0:NB, :], dg[:, :, :, :].rearrange("p a h b -> p (a h b)"),
                                start=True, stop=True), name)
                name = ("sqk", l)
                ps = open_bank(pe, name)
                close(pe.matmul(ps[:, 0:hb], ones[:, :], sx[:, 0, 0:hb], start=True, stop=True), name)
                pe.wait_ge(sem("s0_in"), 16 * (l + 1))
                name = ("skq", l)
                ps = open_bank(pe, name)
                for h in range(NH):
                    for b in range(NB):
                        i = h * NB + b
                        ins = pe.matmul(ps[:, 2 * i:2 * i + 2], s0[:, i, :], cv[:, h:h + NH + 1:NH, SEQ + b],
                                        start=True, stop=True)
                close(ins, name)
                pe.wait_ge(sem("svn_done"), l + 1)
                name = ("svt", l)
                ps = open_bank(pe, name)
                close(pe.transpose(ps[0:hb, 0:P], sx[:, 1, 0:hb], ident), name)
                pe.wait_ge(sem("vm_done"), l + 1)
                for i in range(NB):
                    name = ("so", l, i)
                    ps = open_bank(pe, name)
                    close(pe.matmul(ps[:, :], ktk[:, :], vm[0:hb, 4 * i:4 * i + 4, :].rearrange("p a b -> p (a b)"),
                                    start=True, stop=True), name)

            def drained():
                for b in range(8):
                    if reads[b]:
                        pe.wait_ge(free[b], reads[b])

            def dense():
                drained()
                pe.wait_ge(sem("h_act"), 2 * KD)
                pe.wait_ge(sem("h_smp"), 2)
                base = stream.pos
                BODY = 2 * RING
                assert UP_S % BODY == 0 and DOWN_S == BODY
                with pe.Fori(0, UP_S // BODY) as it:
                    for s in range(BODY):
                        r = (base + s) % RING
                        pe.wait_ge(landed[r], it * 32 + 16 * ((base + s) // RING + 1))
                        if s >= 2:
                            pe.wait_ge(sem("act_done"), it * BODY + s)
                        else:
                            pe.wait_ge(sem("act_done"), it * (BODY - 1 + s) + 1)
                        for half in range(2):
                            for k in range(KD):
                                w = ring[:, r, (half * KD + k) * P:(half * KD + k + 1) * P]
                                ins = pe.matmul(bank[2 * (s % 2) + half][:, 0:N], w, hT[:, k, :],
                                                start=k == 0, stop=k == KD - 1)
                                if half == 0 and k == 0:
                                    ins.then_inc(used, 1)
                        ins.then_inc(sem("up_full"), 1)
                stream.pos += UP_S
                pe.wait_ge(sem("act_done"), FT + 1)
                for m in range(KD):
                    if m >= 2:
                        pe.wait_ge(sem("down_taken"), m - 1)
                    for k in range(FT):
                        ins = mm(pe, bank[4 + m % 2][:, 0:N], act0[:, k, :], k == 0, k == FT - 1)
                    ins.then_inc(sem("down_full"), 1)
                pe.wait_ge(sem("down_taken"), KD)

            def experts_setup():
                pe.wait_ge(ld["wr"], 16)
                pe.wait_ge(sem("h_act"), 4 * KD)
                pe.wait_ge(sem("h_smp"), 4)
                tok_logits(("rl",), wr)
                for g in range(3):
                    m = P if g < 2 else NB
                    for half in range(2):
                        name = ("ht", g, half)
                        ps = open_bank(pe, name)
                        for k in range(4):
                            ins = pe.transpose(ps[0:m, k * P:(k + 1) * P], hT[:, 4 * half + k, P * g:P * g + m], ident)
                        close(ins, name)
                pe.wait_ge(sem("sel_done"), 1)
                ps = open_bank(pe, ("rank",))
                for g in range(4):
                    m = P if g != 2 else NB
                    o = ps[0:m, 8 * g:8 * g + 8]
                    for a in range(min(g, 3)):
                        ka = P if a < 2 else NB
                        ins = pe.matmul(o, ones[0:ka, 0:m], rt[0:ka, a, :], start=a == 0, stop=g == 3 and a == 2)
                    if g < 3:
                        ins = pe.matmul(o, upper[0:m, 0:m], rt[0:m, g, :], start=g == 0, stop=True)
                close(ins, ("rank",))
                drained()

            def expert(q):
                pe.wait_ge(sem("dsel_done"), q * 1 + 1)
                for m in range(KD):
                    for g in range(3):
                        kk = P if g < 2 else NB
                        ins = pe.matmul(bank[6 + m // 4][:, CAP * (m % 4):CAP * (m % 4) + CAP],
                                        htok[0:kk, g, m * P:(m + 1) * P], dsel[0:kk, g, :], start=g == 0, stop=g == 2)
                    if m % 4 == 3:
                        ins.then_inc(sem("gather_full"), 1)
                for g in range(3):
                    m = P if g < 2 else NB
                    ins = pe.transpose(bank[2][0:CAP, P * g:P * g + m], dw[0:m, g, :], ident[0:m, 0:m])
                ins.then_inc(sem("dcT_full"), 1)
                base = BEFORE_EXPERTS
                turns = FFN_S // RING
                pe.wait_ge(sem("hg_done"), 2 * q + 2)
                for s in range(UP_S):
                    r = (base + s) % RING
                    pe.wait_ge(landed[r], q * (16 * turns) + 16 * ((base + s) // RING + 1))
                    pe.wait_ge(sem("act_done"), q * FT + (FT + s))
                    for half in range(2):
                        for k in range(KD):
                            w = ring[:, r, (half * KD + k) * P:(half * KD + k + 1) * P]
                            ins = pe.matmul(bank[s % 2][:, CAP * half:CAP * half + CAP], w, hg[:, k, :],
                                            start=k == 0, stop=k == KD - 1)
                            if half == 0 and k == 0:
                                ins.then_inc(used, 1)
                    ins.then_inc(sem("up_full"), 1)
                for s in range(DOWN_S):
                    r = (base + UP_S + s) % RING
                    pe.wait_ge(landed[r], q * (16 * turns) + 16 * ((base + UP_S + s) // RING + 1))
                    pe.wait_ge(sem("act_done"), q * FT + (FT + 2 * s + 3))
                    for kk in range(2):
                        k = 2 * s + kk
                        for half in range(2):
                            ins = pe.matmul(bank[4 + half][0:CAP, :], actE[:, k, :],
                                            ring[:, r, kk * D + half * 512:kk * D + half * 512 + 512],
                                            start=k == 0, stop=k == FT - 1)
                            if kk == 0 and half == 0:
                                ins.then_inc(used, 1)
                            if k == FT - 1:
                                ins.then_inc(sem("ye_full"), 1)
                pe.wait_ge(sem("dcT_done"), q * 1 + 1)
                pe.wait_ge(sem("ye_done"), q * 2 + 2)
                for m in range(KD):
                    pe.wait_ge(sem("down_taken"), q * KD + (KD + m - 1))
                    pe.matmul(bank[2 + m % 2][:, 0:N], ye[0:CAP, m * P:(m + 1) * P], dcT[0:CAP, :],
                              start=True, stop=True).then_inc(sem("down_full"), 1)
                pe.wait_ge(sem("down_taken"), q * KD + 2 * KD)

            pe.wait_ge(ld["masks"], 16)
            pe.wait_ge(sem("ones_done"), 1)
            mixer(0)
            rms(("ffn", 0))
            dense()
            mixer(1)
            rms(("ffn", 1))
            experts_setup()
            with pe.Fori(0, NE) as e:
                expert(e)
            pe.wait_ge(sem("cnt_done"), 1)
            most = pe.value_load(cnt[0:1, 0:1])
            with pe.If(most > CAP):
                with pe.Fori(NE, PASSES * NE) as q:
                    expert(q)
            pe.wait_ge(sem("sq_done"), count_rms(("end", 0)))
            for k in range(KD):
                ins = pe.matmul(bank[0][:, 0:N], ones[:, :], sq[:, k, :], start=k == 0, stop=k == KD - 1)
            ins.then_inc(sem("end_full"), 1)


        @block.sync
        def _(sp):
            for n in range(RING):
                sp.dma_start(ring[:, n, :], w_in[n]).then_inc(landed[n], 16)
            whole = (BEFORE_EXPERTS - RING) // RING
            with sp.Fori(0, whole) as i:
                for r in range(RING):
                    sp.wait_ge(used, i * RING + (r + 1))
                    sp.dma_start(ring[:, r, :], w_in[i * RING + (RING + r)]).then_inc(landed[r], 16)
            for n in range(RING * (whole + 1), BEFORE_EXPERTS):
                sp.wait_ge(used, n - RING + 1)
                sp.dma_start(ring[:, n % RING, :], w_in[n]).then_inc(landed[n % RING], 16)

            def expert_weights(q, e):
                for s in range(FFN_S):
                    sp.wait_ge(used, q * FFN_S + (BEFORE_EXPERTS + s - RING + 1))
                    r = (BEFORE_EXPERTS + s) % RING
                    sp.dma_start(ring[:, r, :], w_in[e * FFN_S + (BEFORE_EXPERTS + s)]).then_inc(landed[r], 16)

            with sp.Fori(0, NE) as e:
                expert_weights(e, e)
            sp.wait_ge(sem("cnt_done"), 1)
            most = sp.value_load(cnt[0:1, 0:1])
            with sp.If(most > CAP):
                with sp.Fori(1, PASSES) as a:
                    with sp.Fori(0, NE) as e:
                        expert_weights(a * NE + e, e)
            sp.wait_ge(sem("y_done"), KD)
            sp.dma_start(y_out, hT[:, :, :]).then_inc(sem("y_out"), 16)
            sp.wait_ge(sem("y_out"), 16)

        @block.scalar
        def _(act):
            act.dma_start(cT[:, :, :], c_in).then_inc(ld["c"], 16)
            act.dma_start(xT[:, :, :], x_in).then_inc(ld["x"], 16)
            act.dma_start(cols[:, :, :], cols_in).then_inc(ld["cols"], 16)
            act.dma_start(masks[:, :, :], masks_in).then_inc(ld["masks"], 16)
            act.dma_start(wab[:, :, :, :], wab_in).then_inc(ld["wab"], 16)
            act.dma_start(bpk[:, :, :, :], bpk_in[0]).then_inc(sem("b_in"), 16)
            act.dma_start(cpk[:, :, :, :], cpk_in[0]).then_inc(sem("c5_in"), 16)
            act.dma_start(s5s[:, :, :, :, :], s5s_in).then_inc(ld["s5s"], 16)
            act.dma_start(conv0[:, :, :, :, :], conv_in).then_inc(ld["conv0"], 16)
            act.dma_start(selw[:, :, :], sel_in).then_inc(ld["sel"], 16)
            act.dma_start(wr[:, :, :], wr_in).then_inc(ld["wr"], 16)
            act.wait_ge(ld["c"], 16)
            act.activation(cT[:, :, :], cT[:, :, :], ACT.Silu).then_inc(sem("cs_done"), 1)
            act.wait_ge(ld["x"], 16)

            def rms(tag, wait=None):
                if wait:
                    act.wait_ge(sem(wait[0]), wait[1])
                if tag[0] == "ffn":
                    act.wait_ge(sem("gs_out"), 16 * (tag[1] + 1))
                act.activation(sq, xT[:, :, :], ACT.Square).then_inc(sem("sq_done"), 1)

            def root(n):
                act.wait_ge(sem("ss_done"), n)
                act.activation(rstd[:, :], ssb[:, :], ACT.Sqrt).then_inc(sem("root_done"), 1)

            def shift(l, at, n):
                for k in range(KD):
                    act.wait_ge(sem("h_scaled"), KD * n + k + 1)
                    act.activation(hT[:, k, 0:SEQ], hT[:, k, 0:SEQ], ACT.Identity,
                                   bias=mod[:, at + k, 0:1]).then_inc(sem("h_act"), 1)

            def mixer(l):
                rms(("mix", l), ("x_ffn", KD) if l else None)
                root(2 * l + 1)
                shift(l, 0, 2 * l)
                for m in range(IN_T):
                    name = ("in", l, m)
                    ps = filled(act, name)[:, 0:N]
                    if m < UT:
                        ins = act.activation(uT[:, m, :], ps, ACT.Copy)
                    elif m < UT + QT:
                        if m == UT and l == 0:
                            act.wait_ge(sem("pool_zero"), 1)
                        ins = act.activation(raw[:, m - UT, 3:3 + N], ps, ACT.Copy)
                    elif m < UT + QT + NH:
                        ins = act.activation(zs[:, m - UT - QT, :], ps, ACT.Silu)
                    else:
                        ins = act.activation(gates[:, m - UT - QT - NH, :], ps, ACT.Sigmoid)
                    gives(ins, name)
                for i in range(3):
                    act.wait_ge(sem("conv_done"), l + 1)
                    v = cv[:, NH * i:NH * i + NH, :]
                    then(act, act.activation(v, v, ACT.Silu), "cv_silu")
                for i in range(UT):
                    act.wait_ge(sem("y_sum"), UT * l + i + 1)
                    act.activation(uT[:, i, :], uT[:, i, :], ACT.Gelu_apprx_tanh).then_inc(sem("gelu_done"), 1)
                act.wait_ge(sem("y_sum"), UT * l + UT)
                act.activation(sq, cv[:, 0:2 * NH, :], ACT.Square).then_inc(sem("qk_sq"), 1)
                for m in range(KD):
                    name = ("glu", l, 2 * m + 1)
                    ps = filled(act, name)
                    if m >= 2:
                        act.wait_ge(sem("glu_done"), KD * l + m - 1)
                    ins = act.activation(tmp[:, m % 2, :], ps[:, 0:N], ACT.Sigmoid)
                    gives(ins, name)
                act.wait_ge(sem("ax_done"), l + 1)
                then(act, act.activation(gd[:, 1, :], gd[:, 1, :], ACT.Exp, scale=-1.0), "a_gd")
                act.activation(gd[:, 1, :], gd[:, 1, :], ACT.Ln, bias=1.0).then_inc(sem("a_ln"), 1)
                act.activation(gd[:, 3, 0:NH], col(l, "a_log"), ACT.Exp).then_inc(sem("a_ln"), 1)
                act.activation(gd[:, 4, :], gd[:, 4, :], ACT.Sigmoid).then_inc(sem("a_ln"), 1)
                act.wait_ge(sem("nrm_ss"), l + 1)
                act.activation(nrm[:, :, :], nrm[:, :, :], ACT.Sqrt).then_inc(sem("nrm_root"), 1)
                act.wait_ge(sem("gdx_done"), l + 1)
                act.activation(gd[:, 7:10, 0:8], gd[:, 7:10, 0:8], ACT.Exp).then_inc(sem("a_col"), 1)
                act.activation(gd[:, 11, 8:12], gd[:, 0, 8:12], ACT.Exp).then_inc(sem("a_col"), 1)
                for c in range(NC):
                    name = ("gcb", l, c)
                    act.wait_ge(sem("diff_done"), NC * l + c + 1)
                    act.activation(mats["decT"][c], mats["decT"][c], ACT.Exp).then_inc(sem("a_dec"), 1)
                    act.activation(mats["dec"][c], mats["dec"][c], ACT.Exp).then_inc(sem("a_dec"), 1)
                    ps = filled(act, name)
                    gives(act.activation(mats["qg"][c], ps[:, :].rearrange("p (h t) -> p h t", h=NH), ACT.Exp), name)
                for s in range(3):
                    for c in range(NC):
                        for n in ("e", "eT"):
                            name = (n, l, s, c)
                            filled(act, ("eT", l, s, c))
                            ps = filled(act, name)
                            gives(act.activation(mats[n][c], ps[:, :].rearrange("p (h t) -> p h t", h=NH), ACT.Copy), name)
                for s in range(3):
                    for c in range(NC):
                        name = ("yl", l, s, c)
                        ps = filled(act, name)
                        gives(act.activation(mats["y"][c], ps[:, :].rearrange("p (h t) -> p h t", h=NH), ACT.Copy), name)
                for c in range(NC):
                    name = ("wt", l, c)
                    ps = filled(act, name)
                    gives(act.activation(mats["nwT"][c], ps[:, :].rearrange("p (h t) -> p h t", h=NH), ACT.Copy,
                                         scale=-1.0), name)
                for c in range(NC):
                    name = ("vn", l, c)
                    ps = filled(act, name)
                    gives(act.activation(mats["vn"][c], ps[:, :].rearrange("p (h t) -> p h t", h=NH), ACT.Copy), name)
                    name = ("o", l, c)
                    ps = filled(act, name)
                    gives(act.activation(oT[:, :, P * c:P * c + P], ps[:, :].rearrange("p (h t) -> p h t", h=NH),
                                         ACT.Copy), name)
                act.wait_ge(sem("sp_out"), 16 * (l + 1))
                filled(act, ("s", l, NC - 1))
                act.dma_start(s0, gdn_in[l]).then_inc(sem("s0_in"), 16)
                act.wait_ge(sem("os_done"), l + 1)
                taken(act, ("o", l, NC - 1))
                act.activation(osq, oT, ACT.Square).then_inc(sem("o_sq"), 1)
                act.wait_ge(sem("on_ss"), l + 1)
                act.activation(nrm[:, 0:NH, :], nrm[:, 0:NH, :], ACT.Sqrt).then_inc(sem("on_root"), 1)

            mixer(0)
            rms(("ffn", 0), ("x_mix", KD))
            root(2)
            shift(0, 24, 1)
            with act.Fori(0, FT // 2) as it:
                for s in range(2):
                    act.wait_ge(sem("up_full"), it * 2 + (s + 1))
                    act.wait_ge(sem("act_done"), it * 2 + 1)
                    act.activation(sg[:, s, :], bank[2 * s][:, 0:N], ACT.Silu).then_inc(sem("silu_done"), 1)
            filled(act, ("y", 0, UT - 1))
            act.dma_start(bpk[:, :, :, :], bpk_in[1]).then_inc(sem("b_in"), 16)
            act.dma_start(cpk[:, :, :, :], cpk_in[1]).then_inc(sem("c5_in"), 16)
            mixer(1)
            rms(("ffn", 1), ("x_mix", 2 * KD))
            act.dma_start(iota, iota_in).then_inc(ld["iota"], 16)
            root(4)
            shift(1, 24, 3)
            for g in range(3):
                m = P if g < 2 else NB
                for half in range(2):
                    name = ("ht", g, half)
                    ps = filled(act, name)
                    gives(act.activation(htok[0:m, g, 512 * half:512 * half + 512], ps[0:m, :], ACT.Copy), name)
            act.wait_ge(sem("sel_done"), 1)
            act.activation(rtx[:, 6:9, :], rtx[:, 6:9, :], ACT.Exp).then_inc(sem("rexp_done"), 1)

            def expert(q):
                for half in range(2):
                    act.wait_ge(sem("gather_full"), q * 2 + (half + 1))
                    act.activation(hg[:, 4 * half:4 * half + 4, :],
                                   bank[6 + half][:, 0:4 * CAP].rearrange("p (a b) -> p a b", b=CAP),
                                   ACT.Copy).then_inc(sem("hg_done"), 1)
                act.wait_ge(sem("dcT_full"), q * 1 + 1)
                act.activation(dcT[0:CAP, :], bank[2][0:CAP, 0:N], ACT.Copy).then_inc(sem("dcT_done"), 1)
                for s in range(FT):
                    act.wait_ge(sem("up_full"), q * FT + (FT + s + 1))
                    act.wait_ge(sem("act_done"), q * FT + (FT + s))
                    act.activation(sgE[:, s % 2, :], bank[s % 2][:, 0:CAP], ACT.Silu).then_inc(sem("silu_done"), 1)
                for half in range(2):
                    act.wait_ge(sem("ye_full"), q * 2 + (half + 1))
                    act.activation(ye[0:CAP, 512 * half:512 * half + 512], bank[4 + half][0:CAP, :],
                                   ACT.Copy).then_inc(sem("ye_done"), 1)

            with act.Fori(0, NE) as e:
                expert(e)
            act.wait_ge(sem("cnt_done"), 1)
            most = act.value_load(cnt[0:1, 0:1])
            with act.If(most > CAP):
                with act.Fori(NE, PASSES * NE) as q:
                    expert(q)
            rms(("end", 0), ("x_ffn", 2 * KD))
            root(5)

        @block.vector
        def _(v):
            def d(ins):
                then(v, ins, "v")

            def bc(ap, shape):
                return ap.broadcast_to(shape)

            def mean_root(ps, n, width):
                return v.tensor_scalar(ssb[:, :], ps[:, 0:N], 1.0 / width, EPS, ALU.mult, ALU.add)

            state = {"norms": 0}

            def norm(l, which, g, at):
                n = state["norms"]
                state["norms"] += 1
                d(v.scalar_tensor_tensor(mod[:, at + 8:at + 16, :], mod[:, at + 8:at + 16, :], 1.0,
                                         bc(col(l, g)[:, :, None], [P, KD, 1 + NB]), ALU.add, ALU.mult))
                name = ("rms", which, l)
                ps = filled(v, name)
                takes(v, mean_root(ps, n, D), name)
                v.tensor_copy(ini[:, 3:4], ssb[:, 0:1]).then_inc(sem("ss_done"), 1)
                v.wait_ge(sem("root_done"), n + 1)
                d(v.reciprocal(rstd[:, :], rstd[:, :]))
                for k in range(KD):
                    v.scalar_tensor_tensor(hT[:, k, 0:SEQ], xT[:, k, 0:SEQ], mod[:, at + 8 + k, 0:1], rstd[:, 0:SEQ],
                                           ALU.mult, ALU.mult).then_inc(sem("h_scaled"), 1)
                hs = hT[:, :, SEQ:N]
                d(v.tensor_tensor(hs, xT[:, :, SEQ:N], bc(rstd[:, None, SEQ:N], [P, KD, NB]), ALU.mult))
                d(v.tensor_tensor(hs, hs, mod[:, at + 8:at + 16, 1:1 + NB], ALU.mult))
                v.tensor_tensor(hs, hs, mod[:, at:at + 8, 1:1 + NB], ALU.add).then_inc(sem("h_smp"), 1)

            def c_(i):
                return sm[:, i, :]

            def tt(o, a, b, op):
                d(v.tensor_tensor(o, a, b, op))

            def ts(o, a, s1, s2, op0, op1=ALU.bypass):
                if s2 is None:
                    d(v.tensor_scalar(o, a, s1, None, op0))
                else:
                    d(v.tensor_scalar(o, a, s1, s2, op0, op1))

            MAGIC = 12582912.0

            def exp_to(o, x, k, r):
                ts(k, x, 1.4426950408889634, None, ALU.mult)
                ts(k, k, 126.0, -126.0, ALU.min, ALU.max)
                ts(k, k, MAGIC, None, ALU.add)
                ts(k, k, -MAGIC, None, ALU.add)
                d(v.scalar_tensor_tensor(r, k, -0.693359375, x, ALU.mult, ALU.add))
                d(v.scalar_tensor_tensor(r, k, 2.12194440e-4, r, ALU.mult, ALU.add))
                ts(o, r, 1.0 / 5040, 1.0 / 720, ALU.mult, ALU.add)
                for a in (1 / 120, 1 / 24, 1 / 6, 0.5, 1.0, 1.0):
                    tt(o, o, r, ALU.mult)
                    ts(o, o, a, None, ALU.add)
                ts(k, k, 127.0, None, ALU.add)
                d(v.tensor_copy(smi[:, :], k))
                d(v.tensor_single_scalar(smi[:, :], smi[:, :], 23, ALU.logical_shift_left))
                tt(o, o, smi[:, :].bitcast(F32), ALU.mult)

            def s5_params(l):
                lr, li = col(l, "lam_re"), col(l, "lam_im")
                dt, mag, th, k, r, co, si = (c_(i) for i in range(7))
                exp_to(dt, col(l, "log_dt"), k, r)
                tt(th, lr, dt, ALU.mult)
                exp_to(mag, th, k, r)
                tt(th, li, dt, ALU.mult)
                ts(k, th, 1.0 / (2 * math.pi), None, ALU.mult)
                ts(k, k, MAGIC, None, ALU.add)
                ts(k, k, -MAGIC, None, ALU.add)
                d(v.scalar_tensor_tensor(r, k, -6.28125, th, ALU.mult, ALU.add))
                d(v.scalar_tensor_tensor(r, k, -1.9350051879882812e-3, r, ALU.mult, ALU.add))
                d(v.scalar_tensor_tensor(r, k, -3.0199159819e-7, r, ALU.mult, ALU.add))
                ts(r, r, 0.5, None, ALU.mult)
                ts(c_(7), r, -1.0, None, ALU.mult)
                tt(c_(7), c_(7), r, ALU.max)
                d(v.tensor_scalar(c_(7), c_(7), -1.0, math.pi / 2, ALU.mult, ALU.add))
                for o, x in ((c_(8), r), (c_(9), c_(7))):
                    tt(c_(10), x, x, ALU.mult)
                    ts(o, c_(10), 1.0 / 6227020800, -1.0 / 39916800, ALU.mult, ALU.add)
                    for a in (1.0 / 362880, -1.0 / 5040, 1.0 / 120, -1.0 / 6, 1.0):
                        tt(o, o, c_(10), ALU.mult)
                        ts(o, o, a, None, ALU.add)
                    tt(o, o, x, ALU.mult)
                tt(si, c_(8), c_(9), ALU.mult)
                ts(si, si, 2.0, None, ALU.mult)
                tt(co, c_(8), c_(8), ALU.mult)
                d(v.tensor_scalar(co, co, -2.0, 1.0, ALU.mult, ALU.add))
                v.tensor_copy(c_(11), co).then_inc(sem("rot_done"), 1)
                ar_, ai, nr, den, kr, ki = (c_(i) for i in range(12, 18))
                tt(ar_, mag, co, ALU.mult)
                tt(ai, mag, si, ALU.mult)
                ts(nr, ar_, -1.0, None, ALU.add)
                tt(den, lr, lr, ALU.mult)
                tt(c_(18), li, li, ALU.mult)
                tt(den, den, c_(18), ALU.add)
                d(v.reciprocal(den, den))
                tt(kr, nr, lr, ALU.mult)
                tt(c_(18), ai, li, ALU.mult)
                tt(kr, kr, c_(18), ALU.add)
                tt(kr, kr, den, ALU.mult)
                tt(ki, ai, lr, ALU.mult)
                tt(c_(18), nr, li, ALU.mult)
                tt(ki, ki, c_(18), ALU.subtract)
                tt(ki, ki, den, ALU.mult)
                v.wait_ge(sem("c5_in"), 16 * (l + 1))
                W = [P, JT, 32]
                krb, kib = bc(kr[:, :, None], W), bc(ki[:, :, None], W)
                cr, ci, o, o2 = cpk[:, :, 0, :], cpk[:, :, 1, :], ckk[:, :, 0, :], ckk[:, :, 1, :]
                scr = wrot.rearrange("p a b -> p (a b)").rearrange("p (a b) -> p a b", b=32)
                tt(o, cr, krb, ALU.mult)
                tt(scr, ci, kib, ALU.mult)
                tt(o, o, scr, ALU.subtract)
                tt(o2, cr, kib, ALU.mult)
                tt(scr, ci, krb, ALU.mult)
                tt(o2, o2, scr, ALU.add)
                ts(o2, o2, -1.0, None, ALU.mult)
                ts(ci, ci, -1.0, None, ALU.mult)

            def s5_samples(l):
                name = ("bus", l)
                ps = filled(v, name)[:, 0:2 * JT * NB].rearrange("p (j c b) -> p j c b", c=2, b=NB)
                if l == 0:
                    v.wait_ge(ld["s5s"], 16)
                W = [P, JT, NB]
                a, b, e = (sx[:, i, :].rearrange("p (j b) -> p j b", b=NB) for i in range(3))
                A = [bc(c_(i)[:, :, None], W) for i in (12, 13, 16, 17)]
                sr, si = s5s[:, l, :, 0, :], s5s[:, l, :, 1, :]
                br, bi = ps[:, :, 0, :], ps[:, :, 1, :]
                tt(a, sr, A[0], ALU.mult)
                tt(e, si, A[1], ALU.mult)
                tt(a, a, e, ALU.subtract)
                tt(e, br, A[2], ALU.mult)
                tt(a, a, e, ALU.add)
                tt(e, bi, A[3], ALU.mult)
                tt(a, a, e, ALU.subtract)
                tt(b, sr, A[1], ALU.mult)
                tt(e, si, A[0], ALU.mult)
                tt(b, b, e, ALU.add)
                tt(e, br, A[3], ALU.mult)
                tt(b, b, e, ALU.add)
                takes(v, v.tensor_tensor(e, bi, A[2], ALU.mult), name)
                tt(si, b, e, ALU.add)
                v.tensor_copy(sr, a).then_inc(sem("s_smp"), 1)
                v.wait_ge(sem("s_smp"), l + 1)
                if l:
                    v.wait_ge(sem("s5_out"), 16)
                d(v.tensor_copy(s5o[:, :, :, 1:1 + NB], s5s[:, l]))

            def s5_tile(l, j):
                name = ("bu", l, j)
                ps = filled(v, name)[:, :].rearrange("p (c f t) -> p c f t", c=2, f=2)
                V = [P, 2, 2, HALF]
                cb = bc(cosT[:, j, None, None, :], V)
                sbn = bc(sinT[:, j, :, None, :], V)
                w4 = wrot.rearrange("p c (f t) -> p c f t", f=2)
                t4 = trot.rearrange("p c (f t) -> p c f t", f=2)
                u4 = trot2.rearrange("p c (f t) -> p c f t", f=2)
                tt(w4, ps, cb, ALU.mult)
                takes(v, v.tensor_tensor(t4, ps[:, ::-1], sbn, ALU.mult), name)
                tt(w4, w4, t4, ALU.add)
                decay = bc(c_(1)[:, j:j + 1], [P, HALF])
                for c in range(2):
                    d(v.tensor_tensor_scan(t4[:, c, 0, :], decay, w4[:, c, 0, :], 0.0, ALU.mult, ALU.add))
                last_re, last_im = t4[:, 0, 0, HALF - 1:HALF], t4[:, 1, 0, HALF - 1:HALF]
                cE, sE, msE = pw[:, 0, j:j + 1], pw[:, 1, j:j + 1], pw[:, 2, j:j + 1]
                d(v.tensor_scalar(ini[:, 2:3], last_re, cE, None, ALU.mult))
                d(v.scalar_tensor_tensor(ini[:, 0:1], last_im, msE, ini[:, 2:3], ALU.mult, ALU.add))
                d(v.tensor_scalar(ini[:, 2:3], last_im, cE, None, ALU.mult))
                d(v.scalar_tensor_tensor(ini[:, 1:2], last_re, sE, ini[:, 2:3], ALU.mult, ALU.add))
                for c in range(2):
                    d(v.tensor_tensor_scan(t4[:, c, 1, :], decay, w4[:, c, 1, :], ini[:, c:c + 1], ALU.mult, ALU.add))
                if j >= 8:
                    filled(v, ("y", l, j // 4 - 2))
                s4 = st[:, j % 8].rearrange("p c (f t) -> p c f t", f=2)
                tt(w4, t4, cb, ALU.mult)
                tt(u4, t4[:, ::-1], sbn, ALU.mult)
                v.tensor_tensor(s4, w4, u4, ALU.subtract).then_inc(sem("s_back"), 1)
                v.wait_ge(sem("s_back"), JT * l + j + 1)
                fr, fi = st[:, j % 8, 0, SEQ - 1:SEQ], st[:, j % 8, 1, SEQ - 1:SEQ]
                kr, ki = c_(16)[:, j:j + 1], c_(17)[:, j:j + 1]
                d(v.tensor_tensor(ini[:, 2:3], fi, ki, ALU.mult))
                d(v.scalar_tensor_tensor(s5o[:, j, 0, 0:1], fr, kr, ini[:, 2:3], ALU.mult, ALU.subtract))
                d(v.tensor_tensor(ini[:, 2:3], fi, kr, ALU.mult))
                ins = v.scalar_tensor_tensor(s5o[:, j, 1, 0:1], fr, ki, ini[:, 2:3], ALU.mult, ALU.add)
                if j == JT - 1:
                    ins.then_inc(sem("s5o_done"), 1)
                else:
                    d(ins)

            def conv_tile(l, i):
                taken(v, ("in", l, UT + i))
                w = lambda t: col(l, "conv_w", QT * t + i, 1)
                o = cv[:, i, 0:SEQ]
                d(v.tensor_scalar(o, raw[:, i, 0:SEQ], w(0), None, ALU.mult))
                for t in range(1, TAPS):
                    d(v.scalar_tensor_tensor(o, raw[:, i, t:t + SEQ], w(t), o, ALU.mult, ALU.add))

            def conv_samples(l):
                W = [P, QT, NB]
                wv = lambda t: bc(col(l, "conv_w", QT * t, QT)[:, :, None], W)
                o = cv[:, :, SEQ:N]
                e = sx[:, 0, 0:QT * NB].rearrange("p (i b) -> p i b", b=NB)
                if l == 0:
                    v.wait_ge(ld["conv0"], 16)
                tt(o, conv0[:, l, :, :, 0], wv(0), ALU.mult)
                for t in range(1, TAPS):
                    src = conv0[:, l, :, :, t] if t < 3 else raw[:, :, 3 + SEQ:3 + N]
                    tt(e, src, wv(t), ALU.mult)
                    if t < 3:
                        tt(o, o, e, ALU.add)
                if l:
                    v.wait_ge(sem("cv_out"), 16)
                d(v.tensor_copy(cvo[:, :, 0, :], raw[:, :, SEQ:SEQ + 3]))
                d(v.tensor_copy(cvo[:, :, 1:1 + NB, 0:2], conv0[:, l, :, :, 1:3]))
                v.tensor_copy(cvo[:, :, 1:1 + NB, 2], raw[:, :, 3 + SEQ:3 + N]).then_inc(sem("cvo_done"), 1)
                v.wait_ge(sem("cvo_done"), l + 1)
                v.tensor_tensor(o, o, e, ALU.add).then_inc(sem("conv_done"), 1)

            def gate_logits(l):
                name = ("ab", l)
                ps = filled(v, name)[:, 0:24].rearrange("p (g w) -> p g w", w=8)
                if l == 0:
                    d(v.memset(gd[:, :, :], 0.0))
                x, ax, be = (gd[:, i, :].rearrange("p (g h) -> p g h", h=NH) for i in (2, 1, 4))
                bias = col(l, "dt_bias")
                for g0, g1, m in ((0, 2, P), (2, 3, NB)):
                    tt(x[0:m, g0:g1], ps[0:m, g0:g1, 0:NH], bc(bias[0:m, None, :], [m, g1 - g0, NH]), ALU.add)
                d(v.tensor_copy(be[:, 0:2], ps[:, 0:2, NH:]))
                takes(v, v.tensor_copy(be[0:NB, 2:3], ps[0:NB, 2:3, NH:]), name)
                ts(ax, x, -1.0, None, ALU.mult)
                v.tensor_tensor(ax, ax, x, ALU.max).then_inc(sem("ax_done"), 1)

            def gdn_columns(l):
                g3 = [P, 3, NH]
                r = lambda i: gd[:, i, :].rearrange("p (g h) -> p g h", h=NH)
                v.wait_ge(sem("a_ln"), 3 * (l + 1))
                ts(r(2), r(2), 0.0, None, ALU.max)
                tt(r(2), r(2), r(1), ALU.add)
                ts(gd[:, 3, 0:NH], gd[:, 3, 0:NH], -1.0, None, ALU.mult)
                v.tensor_tensor(r(0), r(2), bc(gd[:, 3, None, 0:NH], g3), ALU.mult).then_inc(sem("g_done"), 1)

            def qk_norms(l):
                for i in range(2 * NH):
                    name = ("qkn", l, i)
                    takes(v, v.tensor_scalar(nrm[:, i, :], filled(v, name)[:, 0:N], EPS, None, ALU.add), name)
                v.tensor_copy(ini[:, 3:4], nrm[:, 0, 0:1]).then_inc(sem("nrm_ss"), 1)
                v.wait_ge(sem("nrm_root"), l + 1)
                d(v.reciprocal(nrm[:, :, :], nrm[:, :, :]))
                q, k = cv[:, 0:NH, :], cv[:, NH:2 * NH, :]
                v.wait_ge(sem("cv_silu"), 3 * (l + 1))
                d(v.scalar_tensor_tensor(q, q, HD ** -0.5, nrm[:, 0:NH, :], ALU.mult, ALU.mult))
                v.tensor_tensor(k, k, nrm[:, NH:2 * NH, :], ALU.mult).then_inc(sem("qk_done"), 1)
                v.wait_ge(sem("qk_done"), l + 1)

            def gdn(l):
                H4 = [P, NH, P]
                name = ("gcc", l)
                gc = gd[:, 5, 0:8]
                takes(v, v.tensor_copy(gc, filled(v, name)[:, 0:8]), name)
                psb = [filled(v, ("gcb", l, c))[:, :].rearrange("p (h t) -> p h t", h=NH) for c in range(NC)]
                c4 = lambda i, c: gd[:, i, 4 * c:4 * c + 4]
                for c in range(NC):
                    d(v.tensor_copy(c4(7, c), c4(5, c)))
                    d(v.tensor_copy(c4(9, c), psb[c][:, :, P - 1]))
                    tt(c4(8, c), c4(9, c), c4(5, c), ALU.subtract)
                v.tensor_copy(ini[:, 3:4], gd[:, 8, 0:1]).then_inc(sem("gdx_done"), 1)
                for c in range(NC):
                    bank_t = psb[c]
                    col_t = bc(c4(5, c)[:, :, None], H4)
                    tt(mats["decT"][c], bank_t, col_t, ALU.subtract)
                    ts(mats["dec"][c], mats["decT"][c], -1.0, 0.0, ALU.mult, ALU.min)
                    v.tensor_scalar(mats["decT"][c], mats["decT"][c], 0.0, None, ALU.min).then_inc(sem("diff_done"), 1)
                v.wait_ge(sem("a_col"), 2 * (l + 1))
                tt(gd[:, 10, 0:8], gd[:, 7, 0:8], gd[:, 4, 0:8], ALU.mult)
                for c in range(NC):
                    v.wait_ge(sem("a_dec"), 2 * NC * l + 2 * c + 2)
                    tt(mats["decT"][c], mats["decT"][c], bc(upper[:, None, :], H4), ALU.mult)
                    tt(mats["dec"][c], mats["dec"][c], bc(strict[:, None, :], H4), ALU.mult)
                    tt(mats["dec"][c], mats["dec"][c], bc(c4(4, c)[:, :, None], H4), ALU.mult)
                    name = ("ktok", l, c)
                    ps = filled(v, name)[:, :].rearrange("p (h t) -> p h t", h=NH)
                    tt(mats["kg"][c], ps, bc(c4(8, c)[:, :, None], H4), ALU.mult)
                    takes(v, v.tensor_tensor(mats["kbg"][c], ps, bc(c4(10, c)[:, :, None], H4), ALU.mult), name)
                    name = ("kk", l, c)
                    ps = filled(v, name)[:, :].rearrange("p (h t) -> p h t", h=NH)
                    takes(v, v.tensor_tensor(mats["ln"][c], ps, mats["dec"][c], ALU.mult), name)
                    v.tensor_scalar(mats["ln"][c], mats["ln"][c], -1.0, None, ALU.mult).then_inc(sem("ln_done"), 1)
                    v.wait_ge(sem("ln_done"), NC * l + c + 1)
                    name = ("qk", l, c)
                    ps = filled(v, name)[:, :].rearrange("p (h t) -> p h t", h=NH)
                    takes(v, v.tensor_tensor(mats["att"][c], ps, mats["decT"][c], ALU.mult), name)
                    taken(v, ("gcb", l, c))
                    v.tensor_tensor(mats["qg"][c], mats["qg"][c], cv[:, 0:NH, P * c:P * c + P],
                                    ALU.mult).then_inc(sem("qg_done"), 1)
                for c in range(NC):
                    name = ("lt", l, c)
                    ps = filled(v, name)[:, :].rearrange("p (h t) -> p h t", h=NH)
                    tt(mats["e"][c], mats["ln"][c], bc(blk[:, None, :], H4), ALU.mult)
                    takes(v, v.tensor_copy(mats["lnT"][c], ps), name)
                    tt(mats["p"][c], mats["e"][c], bc(ident[:, None, :], H4), ALU.add)
                    tt(mats["eT"][c], mats["lnT"][c], bc(blkT[:, None, :], H4), ALU.mult)
                    v.tensor_tensor(mats["pT"][c], mats["eT"][c], bc(ident[:, None, :], H4),
                                    ALU.add).then_inc(sem("e_done"), 1)
                    v.wait_ge(sem("e_done"), NC * l + c + 1)
                    name = ("vtok", l, c)
                    ps = filled(v, name)[:, :].rearrange("p (h t) -> p h t", h=NH)
                    takes(v, v.tensor_tensor(mats["vb"][c], ps, bc(c4(4, c)[:, :, None], H4), ALU.mult), name)
                for s in range(3):
                    for c in range(NC):
                        filled(v, ("pT", l, s, c))
                        for n in ("p", "pT"):
                            name = (n, l, s, c)
                            ps = filled(v, name)[:, :].rearrange("p (h t) -> p h t", h=NH)
                            takes(v, v.tensor_tensor(mats[n][c], mats[n][c], ps, ALU.add), name)
                for s in range(3):
                    for c in range(NC):
                        v.tensor_tensor(mats["eT"][c], mats["lnT"][c], bc(masks[:, 5 + s, None, :], H4),
                                        ALU.mult).then_inc(sem("lev_done"), 1)
                    for c in range(NC):
                        filled(v, ("xT", l, s, c))
                        for n, m in (("p", "x"), ("pT", "xT"))[s == 2:]:
                            name = (m, l, s, c)
                            ps = filled(v, name)[:, :].rearrange("p (h t) -> p h t", h=NH)
                            takes(v, v.tensor_tensor(mats[n][c], mats[n][c], ps, ALU.add), name)
                for c in range(NC):
                    name = ("s", l, c)
                    if c == 0:
                        ps = filled(v, name)[:, :].rearrange("p (h t) -> p h t", h=NH)
                        takes(v, v.tensor_copy(s_pr, ps), name)
                    else:
                        ps = filled(v, name)[:, :].rearrange("p (h t) -> p h t", h=NH)
                        tt(s_pr, s_pr, bc(c4(9, c)[:, :, None], H4), ALU.mult)
                        takes(v, v.tensor_tensor(s_pr, s_pr, ps, ALU.add), name)

            def gdn_samples(l):
                hb = NH * NB
                W = [NB, NH, NB]
                v.wait_ge(sem("a_col"), 2 * (l + 1))
                idb = bc(ident[0:NB, None, 0:NB], W)
                tt(dg[:, 0], bc(gd[0:NB, 11, 8:12, None], W), idb, ALU.mult)
                v.tensor_tensor(dg[:, 1], bc(gd[0:NB, 4, 8:12, None], W), idb, ALU.mult).then_inc(sem("dg_done"), 1)
                q, k, vv = (cv[:, NH * i:NH * i + NH, SEQ:N] for i in range(3))
                r = lambda ap: ap.rearrange("p (h b) -> p h b", b=NB)
                d(v.tensor_copy(r(sx[:, 2, 0:hb]), k))
                v.tensor_tensor(r(sx[:, 0, 0:hb]), q, k, ALU.mult).then_inc(sem("qkp_done"), 1)
                name = ("skt", l)
                takes(v, v.tensor_copy(ktk[:, :], filled(v, name)[0:hb, 0:P]), name)
                name = ("sgb", l)
                takes(v, v.tensor_copy(rowb[:, :, :].rearrange("p a b -> p (a b)"), filled(v, name)[:, 0:2 * hb]), name)
                eg, be = rowb[:, 0, :], rowb[:, 1, :]
                name = ("skq", l)
                ps = filled(v, name)[:, 0:2 * hb].rearrange("p (i c) -> p i c", c=2)
                vn, t, o = sx[:, 1, 0:hb], sx[:, 2, 0:hb], sx[:, 3, 0:hb]
                tt(t, ps[:, :, 1], eg, ALU.mult)
                takes(v, v.tensor_tensor(o, ps[:, :, 0], eg, ALU.mult), name)
                tt(r(vn), vv, r(t), ALU.subtract)
                v.tensor_tensor(vn, vn, be, ALU.mult).then_inc(sem("svn_done"), 1)
                v.wait_ge(sem("svn_done"), l + 1)
                name = ("sqk", l)
                takes(v, v.tensor_tensor(t, filled(v, name)[:, 0:hb], vn, ALU.mult), name)
                v.tensor_tensor(oT[:, :, SEQ:N], r(o), r(t), ALU.add).then_inc(sem("os_done"), 1)
                name = ("svt", l)
                ps = filled(v, name)[0:hb, None, 0:P]
                gives(v.tensor_tensor(vm[0:hb], bc(ps, [hb, hb, P]), bc(ident[0:hb, 0:hb, None], [hb, hb, P]),
                                      ALU.mult), name)
                taken(v, name)
                v.tensor_copy(ini[:, 3:4], eg[:, 0:1]).then_inc(sem("vm_done"), 1)
                d(v.tensor_tensor(s0, s0, bc(eg[:, :, None], [P, hb, P]), ALU.mult))
                for i in range(NB):
                    name = ("so", l, i)
                    ps = filled(v, name)[:, :].rearrange("p (a b) -> p a b", b=P)
                    gives(v.tensor_tensor(s0[:, 4 * i:4 * i + 4, :], s0[:, 4 * i:4 * i + 4, :], ps, ALU.add), name)

            def gdn_output(l):
                for h in range(NH):
                    name = ("on", l, h)
                    takes(v, v.tensor_scalar(nrm[:, h, :], filled(v, name)[:, 0:N], 1.0 / HD, EPS, ALU.mult, ALU.add),
                          name)
                v.tensor_copy(ini[:, 3:4], nrm[:, 0, 0:1]).then_inc(sem("on_ss"), 1)
                v.wait_ge(sem("on_root"), l + 1)
                n4 = nrm[:, 0:NH, :]
                d(v.reciprocal(n4, n4))
                d(v.scalar_tensor_tensor(oT, oT, col(l, "gdn_w"), n4, ALU.mult, ALU.mult))
                v.tensor_tensor(oT, oT, zs[:, :, :], ALU.mult).then_inc(sem("o_done"), 1)

            def mixer(l):
                name = ("ada", l)
                if l == 0:
                    v.wait_ge(ld["cols"], 16)
                    v.wait_ge(ld["x"], 16)
                    s5_params(0)
                ps = filled(v, name)[:, 0:ADA_T * (1 + NB)].rearrange("p (m b) -> p m b", b=1 + NB)
                takes(v, v.tensor_tensor(mod[:, :, :], ps, bc(col(l, "b_ada")[:, :, None], [P, ADA_T, 1 + NB]), ALU.add),
                      name)
                norm(l, "mix", "g_mix", 0)
                gate_logits(l)
                v.wait_ge(sem("tab_done"), l + 1)
                s5_samples(l)
                for m in range(UT, IN_T):
                    if m < UT + QT:
                        conv_tile(l, m - UT)
                        if m == UT + QT - 1:
                            conv_samples(l)
                    if (m - UT) % 2 == 1:
                        s5_tile(l, (m - UT) // 2)
                    if (m - UT) % 8 == 7 and m - UT > 8:
                        s5_output(l, (m - UT) // 8 - 1)
                s5_output(l, UT - 1)
                taken(v, ("in", l, IN_T - 1))
                for m in range(KD):
                    taken(v, ("glu", l, 2 * m + 1))
                    name = ("glu", l, 2 * m)
                    ga = gates[:, m, :]
                    takes(v, v.tensor_tensor(ga, ga, filled(v, name)[:, 0:N], ALU.mult), name)
                    v.tensor_tensor(ga, ga, tmp[:, m % 2, :], ALU.mult).then_inc(sem("glu_done"), 1)
                gdn_columns(l)
                qk_norms(l)
                gdn(l)
                v.tensor_copy(ini[:, 3:4], s_pr[:, 0, 0:1]).then_inc(sem("sp_done"), 1)
                gdn_samples(l)
                gdn_output(l)
                v.wait_ge(sem("glu_done"), KD * (l + 1))
                for m in range(KD):
                    name = ("go", l, m)
                    takes(v, v.tensor_tensor(hT[:, m, :], gates[:, KD + m, :], filled(v, name)[:, 0:N], ALU.mult), name)
                    v.tensor_tensor(hT[:, m, :], hT[:, m, :], gates[:, m, :], ALU.add).then_inc(sem("merged"), 1)
                residual(lambda m: (filled(v, ("wo", l, m)), lambda ins: gives(ins, ("wo", l, m))), 16, "x_mix")

            def residual(src, at, done):
                for m in range(KD):
                    ps, mark = src(m)
                    e = tmp[:, 0, 0:NB]
                    d(v.tensor_tensor(e, ps[:, SEQ:N], mod[:, at + m, 1:1 + NB], ALU.mult))
                    d(v.tensor_tensor(xT[:, m, SEQ:N], xT[:, m, SEQ:N], e, ALU.add))
                    ins = v.scalar_tensor_tensor(xT[:, m, 0:SEQ], ps[:, 0:SEQ], mod[:, at + m, 0:1], xT[:, m, 0:SEQ],
                                                 ALU.mult, ALU.add)
                    mark(ins)
                    v.tensor_copy(ini[:, 3:4], mod[:, at + m, 0:1]).then_inc(sem(done), 1)

            def s5_output(l, i):
                name = ("y", l, i)
                ps = filled(v, name)[:, 0:N]
                gives(v.scalar_tensor_tensor(uT[:, i, :], uT[:, i, :], col(l, "s5_d", i, 1), ps, ALU.mult, ALU.add), name)
                taken(v, name)
                v.tensor_copy(ini[:, 3:4], uT[:, i, 0:1]).then_inc(sem("y_sum"), 1)

            def route():
                lg = rtx[:, 0:3, :]
                name = ("rl",)
                ps = filled(v, name)[:, 0:24].rearrange("p (g e) -> p g e", e=NE)
                d(v.memset(rtx[:, :, :], 0.0))
                br = col(1, "b_router")
                tt(lg[:, 0:2], ps[:, 0:2], bc(br[:, None, :], [P, 2, NE]), ALU.add)
                takes(v, v.tensor_tensor(lg[0:NB, 2:3], ps[0:NB, 2:3], bc(br[0:NB, None, :], [NB, 1, NE]), ALU.add), name)
                v.wait_ge(ld["sel"], 16)
                W = [P, NE, NE]
                big = ar(8 * B1, 2, NE, NE)
                for g in range(3):
                    mine, other = bc(lg[:, g, :, None], W), bc(lg[:, g, None, :], W)
                    tt(big[:, 0], other, mine, ALU.is_gt)
                    tt(big[:, 1], other, mine, ALU.is_equal)
                    tt(big[:, 1], big[:, 1], selw[:, :, :], ALU.mult)
                    tt(big[:, 0], big[:, 0], big[:, 1], ALU.add)
                    d(v.tensor_reduce(rtx[:, 3 + g, :], big[:, 0], AX.X, ALU.add))
                d(v.tensor_scalar(rt[:, :, :], rtx[:, 3:6, :], 2.0, None, ALU.is_lt))
                d(v.tensor_reduce(rtx[:, 9, 0:3], lg, AX.X, ALU.max))
                v.tensor_tensor(rtx[:, 6:9, :], lg, bc(rtx[:, 9, 0:3, None], [P, 3, NE]),
                                ALU.subtract).then_inc(sem("sel_done"), 1)
                v.wait_ge(sem("rexp_done"), 1)
                cw = rtx[:, 6:9, :]
                tt(cw, cw, rt[:, :, :], ALU.mult)
                d(v.tensor_reduce(rtx[:, 9, 0:3], cw, AX.X, ALU.add))
                d(v.reciprocal(rtx[:, 9, 0:3], rtx[:, 9, 0:3]))
                tt(cw, cw, bc(rtx[:, 9, 0:3, None], [P, 3, NE]), ALU.mult)
                name = ("rank",)
                ps = filled(v, name)[:, 0:32].rearrange("p (g e) -> p g e", e=NE)
                pos = rtx[:, 3:6, :]
                tt(pos[:, 0:2], ps[:, 0:2], rt[:, 0:2, :], ALU.mult)
                tt(pos[0:NB, 2], ps[0:NB, 2], rt[0:NB, 2, :], ALU.mult)
                ts(pos, pos, -1.0, None, ALU.add)
                d(v.tensor_reduce(rtx[:, 10, 0:1], ps[:, 3], AX.X, ALU.max))
                takes(v, v.tensor_copy(cnt[:, :], rtx[0:1, 10, 0:1]), name)
                v.memset(acc, 0.0).then_inc(sem("cnt_done"), 1)
                v.wait_ge(ld["iota"], 16)
                v.wait_ge(sem("cnt_done"), 1)

            def expert(q, e, a):
                pos, cw = rtx[:, 3:6, :], rtx[:, 6:9, :]
                io = iota[:, 0:CAP] if a is None else iota[:, bass.ds(a * CAP, CAP)]
                for g in range(3):
                    m = P if g < 2 else NB
                    p1, c1 = pos[0:m, g, bass.ds(e, 1)], cw[0:m, g, bass.ds(e, 1)]
                    ioa = iota[0:m, 0:CAP] if a is None else iota[0:m, bass.ds(a * CAP, CAP)]
                    v.tensor_scalar(dw[0:m, g, :], ioa, p1, c1, ALU.is_equal, ALU.mult)
                    ins = v.tensor_scalar(dsel[0:m, g, :], ioa, p1, None, ALU.is_equal)
                ins.then_inc(sem("dsel_done"), 1)
                for s in range(FT):
                    v.wait_ge(sem("silu_done"), q * FT + (FT + s + 1))
                    v.tensor_tensor(actE[:, s, :], sgE[:, s % 2, :], bank[s % 2][:, CAP:2 * CAP],
                                    ALU.mult).then_inc(sem("act_done"), 1)
                for m in range(KD):
                    v.wait_ge(sem("down_full"), q * KD + (KD + m + 1))
                    v.tensor_tensor(acc[:, m, :], acc[:, m, :], bank[2 + m % 2][:, 0:N],
                                    ALU.add).then_inc(sem("down_taken"), 1)

            v.memset(ones[:, :], 1.0).then_inc(sem("ones_done"), 1)
            v.wait_ge(ld["masks"], 16)
            mixer(0)
            norm(0, "ffn", "g_ffn", 24)
            v.tensor_copy(ini[:, 3:4], rstd[:, 0:1]).then_inc(sem("act_done"), 1)
            with v.Fori(0, FT // 2) as it:
                for s in range(2):
                    v.wait_ge(sem("silu_done"), it * 2 + (s + 1))
                    v.tensor_tensor(arena[:, bass.ds(it * (2 * N) + s * N, N)], sg[:, s, :], bank[2 * s + 1][:, 0:N],
                                    ALU.mult).then_inc(sem("act_done"), 1)

            def down(m):
                v.wait_ge(sem("down_full"), m + 1)
                return bank[4 + m % 2], lambda ins: ins.then_inc(sem("down_taken"), 1)

            residual(down, 40, "x_ffn")
            s5_params(1)
            mixer(1)
            norm(1, "ffn", "g_ffn", 24)
            route()
            with v.Fori(0, NE) as e:
                expert(e, e, None)
            v.wait_ge(sem("down_taken"), KD * (NE + 1))
            most = v.value_load(cnt[0:1, 0:1])
            with v.If(most > CAP):
                with v.Fori(1, PASSES) as a:
                    with v.Fori(0, NE) as e:
                        expert(a * NE + e, e, a)
                v.wait_ge(sem("down_taken"), KD * (PASSES * NE + 1))

            def summed(m):
                return acc[:, m, :], lambda ins: ins.then_inc(sem("fin_x"), 1)

            residual(summed, 40, "x_ffn")
            v.wait_ge(sem("end_full"), 1)
            d(mean_root(bank[0], 4, D))
            v.tensor_copy(ini[:, 3:4], ssb[:, 0:1]).then_inc(sem("ss_done"), 1)
            v.wait_ge(sem("root_done"), 5)
            d(v.reciprocal(rstd[:, :], rstd[:, :]))
            for k in range(KD):
                v.scalar_tensor_tensor(hT[:, k, :], xT[:, k, :], col(0, "g_final", k, 1), rstd[:, :],
                                       ALU.mult, ALU.mult).then_inc(sem("y_done"), 1)

        @block.gpsimd
        def _(pool):
            pool.memset(raw[:, :, 0:3], 0.0).then_inc(sem("pool_zero"), 1)

            def p(ins):
                then(pool, ins, "p")

            def tables(l):
                pool.wait_ge(sem("rot_done"), l + 1)
                cd, sd, ms, t1, t2 = (pw[:, i, :] for i in range(5))
                p(pool.tensor_copy(cd, sm[:, 5, :]))
                p(pool.tensor_copy(sd, sm[:, 6, :]))
                p(pool.memset(cosT[:, :, 0:1], 1.0))
                p(pool.memset(sinT[:, :, :, 0:1], 0.0))
                n = 1
                while n < HALF:
                    W = [P, JT, n]
                    c, s = cosT[:, :, 0:n], sinT[:, :, 0, 0:n]
                    co, so, x = cosT[:, :, n:2 * n], sinT[:, :, 0, n:2 * n], sinT[:, :, 1, n:2 * n]
                    cb, sbb = cd[:, :, None].broadcast_to(W), sd[:, :, None].broadcast_to(W)
                    p(pool.tensor_tensor(co, c, cb, ALU.mult))
                    p(pool.tensor_tensor(x, s, sbb, ALU.mult))
                    p(pool.tensor_tensor(co, co, x, ALU.subtract))
                    p(pool.tensor_tensor(so, s, cb, ALU.mult))
                    p(pool.tensor_tensor(x, c, sbb, ALU.mult))
                    p(pool.tensor_tensor(so, so, x, ALU.add))
                    p(pool.tensor_tensor(t1, cd, cd, ALU.mult))
                    p(pool.tensor_tensor(t2, sd, sd, ALU.mult))
                    p(pool.tensor_tensor(sd, sd, cd, ALU.mult))
                    p(pool.tensor_tensor(cd, t1, t2, ALU.subtract))
                    p(pool.tensor_scalar(sd, sd, 2.0, None, ALU.mult))
                    n *= 2
                p(pool.tensor_scalar(ms, sd, -1.0, None, ALU.mult))
                pool.tensor_scalar(sinT[:, :, 1, :], sinT[:, :, 0, :], -1.0, None, ALU.mult).then_inc(sem("tab_done"), 1)

            def layer(l):
                if l:
                    pool.wait_ge(sem("x_ffn"), KD)
                tables(l)
                pool.wait_ge(sem("cvo_done"), l + 1)
                pool.dma_start(conv_out[l], cvo[:, :, :, :]).then_inc(sem("cv_out"), 16)
                pool.wait_ge(sem("s5o_done"), l + 1)
                pool.dma_start(s5_out[l], s5o[:, :, :, :]).then_inc(sem("s5_out"), 16)
                pool.wait_ge(sem("sp_done"), l + 1)
                pool.dma_start(gdnp_out[l], s_pr).then_inc(sem("sp_out"), 16)
                for i in range(NB):
                    taken(pool, ("so", l, i))
                pool.dma_start(gdns_out[l], s0).then_inc(sem("gs_out"), 16)
                pool.wait_ge(sem("gs_out"), 16 * (l + 1))

            layer(0)
            layer(1)
            for n in ("cv_out", "s5_out", "sp_out"):
                pool.wait_ge(sem(n), 32)


def _blocks(w):
    K, M = w.shape
    return w.reshape(K // P, P, M // P, P).transpose(2, 0, 1, 3)


def _slots(blocks):
    n = blocks.shape[0]
    return blocks.reshape(n // SLOT, SLOT, P, P).transpose(0, 2, 1, 3).reshape(n // SLOT, P, SLOT * P)


def _flat(tiles):
    return tiles.reshape(-1, P, P)


def _pairs(w):
    b = _blocks(w)
    h = b.shape[0] // 2
    return _flat(np.stack([b[:h], b[h:]], axis=1))


def _fm(a):
    r, f = a.shape
    return a.T.reshape(f // P, P, r).transpose(1, 0, 2)


def _const():
    i = np.arange(P)
    r, c = i[:, None], i[None, :]
    m = {"ident": r == c, "upper": r <= c, "strict": r > c}
    m["blk"] = (r > c) & (r // BASE == c // BASE)
    m["blkT"] = m["blk"].T
    for s in range(3):
        b = BASE << s
        m[f"lev{s}"] = (r // (2 * b) == c // (2 * b)) & (r // b % 2 == 0) & (c // b % 2 == 1)
    masks = np.stack([m[n] for n in MASKS], axis=1).astype(np.float32)
    iota = np.broadcast_to(np.arange(PASSES * CAP, dtype=np.float32), (P, PASSES * CAP)).copy()
    sel = np.broadcast_to((np.arange(NE)[None, :] < np.arange(NE)[:, None]).astype(np.float32), (P, NE, NE)).copy()
    return masks, iota, sel


def layouts(i):
    L = range(DEPTH)
    x = np.concatenate([i["x_prompt"][0], i["x_sample"][:, 0]], axis=0)
    c = np.concatenate([i["c_prompt"], i["c_sample"]], axis=0)
    masks, iota, sel = _const()
    feat = lambda v: v.reshape(-1, P).T
    row = lambda v: np.broadcast_to(v[None, :], (P, v.shape[0]))
    cols = []
    for l in L:
        dt = np.repeat(i["s5_log_dt"][l], ST)
        parts = dict(g_mix=feat(i["g_mix"][l]), g_ffn=feat(i["g_ffn"][l]), b_ada=feat(i["b_ada"][l]),
                     s5_d=feat(i["s5_d"][l]), conv_w=feat(i["gdn_conv_w"][l].reshape(-1)),
                     gdn_w=i["gdn_norm_w"][l][:, None], lam_re=feat(i["s5_lambda_re"][l].reshape(-1)),
                     lam_im=feat(i["s5_lambda_im"][l].reshape(-1)), log_dt=feat(dt), a_log=row(i["gdn_a_log"][l]),
                     dt_bias=row(i["gdn_dt_bias"][l]), g_final=feat(i["g_final"]), b_router=row(i["b_router"][0]))
        cols.append(np.concatenate([parts[n] for n in COLS], axis=1))
    cols = np.stack(cols, axis=1)
    bpk = np.zeros((DEPTH, UT, 4, 2, C5, 2, 2, ST), np.float32)
    cpk = np.zeros((DEPTH, 2, ST, JT, 2, 2, C5), np.float32)
    for part, (bn, cn) in enumerate((("s5_b_re", "s5_c_re"), ("s5_b_im", "s5_c_im"))):
        b = i[bn].reshape(DEPTH, UT, 4, 2, ST, C5)
        cc = i[cn].reshape(DEPTH, JT, 2, C5, ST)
        for g in range(2):
            bpk[:, :, :, g, :, part, g, :] = b[:, :, :, g].transpose(0, 1, 2, 4, 3)
            cpk[:, g, :, :, part, g, :] = cc[:, :, g].transpose(0, 3, 1, 2)
    bpk = bpk.reshape(DEPTH, UT, P, 2, P).transpose(0, 2, 1, 3, 4)
    cpk = cpk.reshape(DEPTH, P, JT, 2, 32)
    s5 = np.stack([i["state_s5_re"], i["state_s5_im"]], axis=1).reshape(DEPTH, 2, NB, JT, P).transpose(4, 0, 3, 1, 2)
    gdn = i["state_gdn"].transpose(0, 3, 2, 1, 4).reshape(DEPTH, P, NH * NB, P)
    conv = i["state_conv"].reshape(DEPTH, NB, 3, QT, P).transpose(4, 0, 3, 1, 2)
    ab = S5W + 3 * NH * HD + NH * HD
    wab = np.stack([i["w_in"][l][:, ab:ab + 2 * NH].reshape(KD, P, 2 * NH).transpose(1, 0, 2) for l in L], axis=1)
    wr = i["w_router"][0].reshape(KD, P, NE).transpose(1, 0, 2)
    parts = []
    for l in L:
        w = i["w_in"][l]
        w = np.concatenate([w[:, :ab], w[:, ab + 2 * NH:]], axis=1)
        parts += [_slots(_flat(_blocks(i["w_ada"][l]))), _slots(_flat(_blocks(w))),
                  _slots(_pairs(i["w_s5_glu"][l])), _slots(_flat(_blocks(i["w_gdn_out"][l]))),
                  _slots(_flat(_blocks(i["w_out"][l])))]
        if l == 0:
            parts += [_slots(_pairs(i["w_ffn_gate_up"][0])), _slots(_flat(_blocks(i["w_ffn_down"][0])))]
    for e in range(NE):
        parts += [_slots(_pairs(i["w_exp_gate_up"][0, e])),
                  i["w_exp_down"][0, e].reshape(DOWN_S, 2, P, D).transpose(0, 2, 1, 3).reshape(DOWN_S, P, 2 * D)]
    w = np.concatenate(parts, axis=0)
    return dict(x=_fm(x), c=_fm(c), cols=cols, masks=masks, iota=iota, sel=sel, bpk=bpk, cpk=cpk, s5s=s5, gdn=gdn,
                conv=conv, wab=wab, wr=wr, w=w)


OUTS = {"y": (P, KD, N), "s5": (DEPTH, P, JT, 2, 1 + NB), "gdnp": (DEPTH, P, NH, P), "gdns": (DEPTH, P, NH * NB, P),
        "convo": (DEPTH, P, QT, 1 + NB, 3)}


def kernel(**inputs):
    import concourse.bacc as bacc
    from concourse.bass_utils import run_bass_kernel_spmd

    nc = bacc.Bacc("TRN2", target_bir_lowering=False, num_devices=1)
    arrays, args = {}, []
    for name, a in layouts({k: np.asarray(v) for k, v in inputs.items()}).items():
        a = np.ascontiguousarray(a)
        arrays[f"in_{name}"] = a
        args.append(nc.dram_tensor(f"in_{name}", a.shape, F32, kind="ExternalInput").ap())
    for name, shape in OUTS.items():
        args.append(nc.dram_tensor(f"out_{name}", shape, F32, kind="ExternalOutput").ap())
    trunk_program(nc, *args)
    r = run_bass_kernel_spmd(nc, [arrays], core_ids=[0]).results[0]
    y = r["out_y"].transpose(2, 1, 0).reshape(N, D)
    s5 = r["out_s5"].transpose(0, 3, 4, 2, 1).reshape(DEPTH, 2, 1 + NB, G5, ST)
    gp = r["out_gdnp"].transpose(0, 2, 1, 3)[:, None]
    gs = r["out_gdns"].reshape(DEPTH, P, NH, NB, P).transpose(0, 3, 2, 1, 4)
    cv = r["out_convo"].transpose(0, 3, 4, 2, 1).reshape(DEPTH, 1 + NB, 3, QT * P)
    out = (y[None, :SEQ], y[SEQ:, None], s5[:, 0, :1], s5[:, 1, :1], gp, cv[:, :1], s5[:, 0, 1:], s5[:, 1, 1:], gs,
           cv[:, 1:])
    return tuple(np.ascontiguousarray(a) for a in out)
```

```python
import math
from contextlib import ExitStack

import numpy as np

import concourse.bass as bass
from concourse import mybir

ALU = mybir.AluOpType
ACT = mybir.ActivationFunctionType
AX = mybir.AxisListType
F32 = mybir.dt.float32
F32R = mybir.dt.float32r
I32 = mybir.dt.int32

P = 128
D = 1024
SEQ = 256
NB = 8
N = SEQ + NB
KD = D // P
DEPTH = 2
S5W = D // 2
G5, C5, ST = 32, 16, 64
UT = S5W // P
JT = G5 * ST // P
HD = 128
NH = 4
QT = 3 * NH
TAPS = 4
HALF = SEQ // 2
NC = SEQ // HALF
FF = 7 * D // 2
FT = FF // P
NE = 8
CAP = 128
PASSES = -(-N // CAP)
EPS = 1e-6

SLOT = 8
RING = 7
SPL = 4
ADA_T = 6 * D // P
ROUNDS = 3
ADA_S = KD * 2
S5_STEPS = JT
ADA_IN = ([(0, 1), (0, 2), (1, 0)], [(1, 1), (1, 2)])
MIX_S = 36 + 2 * KD * UT // SLOT + KD * NH // SLOT + KD * KD // SLOT
UP_S, DOWN_S = 2 * FT * KD // SLOT, FT * KD // SLOT
FFN_S = UP_S + DOWN_S
MIX0_END = ADA_S * (1 + len(ADA_IN[0])) + MIX_S
FFN0_END = MIX0_END + FFN_S
MIX1_END = FFN0_END + ADA_S * len(ADA_IN[1]) + MIX_S
SLOTS = MIX1_END + NE * FFN_S
CH = 512
NCH = FF // CH

COLS = {}
_at = 0
for _n, _w in (("g_mix", KD), ("g_ffn", KD), ("b_ada", ADA_T), ("s5_d", UT), ("conv_w", TAPS * QT), ("gdn_w", 1),
               ("lam_re", JT), ("lam_im", JT), ("log_dt", JT), ("a_log", NH), ("dt_bias", NH), ("g_final", KD),
               ("b_router", NE)):
    COLS[_n] = (_at, _w)
    _at += _w
NCOL = _at
MASKS = ["ident", "upper", "strict", "blk", "blkT", "lev0", "lev1", "lev2"]
BASE = 16


def trunk_program(nc, x_in, c_in, cols_in, masks_in, iota_in, sel_in, bpk_in, cpk_in, s5s_in, gdn_in, conv_in,
                  wab_in, wr_in, w_in, y_out, s5_out, gdnp_out, gdns_out, conv_out):
    with ExitStack() as ctx:
        def sb(name, shape, dt=F32):
            return ctx.enter_context(nc.sbuf_tensor(name, shape, dt))

        sems = {}

        def sem(name):
            if name not in sems:
                sems[name] = ctx.enter_context(nc.semaphore(name))
            return sems[name]

        xT = sb("xT", [P, KD, N])
        hT = sb("hT", [P, KD, N])
        slab = sb("slab", [P, QT * (3 + N) + QT * N])
        raw = slab[:, 0:QT * (3 + N)].rearrange("p (a b) -> p a b", b=3 + N)
        cv = slab[:, QT * (3 + N):].rearrange("p (a b) -> p a b", b=N)
        arena = sb("arena", [P, 2 * FT * N])
        ring = sb("ring", [P, RING, SLOT * P])
        bpk = sb("bpk", [P, UT, 2, P])
        cpk = sb("cpk", [P, JT, 2, 32])
        ckk = sb("ckk", [P, JT, 2, 32])
        cols = sb("cols", [P, DEPTH, NCOL])
        masks = sb("masks", [P, len(MASKS), P])
        selw = sb("selw", [P, NE, NE])
        ones = sb("ones", [P, P])
        cT = sb("cT", [P, KD, 32])
        mods = sb("mods", [P, DEPTH, ADA_T, 1 + NB])
        whi = sb("whi", [P, SPL, SLOT * P], F32R)
        wlo = sb("wlo", [P, SPL, SLOT * P], F32R)
        s5s = sb("s5s", [P, DEPTH, JT, 2, NB])
        conv0 = sb("conv0", [P, DEPTH, QT, NB, 3])
        wab = sb("wab", [P, DEPTH, KD, 2 * NH])
        wr = sb("wr", [P, KD, NE])
        s5o = sb("s5o", [P, JT, 2, 1 + NB])
        cvo = sb("cvo", [P, QT, 1 + NB, 3])
        rstd = sb("rstd", [P, N])
        tmp = sb("tmp", [P, 2, N])
        ssb = tmp[:, 1, :]
        sm = sb("sm", [P, 19, JT])
        pw = sb("pw", [P, 7, JT])
        smi = sb("smi", [P, JT], I32)
        sx = sb("sx", [P, 4, JT * NB])
        gd = sb("gd", [P, 12, 3 * NH])
        dg = sb("dg", [NB, 2, NH, NB])
        rowb = sb("rowb", [P, 2, NH * NB])
        ktk = sb("ktk", [NH * NB, P])
        ini = sb("ini", [P, 4])
        rt = sb("rt", [P, 3, NE])
        rtx = sb("rtx", [P, 12, NE])
        cnt = sb("cnt", [1, 1], I32)
        bank = [ctx.enter_context(nc.psum_tensor(f"bank{b}", [P, 512], F32)) for b in range(8)]
        where = lambda t: nc.lookup_mls(t).memorylocations[0].addr
        arena_at, slab_at = where(arena), where(slab)

        def over(name, shape, base, at, dt=F32R):
            return nc.alloc_sbuf_tensor_at(name, shape, dt, offset=base + 4 * at)

        gates, adas = over("gates", [P, 2 * KD, N], where(whi), 0, F32), over("adas", [P, 512], where(whi), 2 * KD * N, F32)
        behind = 2 * KD * N + 512
        uT, zs = over("uT", [P, UT, N], where(whi), behind, F32), over("zs", [P, NH, N], where(whi), behind + UT * N, F32)

        ident, upper, strict, blk, blkT = (masks[:, i, :] for i in range(5))

        def ar(at, *shape):
            n = int(np.prod(shape))
            v = arena[:, at:at + n]
            if len(shape) == 2:
                return v.rearrange("p (a b) -> p a b", b=shape[1])
            if len(shape) == 3:
                return v.rearrange("p (a b c) -> p a b c", b=shape[1], c=shape[2])
            return v

        B1 = 1024
        cosT = ar(0, JT, HALF)
        sinT = ar(2 * B1, JT, 2, HALF)
        st = ar(6 * B1, 8, 2, SEQ)
        wrot = ar(10 * B1, 2, SEQ)
        rrot = [ar(10 * B1 + 512, 2, SEQ), ar(11 * B1, 2, SEQ)]
        prot = ar(11 * B1 + 512, 2, SEQ)
        sq = ar(6 * B1, KD, N)
        nrm = ar(0, KD, N)
        onrm = hT[:, 0:NH, :]
        mats = {}
        for i, names in enumerate(("decT vn", "dec y", "ln vb", "lnT", "att", "e", "eT", "p", "pT", "kbg nwT", "kg", "qg")):
            for n in names.split():
                mats[n] = [ar(i * B1 + c * 512, NH, P) for c in range(NC)]
        s_pr = ar(5 * B1, NH, P)
        s0 = ar(5 * B1, NH * NB, P)
        vm = ar(0, NH * NB, P)
        oT = raw[:, 0:NH, 3:3 + N]
        osq = hT[:, NH:2 * NH, :]
        hh, hl = over("hh", [P, KD, N], slab_at, 0), over("hl", [P, KD, N], slab_at, KD * N)
        ahi, alo = over("ahi", [P, FT, N], arena_at, 0), over("alo", [P, FT, N], arena_at, FT * N)
        sg = tmp
        htok = slab[:, 0:3 * D].rearrange("p (a b) -> p a b", b=D)
        acc = cv[:, 0:KD, :]
        gh, gl = over("gh", [P, KD, CAP], arena_at, 0), over("gl", [P, KD, CAP], arena_at, KD * CAP)
        eh, el = over("eh", [P, FT, CAP], arena_at, 2 * B1), over("el", [P, FT, CAP], arena_at, 2 * B1 + FT * CAP)
        at_e = 2 * B1 + 2 * FT * CAP
        erow = ar(at_e, 2, CH)
        srow = ar(at_e + 2 * CH, 2, CH)
        ye = ar(at_e + 4 * CH, D)
        dcT = ar(at_e + 4 * CH + D, N)
        dsel = ar(at_e + 4 * CH + D + N, 3, CAP)
        dw = ar(at_e + 4 * CH + D + N + 3 * CAP, 3, CAP)
        iota = ar(at_e + 4 * CH + D + N + 6 * CAP, PASSES * CAP)

        def col(l, name, i=0, w=None):
            at, width = COLS[name]
            return cols[:, l, at + i:at + i + (width - i if w is None else w)]

        full = [sem(f"full{b}") for b in range(8)]
        free = [sem(f"free{b}") for b in range(8)]
        group, order, reads = {}, [], [0] * 8
        ROT = 7

        def open_bank(pe, name, readers=1):
            b = len(order) % ROT
            if reads[b]:
                pe.wait_ge(free[b], reads[b])
            reads[b] += readers
            group[name] = (b, len(order) // ROT + 1, reads[b])
            order.append(name)
            return bank[b]

        def filled(eng, name):
            b, n, _ = group[name]
            eng.wait_ge(full[b], n)
            return bank[b]

        def gives(ins, name):
            ins.then_inc(free[group[name][0]], 1)

        def taken(eng, name):
            b, _, n = group[name]
            eng.wait_ge(free[b], n)

        landed = [sem(f"landed{r}") for r in range(RING)]
        used = sem("slots_used")

        class Stream:
            pos, blk, owed = 0, 0, False

        stream = Stream()

        def weights(pe):
            r = stream.pos % RING
            if stream.blk == 0:
                pe.wait_ge(landed[r], 16 * (stream.pos // RING + 1))
            b = stream.blk
            stream.blk += 1
            if stream.blk == SLOT:
                stream.pos, stream.blk = stream.pos + 1, 0
            return ring[:, r, b * P:(b + 1) * P]

        def mm(pe, out, rhs, start, stop):
            first = stream.blk == 0
            w = weights(pe)
            ins = pe.matmul(out, w, rhs, start=start, stop=stop)
            if first and stream.owed:
                ins.then_inc(used, 1)
            if first:
                stream.owed = True
            return ins

        count = {}

        def then(eng, ins, name):
            count[name] = count.get(name, 0) + 1
            ins.then_inc(sem(name), 1)
            eng.wait_ge(sem(name), count[name])

        def takes(eng, ins, name):
            gives(ins, name)
            b, _, n = group[name]
            eng.wait_ge(free[b], n)

        LOADS = ("x", "c", "cols", "masks", "iota", "sel", "s5s", "conv0", "wab", "wr")
        for b in range(8):
            sem(f"full{b}")
        ld = {n: sem(f"in_{n}") for n in LOADS}
        block = ctx.enter_context(nc.Block())

        TURN = 4
        ADAS = [(0, 0)] + ADA_IN[0] + ADA_IN[1]

        def silu_after(m):
            return [c for c in range(NCH) if m == KD * (c + 1) + SPL - 1]

        def turned_after(m):
            return [c for c in range(NCH) if m == KD * (c + 1) + TURN + SPL]

        UNITS = 3 * KD
        STEPS = 22
        Y_AFTER = [5, 8, 12]
        ended = []

        def units(step):
            return range(UNITS * step // STEPS, UNITS * (step + 1) // STEPS)

        def ada_ends(l):
            n = len(ADA_IN[l])
            return [-(-ADA_S * (i + 1) // n) - 1 for i in range(n)]

        def count_rms(tag):
            return {("mix", 0): 1, ("ffn", 0): 2, ("mix", 1): 3, ("ffn", 1): 4, ("end", 0): 5}[tag]

        @block.tensor
        def _(pe):
            def rms(tag):
                pe.wait_ge(sem("sq_done"), count_rms(tag))
                ps = open_bank(pe, ("rms",) + tag)
                for k in range(KD):
                    ins = pe.matmul(ps[:, 0:N], ones[:, :], sq[:, k, :], start=k == 0, stop=k == KD - 1)
                    if tag == ("ffn", 0) and k == 0:
                        ins.then_inc(sem("spl_used"), SPL - 1)
                ins.then_inc(full[group[("rms",) + tag][0]], 1)

            def close(ins, name):
                ins.then_inc(full[group[name][0]], 1)

            def project(name, rhs, kt, readers=1):
                ps = open_bank(pe, name, readers)
                for k in range(kt):
                    ins = mm(pe, ps[:, 0:N], rhs(k), k == 0, k == kt - 1)
                close(ins, name)

            def tok_logits(name, w):
                ps = open_bank(pe, name)
                for g in range(3):
                    m = P if g < 2 else NB
                    for k in range(KD):
                        ins = pe.matmul(ps[0:m, 8 * g:8 * g + 8], hT[:, k, P * g:P * g + m], w[:, k, :],
                                        start=k == 0, stop=k == KD - 1)
                close(ins, name)

            def bu(l, j):
                ps = open_bank(pe, ("bu", l, j))
                a = 32 * (j % 4)
                for c in range(2):
                    ins = pe.matmul(ps[:, c * SEQ:(c + 1) * SEQ], bpk[a:a + 32, j // 4, c, :],
                                    uT[a:a + 32, j // 4, 0:SEQ], start=True, stop=True)
                close(ins, ("bu", l, j))

            def batch4(name, fn, readers=1):
                ps = open_bank(pe, name, readers)
                for h in range(NH):
                    ins = fn(ps[:, h * P:(h + 1) * P], h)
                close(ins, name)

            def one(a, b):
                return lambda o, h: pe.matmul(o, a(h), b(h), start=True, stop=True)

            rounds = {"n": 0, "slots": 0}

            def ada_slots(todo, n):
                for _ in range(n):
                    at = rounds["slots"] % ADA_S
                    if at == 0 and rounds["n"]:
                        pe.wait_ge(sem("ada_copied"), rounds["n"])
                    first = True
                    for jj in range(2):
                        j = 2 * (at % 2) + jj
                        w = [weights(pe) for _ in range(4)][0]
                        i = (stream.pos if stream.blk else stream.pos - 1) % RING
                        ins = pe.matmul(bank[7][32 * j:32 * j + 32, :], cT[:, at // 2, :],
                                        ring[:, i, 512 * jj:512 * jj + 512], start=at // 2 == 0, stop=at // 2 == KD - 1,
                                        tile_position=(0, 32 * j))
                        if first and stream.owed:
                            ins.then_inc(used, 1)
                        first, stream.owed = False, True
                    rounds["slots"] += 1
                    if at == ADA_S - 1:
                        ins.then_inc(sem("ada_full"), 1)
                        rounds["n"] += 1

            def ada_turn(l, rd):
                pe.wait_ge(sem("ada_copied"), rounds["n"])
                name = ("adt", l, rd)
                ps = open_bank(pe, name)
                for t in range(4):
                    ins = pe.transpose(ps[:, t * P:(t + 1) * P], adas[:, t * P:(t + 1) * P], ident)
                close(ins, name)

            def mixer(l):
                if l == 0:
                    pe.wait_ge(sem("cs_done"), 1)
                    ada_slots([(0, 0)], ADA_S)
                    ada_turn(0, 0)
                rms(("mix", l))
                if l == 0:
                    pe.wait_ge(ld["wab"], 16)
                pe.wait_ge(sem("h_act"), KD * (2 * l + 1))
                pe.wait_ge(sem("h_smp"), 2 * l + 1)
                tok_logits(("ab", l), wab[:, l])
                for m in range(UT):
                    project(("in", l, m), lambda k: hT[:, k, :], KD)
                pe.wait_ge(sem("b_in"), 16 * (l + 1))
                for m in range(UT):
                    taken(pe, ("in", l, m))
                ps = open_bank(pe, ("bus", l))
                for a in range(4):
                    if a:
                        pe.wait_ge(sem("bus_rows"), 3 * l + a)
                    for j in range(a, JT, 4):
                        for c in range(2):
                            o = NB * (2 * j + c)
                            ins = pe.matmul(ps[:, o:o + NB], bpk[32 * a:32 * a + 32, j // 4, c, :],
                                            uT[32 * a:32 * a + 32, j // 4, SEQ:N], start=True, stop=True)
                    if a < 3:
                        ins.then_inc(sem("bus_rows"), 1)
                close(ins, ("bus", l))
                todo = ADA_IN[l]
                for j in range(S5_STEPS):
                    project(("in", l, UT + j), lambda k: hT[:, k, :], KD)
                    bu(l, j)
                    ada_slots(todo, len(todo))
                    if j in ada_ends(l):
                        ended.append(todo[ada_ends(l).index(j)])
                    elif ended:
                        ada_turn(*ended.pop())
                    if j in Y_AFTER:
                        s5_y(l, Y_AFTER.index(j))
                ada_turn(*ended.pop())
                s5_y(l, UT - 1)
                def unit(u):
                    if u < 2 * KD:
                        project(("in", l, UT + S5_STEPS + u), lambda k: hT[:, k, :], KD)
                    else:
                        m = u - 2 * KD
                        if m == 0:
                            pe.wait_ge(sem("gelu_done"), UT * (l + 1))
                        for half in range(2):
                            project(("glu", l, 2 * m + half), lambda k: uT[:, k, :], UT)

                def fill(step):
                    for u in units(step):
                        unit(u)

                fill(0)
                pe.wait_ge(sem("qk_sq"), l + 1)
                for i in range(2 * NH):
                    ps = open_bank(pe, ("qkn", l, i))
                    close(pe.matmul(ps[:, 0:N], ones[:, :], sq[:, i, :], start=True, stop=True), ("qkn", l, i))
                fill(1)
                gdn(l, fill)
                gdn_samples(l, fill)
                pe.wait_ge(sem("o_sq"), l + 1)
                for h in range(NH):
                    ps = open_bank(pe, ("on", l, h))
                    close(pe.matmul(ps[:, 0:N], ones[:, :], osq[:, h, :], start=True, stop=True), ("on", l, h))
                pe.wait_ge(sem("o_done"), l + 1)
                for m in range(KD):
                    project(("go", l, m), lambda k: oT[:, k, :], NH)
                for m in range(KD):
                    pe.wait_ge(sem("merged"), KD * l + m + 1)
                for m in range(KD):
                    project(("wo", l, m), lambda k: hT[:, k, :], KD)
                stream.owed = False

            def s5_y(l, i):
                pe.wait_ge(sem("s_back"), JT * l + 4 * i + 4)
                pe.wait_ge(sem("s_smp"), l + 1)
                ps = open_bank(pe, ("y", l, i))
                for jj in range(4):
                    j = 4 * i + jj
                    o = ps[32 * jj:32 * jj + 32, :]
                    for c in range(2):
                        pe.matmul(o[:, 0:SEQ], ckk[:, j, c, :], st[:, j % 8, c, :], start=c == 0, stop=c == 1)
                    for c in range(2):
                        ins = pe.matmul(o[:, SEQ:N], cpk[:, j, c, :], s5s[:, l, j, c, :], start=c == 0, stop=c == 1)
                close(ins, ("y", l, i))

            def gdn(l, fill):
                def q(c):
                    return lambda h: cv[:, h, P * c:P * c + P]

                def k(c):
                    return lambda h: cv[:, NH + h, P * c:P * c + P]

                pe.wait_ge(sem("g_done"), l + 1)
                name = ("gcc", l)
                ps = open_bank(pe, name)
                close(pe.matmul(ps[:, 0:8], upper, gd[:, 0, 0:8], start=True, stop=True), name)
                for c in range(NC):
                    batch4(("gcb", l, c), one(lambda h: gd[:, 0, 4 * c + h:4 * c + h + 1].broadcast_to([P, P]),
                                              lambda h: upper))
                fill(2)
                pe.wait_ge(sem("qk_done"), l + 1)
                for c in range(NC):
                    batch4(("ktok", l, c), lambda o, h: pe.transpose(o, k(c)(h), ident))
                for c in range(NC):
                    batch4(("kk", l, c), one(k(c), k(c)))
                    batch4(("qk", l, c), one(k(c), q(c)))
                fill(3)
                for c in range(NC):
                    pe.wait_ge(sem("ln_done"), NC * l + c + 1)
                    batch4(("lt", l, c), lambda o, h: pe.transpose(o, mats["ln"][c][:, h, :], ident))
                    batch4(("vtok", l, c), lambda o, h: pe.transpose(o, cv[:, 2 * NH + h, P * c:P * c + P], ident))
                at = lambda n, c: (lambda h: mats[n][c][:, h, :])
                fill(4)
                for s in range(3):
                    for c in range(NC):
                        if s == 0:
                            pe.wait_ge(sem("e_done"), NC * l + c + 1)
                        else:
                            taken(pe, ("e", l, s - 1, c))
                            taken(pe, ("eT", l, s - 1, c))
                        batch4(("e", l, s, c), one(at("eT", c), at("e", c)))
                        batch4(("eT", l, s, c), one(at("e", c), at("eT", c)))
                    fill(5 + 2 * s)
                    for c in range(NC):
                        taken(pe, ("e", l, s, c))
                        taken(pe, ("eT", l, s, c))
                        if s:
                            taken(pe, ("pT", l, s - 1, c))
                        batch4(("p", l, s, c), one(at("eT", c), at("p", c)))
                        batch4(("pT", l, s, c), one(at("e", c), at("pT", c)))
                    fill(6 + 2 * s)
                for s in range(3):
                    for c in range(NC):
                        taken(pe, ("pT", l, 2, c) if s == 0 else ("xT", l, s - 1, c))
                        pe.wait_ge(sem("lev_done"), NC * (3 * l + s) + c + 1)
                        batch4(("yl", l, s, c), one(at("eT", c), at("p", c)))
                    fill(11 + 2 * s)
                    for c in range(NC):
                        taken(pe, ("yl", l, s, c))
                        if s < 2:
                            batch4(("x", l, s, c), one(at("pT", c), at("y", c)))
                        batch4(("xT", l, s, c), one(at("y", c), at("pT", c)))
                    fill(12 + 2 * s)
                for c in range(NC):
                    taken(pe, ("xT", l, 2, c))
                    taken(pe, ("ktok", l, c))
                    batch4(("wt", l, c), one(at("kbg", c), at("pT", c)))
                fill(17)
                for c in range(NC):
                    taken(pe, ("vtok", l, c))
                    if c:
                        taken(pe, ("wt", l, c))
                        taken(pe, ("s", l, c - 1))
                    name = ("vn", l, c)
                    ps = open_bank(pe, name)
                    for h in range(NH):
                        o = ps[:, h * P:(h + 1) * P]
                        ins = pe.matmul(o, mats["pT"][c][:, h, :], mats["vb"][c][:, h, :], start=True, stop=c == 0)
                        if c:
                            ins = pe.matmul(o, mats["nwT"][c][:, h, :], s_pr[:, h, :], start=False, stop=True)
                    close(ins, name)
                    fill(18 + c)
                    taken(pe, name)
                    taken(pe, ("qk", l, c))
                    pe.wait_ge(sem("qg_done"), NC * l + c + 1)
                    name = ("o", l, c)
                    ps = open_bank(pe, name)
                    for h in range(NH):
                        o = ps[:, h * P:(h + 1) * P]
                        ins = pe.matmul(o, mats["vn"][c][:, h, :], mats["att"][c][:, h, :], start=True, stop=c == 0)
                        if c:
                            ins = pe.matmul(o, s_pr[:, h, :], mats["qg"][c][:, h, :], start=False, stop=True)
                    close(ins, name)
                    batch4(("s", l, c), one(at("kg", c), at("vn", c)))

            def gdn_samples(l, fill):
                hb = NH * NB
                pe.wait_ge(sem("qkp_done"), l + 1)
                name = ("skt", l)
                ps = open_bank(pe, name)
                close(pe.transpose(ps[0:hb, 0:P], sx[:, 2, 0:hb], ident), name)
                pe.wait_ge(sem("dg_done"), l + 1)
                name = ("sgb", l)
                ps = open_bank(pe, name)
                close(pe.matmul(ps[:, 0:2 * hb], ones[0:NB, :], dg[:, :, :, :].rearrange("p a h b -> p (a h b)"),
                                start=True, stop=True), name)
                name = ("sqk", l)
                ps = open_bank(pe, name)
                close(pe.matmul(ps[:, 0:hb], ones[:, :], sx[:, 0, 0:hb], start=True, stop=True), name)
                fill(20)
                pe.wait_ge(sem("s0_in"), 16 * (l + 1))
                name = ("skq", l)
                ps = open_bank(pe, name)
                for h in range(NH):
                    for b in range(NB):
                        i = h * NB + b
                        ins = pe.matmul(ps[:, 2 * i:2 * i + 2], s0[:, i, :], cv[:, h:h + NH + 1:NH, SEQ + b],
                                        start=True, stop=True)
                close(ins, name)
                fill(21)
                pe.wait_ge(sem("svn_done"), l + 1)
                name = ("svt", l)
                ps = open_bank(pe, name)
                close(pe.transpose(ps[0:hb, 0:P], sx[:, 1, 0:hb], ident), name)
                pe.wait_ge(sem("vm_done"), l + 1)
                for i in range(NB):
                    name = ("so", l, i)
                    ps = open_bank(pe, name)
                    close(pe.matmul(ps[:, :], ktk[:, :], vm[0:hb, 4 * i:4 * i + 4, :].rearrange("p a b -> p (a b)"),
                                    start=True, stop=True), name)

            def drained():
                for b in range(8):
                    if reads[b]:
                        pe.wait_ge(free[b], reads[b])

            def product3(o, k, wh, wl, xh, xl, first, last, turned):
                for n, (a, b) in enumerate(((xh, wh), (xh, wl), (xl, wh))):
                    lhs, rhs = (a, b) if turned else (b, a)
                    ins = pe.matmul(o, lhs, rhs, start=first and n == 0, stop=last and n == 2)
                    yield ins

            def dense():
                drained()
                pe.wait_ge(sem("hl_done"), 1)
                BODY = 4 * RING
                with pe.Fori(0, UP_S // BODY) as it:
                    for s in range(BODY):
                        f, half = s // 2, s % 2
                        pe.wait_ge(sem("lo_done"), it * BODY + (s + 1))
                        if half == 0:
                            pe.wait_ge(sem("act_done"), it * (BODY // 2) + f if f >= 2 else it * (BODY // 2 - 1 + f) + 1)
                        for k in range(KD):
                            w = [t[:, s % SPL, k * P:(k + 1) * P] for t in (whi, wlo)]
                            for ins in product3(bank[2 * (f % 2) + half][:, 0:N], k, *w, hh[:, k, :], hl[:, k, :],
                                                k == 0, k == KD - 1, False):
                                if k == 0 and not ins_done:
                                    ins.then_inc(sem("spl_used"), 1)
                                    ins_done.append(1)
                        ins_done.clear()
                        if half:
                            ins.then_inc(sem("up_full"), 1)
                for m in range(KD):
                    if m >= 2:
                        pe.wait_ge(sem("down_taken"), m - 1)
                    for k in range(FT):
                        b = m * FT + k
                        s, i = UP_S + b // SLOT, b % SLOT
                        if i == 0:
                            pe.wait_ge(sem("lo_done"), s + 1)
                        if m == 0 and k % 2 == 0:
                            pe.wait_ge(sem("al_done"), k + 2)
                        w = [t[:, s % SPL, i * P:(i + 1) * P] for t in (whi, wlo)]
                        for ins in product3(bank[4 + m % 2][:, 0:N], k, *w, ahi[:, k, :], alo[:, k, :],
                                            k == 0, k == FT - 1, False):
                            if i == 0 and not ins_done:
                                ins.then_inc(sem("spl_used"), 1)
                                ins_done.append(1)
                        ins_done.clear()
                    ins.then_inc(sem("down_full"), 1)
                pe.wait_ge(sem("down_taken"), KD)
                stream.pos += FFN_S

            def experts_setup():
                pe.wait_ge(ld["wr"], 16)
                pe.wait_ge(sem("h_act"), 4 * KD)
                pe.wait_ge(sem("h_smp"), 4)
                tok_logits(("rl",), wr)
                for g in range(3):
                    m = P if g < 2 else NB
                    for half in range(2):
                        name = ("ht", g, half)
                        ps = open_bank(pe, name)
                        for k in range(4):
                            ins = pe.transpose(ps[0:m, k * P:(k + 1) * P], hT[:, 4 * half + k, P * g:P * g + m], ident)
                        close(ins, name)
                pe.wait_ge(sem("sel_done"), 1)
                ps = open_bank(pe, ("rank",))
                for g in range(4):
                    m = P if g != 2 else NB
                    o = ps[0:m, 8 * g:8 * g + 8]
                    for a in range(min(g, 3)):
                        ka = P if a < 2 else NB
                        ins = pe.matmul(o, ones[0:ka, 0:m], rt[0:ka, a, :], start=a == 0, stop=g == 3 and a == 2)
                    if g < 3:
                        ins = pe.matmul(o, upper[0:m, 0:m], rt[0:m, g, :], start=g == 0, stop=True)
                close(ins, ("rank",))
                drained()

            def expert(q):
                base = FFN_S
                pe.wait_ge(sem("dsel_done"), q * 1 + 1)
                for m in range(KD):
                    for g in range(3):
                        kk = P if g < 2 else NB
                        ins = pe.matmul(bank[m // 4][:, CAP * (m % 4):CAP * (m % 4) + CAP],
                                        htok[0:kk, g, m * P:(m + 1) * P], dsel[0:kk, g, :], start=g == 0, stop=g == 2)
                    if m % 4 == 3:
                        ins.then_inc(sem("gather_full"), 1)
                for g in range(3):
                    m = P if g < 2 else NB
                    ins = pe.transpose(bank[4][0:CAP, P * g:P * g + m], dw[0:m, g, :], ident[0:m, 0:m])
                ins.then_inc(sem("dcT_full"), 1)
                pe.wait_ge(sem("gl_done"), q * 2 + 2)

                def turn(c):
                    pe.wait_ge(sem("act_done"), q * NCH + (FT + 1 + c + 1))
                    if c == 0:
                        pe.wait_ge(sem("dcT_done"), q * 1 + 1)
                    if c >= 2:
                        pe.wait_ge(sem("turned_done"), q * NCH + (c - 1))
                    for t in range(CH // P):
                        ins = pe.transpose(bank[4 + c % 2][:, CAP * t:CAP * t + CAP], erow[0:CAP, c % 2, t * P:(t + 1) * P],
                                           ident[0:CAP, 0:CAP])
                    ins.then_inc(sem("turned_full"), 1)

                for s in range(UP_S):
                    c, k = s // KD, s % KD
                    pe.wait_ge(sem("lo_done"), q * FFN_S + (base + s + 1))
                    if k == 0 and c >= 2:
                        pe.wait_ge(sem("act_done"), q * NCH + (FT + 1 + c - 1))
                    w = [t[:, s % SPL, :] for t in (whi, wlo)]
                    o = [bank[2 * (c % 2) + half][0:CAP, :] for half in range(2)]
                    for n, (x, part) in enumerate(((gh, 0), (gh, 1), (gl, 0))):
                        for half in range(2):
                            ins = pe.matmul(o[half], x[:, k, :], w[part][:, CH * half:CH * half + CH],
                                            start=k == 0 and n == 0, stop=k == KD - 1 and n == 2)
                            if n == 0 and half == 0:
                                ins.then_inc(sem("spl_used"), 1)
                    if k == KD - 1:
                        ins.then_inc(sem("up_full"), 1)
                    if k == TURN and c:
                        turn(c - 1)
                for s in range(DOWN_S):
                    m = UP_S + s
                    pe.wait_ge(sem("lo_done"), q * FFN_S + (base + m + 1))
                    if s % (CH // P) == 0:
                        pe.wait_ge(sem("turned_done"), q * NCH + (s // (CH // P) + 1))
                    w = [t[:, m % SPL, :] for t in (whi, wlo)]
                    for n, (x, part) in enumerate(((eh, 0), (eh, 1), (el, 0))):
                        for half in range(2):
                            ins = pe.matmul(bank[6 + half][0:CAP, :], x[:, s, :], w[part][:, CH * half:CH * half + CH],
                                            start=s == 0 and n == 0, stop=s == FT - 1 and n == 2)
                            if n == 0 and half == 0:
                                ins.then_inc(sem("spl_used"), 1)
                            if s == FT - 1 and n == 2:
                                ins.then_inc(sem("ye_full"), 1)
                    if s == TURN:
                        turn(NCH - 1)
                pe.wait_ge(sem("ye_done"), q * 2 + 2)
                for m in range(KD):
                    pe.wait_ge(sem("down_taken"), q * KD + (KD + m - 1))
                    pe.matmul(bank[4 + m % 2][:, 0:N], ye[0:CAP, m * P:(m + 1) * P], dcT[0:CAP, :],
                              start=True, stop=True).then_inc(sem("down_full"), 1)
                pe.wait_ge(sem("down_taken"), q * KD + 2 * KD)

            ins_done = []
            pe.wait_ge(ld["masks"], 16)
            pe.wait_ge(sem("ones_done"), 1)
            mixer(0)
            rms(("ffn", 0))
            dense()
            mixer(1)
            rms(("ffn", 1))
            experts_setup()
            with pe.Fori(0, NE) as e:
                expert(e)
            pe.wait_ge(sem("cnt_done"), 1)
            most = pe.value_load(cnt[0:1, 0:1])
            with pe.If(most > CAP):
                with pe.Fori(NE, PASSES * NE) as q:
                    expert(q)
            pe.wait_ge(sem("sq_done"), count_rms(("end", 0)))
            for k in range(KD):
                ins = pe.matmul(bank[0][:, 0:N], ones[:, :], sq[:, k, :], start=k == 0, stop=k == KD - 1)
            ins.then_inc(sem("end_full"), 1)


        @block.sync
        def _(sp):
            def segment(n0, n1, before, gone, each, turns=0, e=None, q=None):
                def load(n, at=None):
                    sp.dma_start(ring[:, n % RING, :], w_in[n if at is None else at]).then_inc(landed[n % RING], 16)

                for n in range(n0, n0 + RING):
                    before(n - RING)
                    load(n)
                whole = (n1 - n0 - RING) // RING
                with sp.Fori(0, whole) as i:
                    for r in range(RING):
                        sp.wait_ge(sem(gone), i * RING + (each + r + 1))
                        load(n0 + RING + r, i * RING + (n0 + RING + r))
                for n in range(n0 + RING * (whole + 1), n1):
                    sp.wait_ge(sem(gone), each + n - n0 - RING + 1)
                    load(n)

            def mixer_slot(l, n0, n1):
                def wait(n):
                    if n == n1 - 1:
                        filled(sp, ("wo", l, KD - 1))
                    else:
                        sp.wait_ge(used, (MIX0_END - 1) * l + n - n0 + 1)
                return wait

            segment(0, MIX0_END, lambda n: None, "slots_used", 0)
            segment(MIX0_END, FFN0_END, mixer_slot(0, 0, MIX0_END), "lo_done", 0)
            segment(FFN0_END, MIX1_END, lambda n: sp.wait_ge(sem("lo_done"), n - MIX0_END + 1), "slots_used", MIX0_END - 1)
            m1 = mixer_slot(1, FFN0_END, MIX1_END)
            for n in range(MIX1_END, MIX1_END + RING):
                m1(n - RING)
                sp.dma_start(ring[:, n % RING, :], w_in[n]).then_inc(landed[n % RING], 16)

            def expert_weights(q, e, s0, s1):
                for s in range(s0, s1):
                    sp.wait_ge(sem("lo_done"), q * FFN_S + (FFN_S + s - RING + 1))
                    r = (MIX1_END + s) % RING
                    sp.dma_start(ring[:, r, :], w_in[e * FFN_S + (MIX1_END + s)]).then_inc(landed[r], 16)

            expert_weights(0, 0, RING, FFN_S)
            with sp.Fori(1, NE) as e:
                expert_weights(e, e, 0, FFN_S)
            sp.wait_ge(sem("cnt_done"), 1)
            most = sp.value_load(cnt[0:1, 0:1])
            with sp.If(most > CAP):
                with sp.Fori(1, PASSES) as a:
                    with sp.Fori(0, NE) as e:
                        expert_weights(a * NE + e, e, 0, FFN_S)
            sp.wait_ge(sem("y_done"), KD)
            sp.dma_start(y_out, hT[:, :, :]).then_inc(sem("y_out"), 16)
            sp.wait_ge(sem("y_out"), 16)

        @block.scalar
        def _(act):
            act.wait_ge(sem("c_zero"), 1)
            act.dma_start(cT[:, :, 0:1 + NB], c_in).then_inc(ld["c"], 16)
            act.dma_start(xT[:, :, :], x_in).then_inc(ld["x"], 16)
            act.dma_start(cols[:, :, :], cols_in).then_inc(ld["cols"], 16)
            act.dma_start(masks[:, :, :], masks_in).then_inc(ld["masks"], 16)
            act.dma_start(wab[:, :, :, :], wab_in).then_inc(ld["wab"], 16)
            act.dma_start(bpk[:, :, :, :], bpk_in[0]).then_inc(sem("b_in"), 16)
            act.dma_start(cpk[:, :, :, :], cpk_in[0]).then_inc(sem("c5_in"), 16)
            act.dma_start(s5s[:, :, :, :, :], s5s_in).then_inc(ld["s5s"], 16)
            act.dma_start(conv0[:, :, :, :, :], conv_in).then_inc(ld["conv0"], 16)
            act.dma_start(selw[:, :, :], sel_in).then_inc(ld["sel"], 16)
            act.dma_start(wr[:, :, :], wr_in).then_inc(ld["wr"], 16)
            act.wait_ge(ld["c"], 16)
            act.activation(cT[:, :, :], cT[:, :, :], ACT.Silu).then_inc(sem("cs_done"), 1)
            act.wait_ge(ld["x"], 16)

            def rms(tag, wait=None):
                if wait:
                    act.wait_ge(sem(wait[0]), wait[1])
                if tag[0] == "ffn":
                    act.wait_ge(sem("gs_out"), 16 * (tag[1] + 1))
                act.activation(sq, xT[:, :, :], ACT.Square).then_inc(sem("sq_done"), 1)

            def root(n):
                act.wait_ge(sem("ss_done"), n)
                act.activation(rstd[:, :], ssb[:, :], ACT.Sqrt).then_inc(sem("root_done"), 1)

            def shift(l, at, n):
                for k in range(KD):
                    act.wait_ge(sem("h_scaled"), KD * n + k + 1)
                    act.activation(hT[:, k, 0:SEQ], hT[:, k, 0:SEQ], ACT.Identity,
                                   bias=mods[:, l, at + k, 0:1]).then_inc(sem("h_act"), 1)

            def ada_copy(n):
                act.wait_ge(sem("ada_full"), n)
                if n > 1:
                    filled(act, ("adt",) + ADAS[n - 2])
                act.activation(adas[:, :], bank[7][:, :], ACT.Copy).then_inc(sem("ada_copied"), 1)

            def unit(l, u):
                if u < 2 * KD:
                    name = ("in", l, UT + S5_STEPS + u)
                    gives(act.activation(gates[:, u, :], filled(act, name)[:, 0:N], ACT.Sigmoid), name)
                else:
                    m = u - 2 * KD
                    name = ("glu", l, 2 * m + 1)
                    ps = filled(act, name)
                    if m >= 2:
                        act.wait_ge(sem("glu_done"), KD * l + m - 1)
                    gives(act.activation(tmp[:, m % 2, :], ps[:, 0:N], ACT.Sigmoid), name)

            def mixer(l):
                def fill(step):
                    for u in units(step):
                        unit(l, u)

                rms(("mix", l), ("x_ffn", KD) if l else None)
                if l == 0:
                    ada_copy(1)
                root(2 * l + 1)
                shift(l, 0, 2 * l)
                for m in range(UT + S5_STEPS):
                    name = ("in", l, m)
                    ps = filled(act, name)[:, 0:N]
                    if m < UT:
                        ins = act.activation(uT[:, m, :], ps, ACT.Copy)
                    elif m < UT + QT:
                        if m == UT:
                            act.wait_ge(sem("pool_zero"), l + 1)
                        ins = act.activation(raw[:, m - UT, 3:3 + N], ps, ACT.Copy)
                    else:
                        ins = act.activation(zs[:, m - UT - QT, :], ps, ACT.Silu)
                    gives(ins, name)
                    if m >= UT and m - UT in ada_ends(l):
                        ada_copy(ADAS.index(ADA_IN[l][ada_ends(l).index(m - UT)]) + 1)
                for i in range(3):
                    act.wait_ge(sem("conv_done"), l + 1)
                    v = cv[:, NH * i:NH * i + NH, :]
                    then(act, act.activation(v, v, ACT.Silu), "cv_silu")
                for i in range(UT):
                    act.wait_ge(sem("y_sum"), UT * l + i + 1)
                    act.activation(uT[:, i, :], uT[:, i, :], ACT.Gelu_apprx_tanh).then_inc(sem("gelu_done"), 1)
                act.activation(sq, cv[:, 0:2 * NH, :], ACT.Square).then_inc(sem("qk_sq"), 1)
                fill(0)
                act.wait_ge(sem("ax_done"), l + 1)
                then(act, act.activation(gd[:, 1, :], gd[:, 1, :], ACT.Exp, scale=-1.0), "a_gd")
                act.activation(gd[:, 1, :], gd[:, 1, :], ACT.Ln, bias=1.0).then_inc(sem("a_ln"), 1)
                act.activation(gd[:, 3, 0:NH], col(l, "a_log"), ACT.Exp).then_inc(sem("a_ln"), 1)
                act.activation(gd[:, 4, :], gd[:, 4, :], ACT.Sigmoid).then_inc(sem("a_ln"), 1)
                fill(1)
                act.wait_ge(sem("nrm_ss"), l + 1)
                act.activation(nrm[:, :, :], nrm[:, :, :], ACT.Sqrt).then_inc(sem("nrm_root"), 1)
                fill(2)
                act.wait_ge(sem("gdx_done"), l + 1)
                act.activation(gd[:, 7:10, 0:8], gd[:, 7:10, 0:8], ACT.Exp).then_inc(sem("a_col"), 1)
                act.activation(gd[:, 11, 8:12], gd[:, 0, 8:12], ACT.Exp).then_inc(sem("a_col"), 1)
                for c in range(NC):
                    name = ("gcb", l, c)
                    act.wait_ge(sem("diff_done"), NC * l + c + 1)
                    act.activation(mats["decT"][c], mats["decT"][c], ACT.Exp).then_inc(sem("a_dec"), 1)
                    act.activation(mats["dec"][c], mats["dec"][c], ACT.Exp).then_inc(sem("a_dec"), 1)
                    ps = filled(act, name)
                    gives(act.activation(mats["qg"][c], ps[:, :].rearrange("p (h t) -> p h t", h=NH), ACT.Exp), name)
                fill(3)
                fill(4)
                for s in range(3):
                    if s:
                        fill(4 + 2 * s)
                    for c in range(NC):
                        for n in ("e", "eT"):
                            name = (n, l, s, c)
                            filled(act, ("eT", l, s, c))
                            ps = filled(act, name)
                            gives(act.activation(mats[n][c], ps[:, :].rearrange("p (h t) -> p h t", h=NH), ACT.Copy), name)
                    fill(5 + 2 * s)
                for s in range(3):
                    fill(10 + 2 * s)
                    for c in range(NC):
                        name = ("yl", l, s, c)
                        ps = filled(act, name)
                        gives(act.activation(mats["y"][c], ps[:, :].rearrange("p (h t) -> p h t", h=NH), ACT.Copy), name)
                    fill(11 + 2 * s)
                fill(16)
                for c in range(NC):
                    name = ("wt", l, c)
                    ps = filled(act, name)
                    gives(act.activation(mats["nwT"][c], ps[:, :].rearrange("p (h t) -> p h t", h=NH), ACT.Copy,
                                         scale=-1.0), name)
                fill(17)
                for c in range(NC):
                    name = ("vn", l, c)
                    ps = filled(act, name)
                    gives(act.activation(mats["vn"][c], ps[:, :].rearrange("p (h t) -> p h t", h=NH), ACT.Copy), name)
                    fill(18 + c)
                    name = ("o", l, c)
                    ps = filled(act, name)
                    gives(act.activation(oT[:, :, P * c:P * c + P], ps[:, :].rearrange("p (h t) -> p h t", h=NH),
                                         ACT.Copy), name)
                act.wait_ge(sem("sp_out"), 16 * (l + 1))
                filled(act, ("s", l, NC - 1))
                act.dma_start(s0, gdn_in[l]).then_inc(sem("s0_in"), 16)
                fill(20)
                fill(21)
                act.wait_ge(sem("os_done"), l + 1)
                taken(act, ("o", l, NC - 1))
                act.activation(osq, oT, ACT.Square).then_inc(sem("o_sq"), 1)
                act.wait_ge(sem("on_ss"), l + 1)
                act.activation(onrm, onrm, ACT.Sqrt).then_inc(sem("on_root"), 1)

            mixer(0)
            rms(("ffn", 0), ("x_mix", KD))
            root(2)
            shift(0, 24, 1)
            act.wait_ge(sem("h_smp"), 2)
            act.wait_ge(sem("h_act"), 2 * KD)
            act.activation(hh[:, :, :], hT[:, :, :], ACT.Copy).then_inc(sem("hh_done"), 1)

            def high(r, land, m, count):
                act.wait_ge(landed[r], land)
                act.wait_ge(sem("spl_used"), count)
                act.activation(whi[:, m % SPL, :], ring[:, r, :], ACT.Copy).then_inc(sem("hi_done"), 1)

            BODY = 4 * RING

            def dense_tile(it, f):
                act.wait_ge(sem("up_full"), it * (BODY // 2) + (f + 1))
                act.wait_ge(sem("act_done"), it * (BODY // 2) + (f + 1))
                act.activation(sg[:, f % 2, :], bank[2 * (f % 2)][:, 0:N], ACT.Silu).then_inc(sem("silu_done"), 1)
                act.wait_ge(sem("act_done"), it * (BODY // 2) + (f + 2))
                act.activation(ahi[:, bass.ds(it * (BODY // 2) + f, 1), :], sg[:, f % 2:f % 2 + 1, :],
                               ACT.Copy).then_inc(sem("ah_done"), 1)

            with act.Fori(0, UP_S // BODY) as it:
                for s in range(BODY):
                    high((MIX0_END + s) % RING, it * (16 * BODY // RING) + 16 * ((MIX0_END + s) // RING + 1), s,
                         it * BODY + (s + 1))
                    if s >= 5 and s % 2 == 1:
                        dense_tile(it, (s - 5) // 2)
                dense_tile(it, BODY // 2 - 2)
                dense_tile(it, BODY // 2 - 1)
            for s in range(UP_S, FFN_S):
                n = MIX0_END + s
                high(n % RING, 16 * (n // RING + 1), s, s + 1)
            filled(act, ("y", 0, UT - 1))
            act.dma_start(bpk[:, :, :, :], bpk_in[1]).then_inc(sem("b_in"), 16)
            act.dma_start(cpk[:, :, :, :], cpk_in[1]).then_inc(sem("c5_in"), 16)
            mixer(1)
            rms(("ffn", 1), ("x_mix", 2 * KD))
            act.dma_start(iota, iota_in).then_inc(ld["iota"], 16)
            root(4)
            shift(1, 24, 3)
            for g in range(3):
                m = P if g < 2 else NB
                for half in range(2):
                    name = ("ht", g, half)
                    ps = filled(act, name)
                    gives(act.activation(htok[0:m, g, 512 * half:512 * half + 512], ps[0:m, :], ACT.Copy), name)
            act.wait_ge(sem("sel_done"), 1)
            act.activation(rtx[:, 6:9, :], rtx[:, 6:9, :], ACT.Exp).then_inc(sem("rexp_done"), 1)

            def expert(q):
                for half in range(2):
                    act.wait_ge(sem("gather_full"), q * 2 + (half + 1))
                    act.activation(gh[:, 4 * half:4 * half + 4, :],
                                   bank[half][:, 0:4 * CAP].rearrange("p (a b) -> p a b", b=CAP),
                                   ACT.Copy).then_inc(sem("gh_done"), 1)
                act.wait_ge(sem("dcT_full"), q * 1 + 1)
                act.activation(dcT[0:CAP, :], bank[4][0:CAP, 0:N], ACT.Copy).then_inc(sem("dcT_done"), 1)
                for m in range(FFN_S):
                    n = MIX1_END + m
                    high(n % RING, q * (16 * FFN_S // RING) + 16 * (n // RING + 1), m, q * FFN_S + (FFN_S + m + 1))
                    for c in silu_after(m):
                        act.wait_ge(sem("up_full"), q * NCH + (FT + c + 1))
                        act.wait_ge(sem("act_done"), q * NCH + (FT + 1 + c - 1))
                        act.activation(srow[0:CAP, c % 2, :], bank[2 * (c % 2)][0:CAP, :],
                                       ACT.Silu).then_inc(sem("silu_done"), 1)
                    for c in turned_after(m):
                        act.wait_ge(sem("turned_full"), q * NCH + (c + 1))
                        act.activation(eh[:, 4 * c:4 * c + 4, :],
                                       bank[4 + c % 2][:, 0:4 * CAP].rearrange("p (a b) -> p a b", b=CAP),
                                       ACT.Copy).then_inc(sem("eh_done"), 1)
                for half in range(2):
                    act.wait_ge(sem("ye_full"), q * 2 + (half + 1))
                    act.activation(ye[0:CAP, 512 * half:512 * half + 512], bank[6 + half][0:CAP, :],
                                   ACT.Copy).then_inc(sem("ye_done"), 1)

            with act.Fori(0, NE) as e:
                expert(e)
            act.wait_ge(sem("cnt_done"), 1)
            most = act.value_load(cnt[0:1, 0:1])
            with act.If(most > CAP):
                with act.Fori(NE, PASSES * NE) as q:
                    expert(q)
            rms(("end", 0), ("x_ffn", 2 * KD))
            root(5)

        @block.vector
        def _(v):
            def d(ins):
                then(v, ins, "v")

            def bc(ap, shape):
                return ap.broadcast_to(shape)

            def mean_root(ps, n, width):
                return v.tensor_scalar(ssb[:, :], ps[:, 0:N], 1.0 / width, EPS, ALU.mult, ALU.add)

            state = {"norms": 0}

            def norm(l, which, g, at):
                n = state["norms"]
                state["norms"] += 1
                mod = mods[:, l]
                d(v.scalar_tensor_tensor(mod[:, at + 8:at + 16, :], mod[:, at + 8:at + 16, :], 1.0,
                                         bc(col(l, g)[:, :, None], [P, KD, 1 + NB]), ALU.add, ALU.mult))
                name = ("rms", which, l)
                ps = filled(v, name)
                takes(v, mean_root(ps, n, D), name)
                v.tensor_copy(ini[:, 3:4], ssb[:, 0:1]).then_inc(sem("ss_done"), 1)
                v.wait_ge(sem("root_done"), n + 1)
                d(v.reciprocal(rstd[:, :], rstd[:, :]))
                for k in range(KD):
                    v.scalar_tensor_tensor(hT[:, k, 0:SEQ], xT[:, k, 0:SEQ], mod[:, at + 8 + k, 0:1], rstd[:, 0:SEQ],
                                           ALU.mult, ALU.mult).then_inc(sem("h_scaled"), 1)
                hs = hT[:, :, SEQ:N]
                d(v.tensor_tensor(hs, xT[:, :, SEQ:N], bc(rstd[:, None, SEQ:N], [P, KD, NB]), ALU.mult))
                d(v.tensor_tensor(hs, hs, mod[:, at + 8:at + 16, 1:1 + NB], ALU.mult))
                v.tensor_tensor(hs, hs, mod[:, at:at + 8, 1:1 + NB], ALU.add).then_inc(sem("h_smp"), 1)

            def c_(i):
                return sm[:, i, :]

            def tt(o, a, b, op):
                d(v.tensor_tensor(o, a, b, op))

            def ts(o, a, s1, s2, op0, op1=ALU.bypass):
                if s2 is None:
                    d(v.tensor_scalar(o, a, s1, None, op0))
                else:
                    d(v.tensor_scalar(o, a, s1, s2, op0, op1))

            MAGIC = 12582912.0

            def exp_to(o, x, k, r):
                ts(k, x, 1.4426950408889634, None, ALU.mult)
                ts(k, k, 126.0, -126.0, ALU.min, ALU.max)
                ts(k, k, MAGIC, None, ALU.add)
                ts(k, k, -MAGIC, None, ALU.add)
                d(v.scalar_tensor_tensor(r, k, -0.693359375, x, ALU.mult, ALU.add))
                d(v.scalar_tensor_tensor(r, k, 2.12194440e-4, r, ALU.mult, ALU.add))
                ts(o, r, 1.0 / 5040, 1.0 / 720, ALU.mult, ALU.add)
                for a in (1 / 120, 1 / 24, 1 / 6, 0.5, 1.0, 1.0):
                    tt(o, o, r, ALU.mult)
                    ts(o, o, a, None, ALU.add)
                ts(k, k, 127.0, None, ALU.add)
                d(v.tensor_copy(smi[:, :], k))
                d(v.tensor_single_scalar(smi[:, :], smi[:, :], 23, ALU.logical_shift_left))
                tt(o, o, smi[:, :].bitcast(F32), ALU.mult)

            def ada_mod(l, rd):
                name = ("adt", l, rd)
                ps = filled(v, name)[:, :].rearrange("p (t j x) -> p j t x", t=4, j=4)[:, :, :, 0:1 + NB]
                o = mods[:, l, 16 * rd:16 * rd + 16, :].rearrange("p (j t) b -> p j t b", t=4)
                b = col(l, "b_ada", 16 * rd, 16).rearrange("p (j t) -> p j t", t=4)
                takes(v, v.tensor_tensor(o, ps, bc(b[:, :, :, None], [P, 4, 4, 1 + NB]), ALU.add), name)

            def s5_params(l):
                lr, li = col(l, "lam_re"), col(l, "lam_im")
                dt, mag, th, k, r, co, si = (c_(i) for i in range(7))
                exp_to(dt, col(l, "log_dt"), k, r)
                tt(th, lr, dt, ALU.mult)
                exp_to(mag, th, k, r)
                tt(th, li, dt, ALU.mult)
                ts(k, th, 1.0 / (2 * math.pi), None, ALU.mult)
                ts(k, k, MAGIC, None, ALU.add)
                ts(k, k, -MAGIC, None, ALU.add)
                d(v.scalar_tensor_tensor(r, k, -6.28125, th, ALU.mult, ALU.add))
                d(v.scalar_tensor_tensor(r, k, -1.9350051879882812e-3, r, ALU.mult, ALU.add))
                d(v.scalar_tensor_tensor(r, k, -3.0199159819e-7, r, ALU.mult, ALU.add))
                ts(r, r, 0.5, None, ALU.mult)
                ts(c_(7), r, -1.0, None, ALU.mult)
                tt(c_(7), c_(7), r, ALU.max)
                d(v.tensor_scalar(c_(7), c_(7), -1.0, math.pi / 2, ALU.mult, ALU.add))
                for o, x in ((c_(8), r), (c_(9), c_(7))):
                    tt(c_(10), x, x, ALU.mult)
                    ts(o, c_(10), 1.0 / 6227020800, -1.0 / 39916800, ALU.mult, ALU.add)
                    for a in (1.0 / 362880, -1.0 / 5040, 1.0 / 120, -1.0 / 6, 1.0):
                        tt(o, o, c_(10), ALU.mult)
                        ts(o, o, a, None, ALU.add)
                    tt(o, o, x, ALU.mult)
                tt(si, c_(8), c_(9), ALU.mult)
                ts(si, si, 2.0, None, ALU.mult)
                tt(co, c_(8), c_(8), ALU.mult)
                d(v.tensor_scalar(co, co, -2.0, 1.0, ALU.mult, ALU.add))
                v.tensor_copy(c_(11), co).then_inc(sem("rot_done"), 1)
                ar_, ai, nr, den, kr, ki = (c_(i) for i in range(12, 18))
                tt(ar_, mag, co, ALU.mult)
                tt(ai, mag, si, ALU.mult)
                ts(nr, ar_, -1.0, None, ALU.add)
                tt(den, lr, lr, ALU.mult)
                tt(c_(18), li, li, ALU.mult)
                tt(den, den, c_(18), ALU.add)
                d(v.reciprocal(den, den))
                tt(kr, nr, lr, ALU.mult)
                tt(c_(18), ai, li, ALU.mult)
                tt(kr, kr, c_(18), ALU.add)
                tt(kr, kr, den, ALU.mult)
                tt(ki, ai, lr, ALU.mult)
                tt(c_(18), nr, li, ALU.mult)
                tt(ki, ki, c_(18), ALU.subtract)
                tt(ki, ki, den, ALU.mult)
                v.wait_ge(sem("c5_in"), 16 * (l + 1))
                W = [P, JT, 32]
                krb, kib = bc(kr[:, :, None], W), bc(ki[:, :, None], W)
                cr, ci, o, o2 = cpk[:, :, 0, :], cpk[:, :, 1, :], ckk[:, :, 0, :], ckk[:, :, 1, :]
                scr = wrot.rearrange("p a b -> p (a b)").rearrange("p (a b) -> p a b", b=32)
                tt(o, cr, krb, ALU.mult)
                tt(scr, ci, kib, ALU.mult)
                tt(o, o, scr, ALU.subtract)
                tt(o2, cr, kib, ALU.mult)
                tt(scr, ci, krb, ALU.mult)
                tt(o2, o2, scr, ALU.add)
                ts(o2, o2, -1.0, None, ALU.mult)
                ts(ci, ci, -1.0, None, ALU.mult)

            def s5_samples(l):
                name = ("bus", l)
                ps = filled(v, name)[:, 0:2 * JT * NB].rearrange("p (j c b) -> p j c b", c=2, b=NB)
                if l == 0:
                    v.wait_ge(ld["s5s"], 16)
                W = [P, JT, NB]
                a, b, e = (sx[:, i, :].rearrange("p (j b) -> p j b", b=NB) for i in range(3))
                A = [bc(c_(i)[:, :, None], W) for i in (12, 13, 16, 17)]
                sr, si = s5s[:, l, :, 0, :], s5s[:, l, :, 1, :]
                br, bi = ps[:, :, 0, :], ps[:, :, 1, :]
                tt(a, sr, A[0], ALU.mult)
                tt(e, si, A[1], ALU.mult)
                tt(a, a, e, ALU.subtract)
                tt(e, br, A[2], ALU.mult)
                tt(a, a, e, ALU.add)
                tt(e, bi, A[3], ALU.mult)
                tt(a, a, e, ALU.subtract)
                tt(b, sr, A[1], ALU.mult)
                tt(e, si, A[0], ALU.mult)
                tt(b, b, e, ALU.add)
                tt(e, br, A[3], ALU.mult)
                tt(b, b, e, ALU.add)
                takes(v, v.tensor_tensor(e, bi, A[2], ALU.mult), name)
                tt(si, b, e, ALU.add)
                v.tensor_copy(sr, a).then_inc(sem("s_smp"), 1)
                v.wait_ge(sem("s_smp"), l + 1)
                if l:
                    v.wait_ge(sem("s5_out"), 16)
                d(v.tensor_copy(s5o[:, :, :, 1:1 + NB], s5s[:, l]))

            def s5_tile(l, j):
                name = ("bu", l, j)
                ps = filled(v, name)[:, :].rearrange("p (c f t) -> p c f t", c=2, f=2)
                V = [P, 2, 2, HALF]
                cb = bc(cosT[:, j, None, None, :], V)
                sbn = bc(sinT[:, j, :, None, :], V)
                w4 = wrot.rearrange("p c (f t) -> p c f t", f=2)
                t4 = rrot[j % 2].rearrange("p c (f t) -> p c f t", f=2)
                if j >= 2 or l:
                    v.wait_ge(sem("s_back"), JT * l + j - 1)
                tt(w4, ps, cb, ALU.mult)
                takes(v, v.tensor_tensor(t4, ps[:, ::-1], sbn, ALU.mult), name)
                tt(w4, w4, t4, ALU.add)
                decay = bc(c_(1)[:, j:j + 1], [P, HALF])
                for c in range(2):
                    d(v.tensor_tensor_scan(t4[:, c, 0, :], decay, w4[:, c, 0, :], 0.0, ALU.mult, ALU.add))
                last_re, last_im = t4[:, 0, 0, HALF - 1:HALF], t4[:, 1, 0, HALF - 1:HALF]
                cE, sE, msE = pw[:, 0, j:j + 1], pw[:, 1, j:j + 1], pw[:, 2, j:j + 1]
                d(v.tensor_scalar(ini[:, 2:3], last_re, cE, None, ALU.mult))
                d(v.scalar_tensor_tensor(ini[:, 0:1], last_im, msE, ini[:, 2:3], ALU.mult, ALU.add))
                d(v.tensor_scalar(ini[:, 2:3], last_im, cE, None, ALU.mult))
                d(v.scalar_tensor_tensor(ini[:, 1:2], last_re, sE, ini[:, 2:3], ALU.mult, ALU.add))
                d(v.tensor_tensor_scan(t4[:, 0, 1, :], decay, w4[:, 0, 1, :], ini[:, 0:1], ALU.mult, ALU.add))
                v.tensor_tensor_scan(t4[:, 1, 1, :], decay, w4[:, 1, 1, :], ini[:, 1:2],
                                     ALU.mult, ALU.add).then_inc(sem("scanned"), 1)
                v.wait_ge(sem("scanned"), JT * l + j + 1)

            def s5_last(l):
                v.wait_ge(sem("s_back"), JT * (l + 1))
                fr, fi, e = pw[:, 5, :], pw[:, 6, :], sm[:, 18, :]
                tt(e, fi, c_(17), ALU.mult)
                o = s5o[:, :, :, 0]
                tt(o[:, :, 0], fr, c_(16), ALU.mult)
                tt(o[:, :, 0], o[:, :, 0], e, ALU.subtract)
                tt(e, fi, c_(16), ALU.mult)
                tt(o[:, :, 1], fr, c_(17), ALU.mult)
                v.tensor_tensor(o[:, :, 1], o[:, :, 1], e, ALU.add).then_inc(sem("s5o_done"), 1)

            def conv_tile(l, i):
                taken(v, ("in", l, UT + i))
                w = lambda t: col(l, "conv_w", QT * t + i, 1)
                o = cv[:, i, 0:SEQ]
                d(v.tensor_scalar(o, raw[:, i, 0:SEQ], w(0), None, ALU.mult))
                for t in range(1, TAPS):
                    d(v.scalar_tensor_tensor(o, raw[:, i, t:t + SEQ], w(t), o, ALU.mult, ALU.add))

            def conv_samples(l):
                W = [P, QT, NB]
                wv = lambda t: bc(col(l, "conv_w", QT * t, QT)[:, :, None], W)
                o = cv[:, :, SEQ:N]
                e = sx[:, 0, 0:QT * NB].rearrange("p (i b) -> p i b", b=NB)
                if l == 0:
                    v.wait_ge(ld["conv0"], 16)
                tt(o, conv0[:, l, :, :, 0], wv(0), ALU.mult)
                for t in range(1, TAPS):
                    src = conv0[:, l, :, :, t] if t < 3 else raw[:, :, 3 + SEQ:3 + N]
                    tt(e, src, wv(t), ALU.mult)
                    if t < 3:
                        tt(o, o, e, ALU.add)
                if l:
                    v.wait_ge(sem("cv_out"), 16)
                d(v.tensor_copy(cvo[:, :, 0, :], raw[:, :, SEQ:SEQ + 3]))
                d(v.tensor_copy(cvo[:, :, 1:1 + NB, 0:2], conv0[:, l, :, :, 1:3]))
                v.tensor_copy(cvo[:, :, 1:1 + NB, 2], raw[:, :, 3 + SEQ:3 + N]).then_inc(sem("cvo_done"), 1)
                v.wait_ge(sem("cvo_done"), l + 1)
                v.tensor_tensor(o, o, e, ALU.add).then_inc(sem("conv_done"), 1)

            def gate_logits(l):
                name = ("ab", l)
                ps = filled(v, name)[:, 0:24].rearrange("p (g w) -> p g w", w=8)
                if l == 0:
                    d(v.memset(gd[:, :, :], 0.0))
                x, ax, be = (gd[:, i, :].rearrange("p (g h) -> p g h", h=NH) for i in (2, 1, 4))
                bias = col(l, "dt_bias")
                for g0, g1, m in ((0, 2, P), (2, 3, NB)):
                    tt(x[0:m, g0:g1], ps[0:m, g0:g1, 0:NH], bc(bias[0:m, None, :], [m, g1 - g0, NH]), ALU.add)
                d(v.tensor_copy(be[:, 0:2], ps[:, 0:2, NH:]))
                takes(v, v.tensor_copy(be[0:NB, 2:3], ps[0:NB, 2:3, NH:]), name)
                ts(ax, x, -1.0, None, ALU.mult)
                v.tensor_tensor(ax, ax, x, ALU.max).then_inc(sem("ax_done"), 1)

            def gdn_columns(l):
                g3 = [P, 3, NH]
                r = lambda i: gd[:, i, :].rearrange("p (g h) -> p g h", h=NH)
                v.wait_ge(sem("a_ln"), 3 * (l + 1))
                ts(r(2), r(2), 0.0, None, ALU.max)
                tt(r(2), r(2), r(1), ALU.add)
                ts(gd[:, 3, 0:NH], gd[:, 3, 0:NH], -1.0, None, ALU.mult)
                v.tensor_tensor(r(0), r(2), bc(gd[:, 3, None, 0:NH], g3), ALU.mult).then_inc(sem("g_done"), 1)

            def qk_norms(l):
                v.wait_ge(sem("s5_free"), l + 1)
                for i in range(2 * NH):
                    name = ("qkn", l, i)
                    takes(v, v.tensor_scalar(nrm[:, i, :], filled(v, name)[:, 0:N], EPS, None, ALU.add), name)
                v.tensor_copy(ini[:, 3:4], nrm[:, 0, 0:1]).then_inc(sem("nrm_ss"), 1)
                v.wait_ge(sem("nrm_root"), l + 1)
                d(v.reciprocal(nrm[:, :, :], nrm[:, :, :]))
                q, k = cv[:, 0:NH, :], cv[:, NH:2 * NH, :]
                v.wait_ge(sem("cv_silu"), 3 * (l + 1))
                d(v.scalar_tensor_tensor(q, q, HD ** -0.5, nrm[:, 0:NH, :], ALU.mult, ALU.mult))
                v.tensor_tensor(k, k, nrm[:, NH:2 * NH, :], ALU.mult).then_inc(sem("qk_done"), 1)
                v.wait_ge(sem("qk_done"), l + 1)

            def gdn(l, fill):
                H4 = [P, NH, P]
                name = ("gcc", l)
                gc = gd[:, 5, 0:8]
                takes(v, v.tensor_copy(gc, filled(v, name)[:, 0:8]), name)
                psb = [filled(v, ("gcb", l, c))[:, :].rearrange("p (h t) -> p h t", h=NH) for c in range(NC)]
                c4 = lambda i, c: gd[:, i, 4 * c:4 * c + 4]
                for c in range(NC):
                    d(v.tensor_copy(c4(7, c), c4(5, c)))
                    d(v.tensor_copy(c4(9, c), psb[c][:, :, P - 1]))
                    tt(c4(8, c), c4(9, c), c4(5, c), ALU.subtract)
                v.tensor_copy(ini[:, 3:4], gd[:, 8, 0:1]).then_inc(sem("gdx_done"), 1)
                for c in range(NC):
                    bank_t = psb[c]
                    col_t = bc(c4(5, c)[:, :, None], H4)
                    tt(mats["decT"][c], bank_t, col_t, ALU.subtract)
                    ts(mats["dec"][c], mats["decT"][c], -1.0, 0.0, ALU.mult, ALU.min)
                    v.tensor_scalar(mats["decT"][c], mats["decT"][c], 0.0, None, ALU.min).then_inc(sem("diff_done"), 1)
                v.wait_ge(sem("a_col"), 2 * (l + 1))
                tt(gd[:, 10, 0:8], gd[:, 7, 0:8], gd[:, 4, 0:8], ALU.mult)
                for c in range(NC):
                    v.wait_ge(sem("a_dec"), 2 * NC * l + 2 * c + 2)
                    tt(mats["decT"][c], mats["decT"][c], bc(upper[:, None, :], H4), ALU.mult)
                    tt(mats["dec"][c], mats["dec"][c], bc(strict[:, None, :], H4), ALU.mult)
                    tt(mats["dec"][c], mats["dec"][c], bc(c4(4, c)[:, :, None], H4), ALU.mult)
                    name = ("ktok", l, c)
                    ps = filled(v, name)[:, :].rearrange("p (h t) -> p h t", h=NH)
                    tt(mats["kg"][c], ps, bc(c4(8, c)[:, :, None], H4), ALU.mult)
                    takes(v, v.tensor_tensor(mats["kbg"][c], ps, bc(c4(10, c)[:, :, None], H4), ALU.mult), name)
                    name = ("kk", l, c)
                    ps = filled(v, name)[:, :].rearrange("p (h t) -> p h t", h=NH)
                    takes(v, v.tensor_tensor(mats["ln"][c], ps, mats["dec"][c], ALU.mult), name)
                    v.tensor_scalar(mats["ln"][c], mats["ln"][c], -1.0, None, ALU.mult).then_inc(sem("ln_done"), 1)
                    v.wait_ge(sem("ln_done"), NC * l + c + 1)
                    name = ("qk", l, c)
                    ps = filled(v, name)[:, :].rearrange("p (h t) -> p h t", h=NH)
                    takes(v, v.tensor_tensor(mats["att"][c], ps, mats["decT"][c], ALU.mult), name)
                    taken(v, ("gcb", l, c))
                    v.tensor_tensor(mats["qg"][c], mats["qg"][c], cv[:, 0:NH, P * c:P * c + P],
                                    ALU.mult).then_inc(sem("qg_done"), 1)
                fill(3)
                for c in range(NC):
                    name = ("lt", l, c)
                    ps = filled(v, name)[:, :].rearrange("p (h t) -> p h t", h=NH)
                    tt(mats["e"][c], mats["ln"][c], bc(blk[:, None, :], H4), ALU.mult)
                    takes(v, v.tensor_copy(mats["lnT"][c], ps), name)
                    tt(mats["p"][c], mats["e"][c], bc(ident[:, None, :], H4), ALU.add)
                    tt(mats["eT"][c], mats["lnT"][c], bc(blkT[:, None, :], H4), ALU.mult)
                    v.tensor_tensor(mats["pT"][c], mats["eT"][c], bc(ident[:, None, :], H4),
                                    ALU.add).then_inc(sem("e_done"), 1)
                    v.wait_ge(sem("e_done"), NC * l + c + 1)
                    name = ("vtok", l, c)
                    ps = filled(v, name)[:, :].rearrange("p (h t) -> p h t", h=NH)
                    takes(v, v.tensor_tensor(mats["vb"][c], ps, bc(c4(4, c)[:, :, None], H4), ALU.mult), name)
                fill(4)
                for s in range(3):
                    fill(5 + 2 * s)
                    for c in range(NC):
                        filled(v, ("pT", l, s, c))
                        for n in ("p", "pT"):
                            name = (n, l, s, c)
                            ps = filled(v, name)[:, :].rearrange("p (h t) -> p h t", h=NH)
                            takes(v, v.tensor_tensor(mats[n][c], mats[n][c], ps, ALU.add), name)
                    fill(6 + 2 * s)
                for s in range(3):
                    for c in range(NC):
                        v.tensor_tensor(mats["eT"][c], mats["lnT"][c], bc(masks[:, 5 + s, None, :], H4),
                                        ALU.mult).then_inc(sem("lev_done"), 1)
                    fill(11 + 2 * s)
                    for c in range(NC):
                        filled(v, ("xT", l, s, c))
                        for n, m in (("p", "x"), ("pT", "xT"))[s == 2:]:
                            name = (m, l, s, c)
                            ps = filled(v, name)[:, :].rearrange("p (h t) -> p h t", h=NH)
                            takes(v, v.tensor_tensor(mats[n][c], mats[n][c], ps, ALU.add), name)
                    fill(12 + 2 * s)
                fill(17)
                for c in range(NC):
                    fill(18 + c)
                    name = ("s", l, c)
                    if c == 0:
                        ps = filled(v, name)[:, :].rearrange("p (h t) -> p h t", h=NH)
                        takes(v, v.tensor_copy(s_pr, ps), name)
                    else:
                        ps = filled(v, name)[:, :].rearrange("p (h t) -> p h t", h=NH)
                        tt(s_pr, s_pr, bc(c4(9, c)[:, :, None], H4), ALU.mult)
                        takes(v, v.tensor_tensor(s_pr, s_pr, ps, ALU.add), name)

            def gdn_samples(l, fill):
                hb = NH * NB
                W = [NB, NH, NB]
                v.wait_ge(sem("a_col"), 2 * (l + 1))
                idb = bc(ident[0:NB, None, 0:NB], W)
                tt(dg[:, 0], bc(gd[0:NB, 11, 8:12, None], W), idb, ALU.mult)
                v.tensor_tensor(dg[:, 1], bc(gd[0:NB, 4, 8:12, None], W), idb, ALU.mult).then_inc(sem("dg_done"), 1)
                q, k, vv = (cv[:, NH * i:NH * i + NH, SEQ:N] for i in range(3))
                r = lambda ap: ap.rearrange("p (h b) -> p h b", b=NB)
                d(v.tensor_copy(r(sx[:, 2, 0:hb]), k))
                v.tensor_tensor(r(sx[:, 0, 0:hb]), q, k, ALU.mult).then_inc(sem("qkp_done"), 1)
                name = ("skt", l)
                takes(v, v.tensor_copy(ktk[:, :], filled(v, name)[0:hb, 0:P]), name)
                name = ("sgb", l)
                takes(v, v.tensor_copy(rowb[:, :, :].rearrange("p a b -> p (a b)"), filled(v, name)[:, 0:2 * hb]), name)
                eg, be = rowb[:, 0, :], rowb[:, 1, :]
                fill(20)
                name = ("skq", l)
                ps = filled(v, name)[:, 0:2 * hb].rearrange("p (i c) -> p i c", c=2)
                vn, t, o = sx[:, 1, 0:hb], sx[:, 2, 0:hb], sx[:, 3, 0:hb]
                tt(t, ps[:, :, 1], eg, ALU.mult)
                takes(v, v.tensor_tensor(o, ps[:, :, 0], eg, ALU.mult), name)
                tt(r(vn), vv, r(t), ALU.subtract)
                v.tensor_tensor(vn, vn, be, ALU.mult).then_inc(sem("svn_done"), 1)
                v.wait_ge(sem("svn_done"), l + 1)
                name = ("sqk", l)
                takes(v, v.tensor_tensor(t, filled(v, name)[:, 0:hb], vn, ALU.mult), name)
                v.tensor_tensor(oT[:, :, SEQ:N], r(o), r(t), ALU.add).then_inc(sem("os_done"), 1)
                fill(21)
                name = ("svt", l)
                ps = filled(v, name)[0:hb, None, 0:P]
                gives(v.tensor_tensor(vm[0:hb], bc(ps, [hb, hb, P]), bc(ident[0:hb, 0:hb, None], [hb, hb, P]),
                                      ALU.mult), name)
                taken(v, name)
                v.tensor_copy(ini[:, 3:4], eg[:, 0:1]).then_inc(sem("vm_done"), 1)
                d(v.tensor_tensor(s0, s0, bc(eg[:, :, None], [P, hb, P]), ALU.mult))
                for i in range(NB):
                    name = ("so", l, i)
                    ps = filled(v, name)[:, :].rearrange("p (a b) -> p a b", b=P)
                    gives(v.tensor_tensor(s0[:, 4 * i:4 * i + 4, :], s0[:, 4 * i:4 * i + 4, :], ps, ALU.add), name)

            def gdn_output(l):
                for h in range(NH):
                    name = ("on", l, h)
                    takes(v, v.tensor_scalar(onrm[:, h, :], filled(v, name)[:, 0:N], 1.0 / HD, EPS, ALU.mult, ALU.add),
                          name)
                v.tensor_copy(ini[:, 3:4], onrm[:, 0, 0:1]).then_inc(sem("on_ss"), 1)
                v.wait_ge(sem("on_root"), l + 1)
                n4 = onrm
                d(v.reciprocal(n4, n4))
                d(v.scalar_tensor_tensor(oT, oT, col(l, "gdn_w"), n4, ALU.mult, ALU.mult))
                v.tensor_tensor(oT, oT, zs[:, :, :], ALU.mult).then_inc(sem("o_done"), 1)

            def unit(l, u):
                if u < 2 * KD:
                    return
                m = u - 2 * KD
                taken(v, ("glu", l, 2 * m + 1))
                name = ("glu", l, 2 * m)
                ga = gates[:, m, :]
                takes(v, v.tensor_tensor(ga, ga, filled(v, name)[:, 0:N], ALU.mult), name)
                v.tensor_tensor(ga, ga, tmp[:, m % 2, :], ALU.mult).then_inc(sem("glu_done"), 1)

            def mixer(l):
                def fill(step):
                    for u in units(step):
                        unit(l, u)

                if l == 0:
                    v.wait_ge(ld["cols"], 16)
                    v.wait_ge(ld["x"], 16)
                    s5_params(0)
                    ada_mod(0, 0)
                norm(l, "mix", "g_mix", 0)
                gate_logits(l)
                v.wait_ge(sem("tab_done"), l + 1)
                s5_samples(l)
                ends = ada_ends(l)
                for j in range(S5_STEPS):
                    s5_tile(l, j)
                    if j < QT:
                        conv_tile(l, j)
                    elif j == QT:
                        conv_samples(l)
                    if j - 1 in ends:
                        ada_mod(*ADA_IN[l][ends.index(j - 1)])
                    if j in Y_AFTER:
                        s5_output(l, Y_AFTER.index(j))
                ada_mod(*ADA_IN[l][-1])
                s5_output(l, UT - 1)
                s5_last(l)
                v.tensor_copy(ini[:, 3:4], s5o[:, 0, 0, 0:1]).then_inc(sem("s5_free"), 1)
                gdn_columns(l)
                fill(0)
                fill(1)
                qk_norms(l)
                fill(2)
                gdn(l, fill)
                v.tensor_copy(ini[:, 3:4], s_pr[:, 0, 0:1]).then_inc(sem("sp_done"), 1)
                gdn_samples(l, fill)
                gdn_output(l)
                v.wait_ge(sem("glu_done"), KD * (l + 1))
                for m in range(KD):
                    name = ("go", l, m)
                    takes(v, v.tensor_tensor(hT[:, m, :], gates[:, KD + m, :], filled(v, name)[:, 0:N], ALU.mult), name)
                    v.tensor_tensor(hT[:, m, :], hT[:, m, :], gates[:, m, :], ALU.add).then_inc(sem("merged"), 1)
                residual(lambda m: (filled(v, ("wo", l, m)), lambda ins: gives(ins, ("wo", l, m))), 16, "x_mix", mods[:, l])

            def residual(src, at, done, mod, tiles=range(KD)):
                for m in tiles:
                    ps, mark = src(m)
                    e = tmp[:, 0, 0:NB]
                    d(v.tensor_tensor(e, ps[:, SEQ:N], mod[:, at + m, 1:1 + NB], ALU.mult))
                    d(v.tensor_tensor(xT[:, m, SEQ:N], xT[:, m, SEQ:N], e, ALU.add))
                    ins = v.scalar_tensor_tensor(xT[:, m, 0:SEQ], ps[:, 0:SEQ], mod[:, at + m, 0:1], xT[:, m, 0:SEQ],
                                                 ALU.mult, ALU.add)
                    mark(ins)
                    v.tensor_copy(ini[:, 3:4], mod[:, at + m, 0:1]).then_inc(sem(done), 1)

            def s5_output(l, i):
                name = ("y", l, i)
                ps = filled(v, name)[:, 0:N]
                gives(v.scalar_tensor_tensor(uT[:, i, :], uT[:, i, :], col(l, "s5_d", i, 1), ps, ALU.mult, ALU.add), name)
                taken(v, name)
                v.tensor_copy(ini[:, 3:4], uT[:, i, 0:1]).then_inc(sem("y_sum"), 1)

            def route():
                lg = rtx[:, 0:3, :]
                name = ("rl",)
                ps = filled(v, name)[:, 0:24].rearrange("p (g e) -> p g e", e=NE)
                d(v.memset(rtx[:, :, :], 0.0))
                br = col(1, "b_router")
                tt(lg[:, 0:2], ps[:, 0:2], bc(br[:, None, :], [P, 2, NE]), ALU.add)
                takes(v, v.tensor_tensor(lg[0:NB, 2:3], ps[0:NB, 2:3], bc(br[0:NB, None, :], [NB, 1, NE]), ALU.add), name)
                v.wait_ge(ld["sel"], 16)
                W = [P, NE, NE]
                big = ar(8 * B1, 2, NE, NE)
                for g in range(3):
                    mine, other = bc(lg[:, g, :, None], W), bc(lg[:, g, None, :], W)
                    tt(big[:, 0], other, mine, ALU.is_gt)
                    tt(big[:, 1], other, mine, ALU.is_equal)
                    tt(big[:, 1], big[:, 1], selw[:, :, :], ALU.mult)
                    tt(big[:, 0], big[:, 0], big[:, 1], ALU.add)
                    d(v.tensor_reduce(rtx[:, 3 + g, :], big[:, 0], AX.X, ALU.add))
                d(v.tensor_scalar(rt[:, :, :], rtx[:, 3:6, :], 2.0, None, ALU.is_lt))
                d(v.tensor_reduce(rtx[:, 9, 0:3], lg, AX.X, ALU.max))
                v.tensor_tensor(rtx[:, 6:9, :], lg, bc(rtx[:, 9, 0:3, None], [P, 3, NE]),
                                ALU.subtract).then_inc(sem("sel_done"), 1)
                v.wait_ge(sem("rexp_done"), 1)
                cw = rtx[:, 6:9, :]
                tt(cw, cw, rt[:, :, :], ALU.mult)
                d(v.tensor_reduce(rtx[:, 9, 0:3], cw, AX.X, ALU.add))
                d(v.reciprocal(rtx[:, 9, 0:3], rtx[:, 9, 0:3]))
                tt(cw, cw, bc(rtx[:, 9, 0:3, None], [P, 3, NE]), ALU.mult)
                name = ("rank",)
                ps = filled(v, name)[:, 0:32].rearrange("p (g e) -> p g e", e=NE)
                pos = rtx[:, 3:6, :]
                tt(pos[:, 0:2], ps[:, 0:2], rt[:, 0:2, :], ALU.mult)
                tt(pos[0:NB, 2], ps[0:NB, 2], rt[0:NB, 2, :], ALU.mult)
                ts(pos, pos, -1.0, None, ALU.add)
                d(v.tensor_reduce(rtx[:, 10, 0:1], ps[:, 3], AX.X, ALU.max))
                takes(v, v.tensor_copy(cnt[:, :], rtx[0:1, 10, 0:1]), name)
                v.memset(acc, 0.0).then_inc(sem("cnt_done"), 1)
                v.wait_ge(ld["iota"], 16)
                v.wait_ge(sem("cnt_done"), 1)

            def expert(q, e, a):
                pos, cw = rtx[:, 3:6, :], rtx[:, 6:9, :]
                io = iota[:, 0:CAP] if a is None else iota[:, bass.ds(a * CAP, CAP)]
                for g in range(3):
                    m = P if g < 2 else NB
                    p1, c1 = pos[0:m, g, bass.ds(e, 1)], cw[0:m, g, bass.ds(e, 1)]
                    ioa = iota[0:m, 0:CAP] if a is None else iota[0:m, bass.ds(a * CAP, CAP)]
                    v.tensor_scalar(dw[0:m, g, :], ioa, p1, c1, ALU.is_equal, ALU.mult)
                    ins = v.tensor_scalar(dsel[0:m, g, :], ioa, p1, None, ALU.is_equal)
                ins.then_inc(sem("dsel_done"), 1)
                four = lambda b: b[:, 0:4 * CAP].rearrange("p (a b) -> p a b", b=CAP)
                for half in range(2):
                    v.wait_ge(sem("gh_done"), q * 2 + (half + 1))
                    i = slice(4 * half, 4 * half + 4)
                    v.tensor_tensor(gl[:, i, :], four(bank[half]), gh[:, i, :].bitcast(F32),
                                    ALU.subtract).then_inc(sem("gl_done"), 1)
                for m in range(FFN_S):
                    low(m, q * FFN_S + (FFN_S + m + 1))
                    for c in silu_after(m):
                        v.wait_ge(sem("silu_done"), q * NCH + (FT + c + 1))
                        v.tensor_tensor(erow[0:CAP, c % 2, :], srow[0:CAP, c % 2, :], bank[2 * (c % 2) + 1][0:CAP, :],
                                        ALU.mult).then_inc(sem("act_done"), 1)
                    for c in turned_after(m):
                        v.wait_ge(sem("eh_done"), q * NCH + (c + 1))
                        i = slice(4 * c, 4 * c + 4)
                        v.tensor_tensor(el[:, i, :], four(bank[4 + c % 2]), eh[:, i, :].bitcast(F32),
                                        ALU.subtract).then_inc(sem("turned_done"), 1)
                for m in range(KD):
                    v.wait_ge(sem("down_full"), q * KD + (KD + m + 1))
                    v.tensor_tensor(acc[:, m, :], acc[:, m, :], bank[4 + m % 2][:, 0:N],
                                    ALU.add).then_inc(sem("down_taken"), 1)

            v.memset(ones[:, :], 1.0).then_inc(sem("ones_done"), 1)
            v.wait_ge(ld["masks"], 16)
            mixer(0)
            norm(0, "ffn", "g_ffn", 24)
            v.tensor_copy(ini[:, 3:4], rstd[:, 0:1]).then_inc(sem("act_done"), 1)
            v.wait_ge(sem("hh_done"), 1)
            v.tensor_tensor(hl[:, :, :], hT[:, :, :], hh[:, :, :].bitcast(F32), ALU.subtract).then_inc(sem("hl_done"), 1)

            def low(m, count):
                v.wait_ge(sem("hi_done"), count)
                v.tensor_tensor(wlo[:, m % SPL, :], ring[:, (low.base + m) % RING, :], whi[:, m % SPL, :].bitcast(F32),
                                ALU.subtract).then_inc(sem("lo_done"), 1)

            low.base = MIX0_END
            BODY = 4 * RING

            def dense_tile(it, f):
                v.wait_ge(sem("silu_done"), it * (BODY // 2) + (f + 1))
                v.tensor_tensor(sg[:, f % 2, :], sg[:, f % 2, :], bank[2 * (f % 2) + 1][:, 0:N],
                                ALU.mult).then_inc(sem("act_done"), 1)
                v.wait_ge(sem("ah_done"), it * (BODY // 2) + (f + 1))
                i = bass.ds(it * (BODY // 2) + f, 1)
                v.tensor_tensor(alo[:, i, :], sg[:, f % 2:f % 2 + 1, :], ahi[:, i, :].bitcast(F32),
                                ALU.subtract).then_inc(sem("al_done"), 1)

            with v.Fori(0, UP_S // BODY) as it:
                for s in range(BODY):
                    low(s, it * BODY + (s + 1))
                    if s >= 5 and s % 2 == 1:
                        dense_tile(it, (s - 5) // 2)
                dense_tile(it, BODY // 2 - 2)
                dense_tile(it, BODY // 2 - 1)

            def down(m):
                v.wait_ge(sem("down_full"), m + 1)
                return bank[4 + m % 2], lambda ins: ins.then_inc(sem("down_taken"), 1)

            done = 0
            for s in range(UP_S, FFN_S):
                low(s, s + 1)
                while done < KD and (FT * (done + 1) - 1) // SLOT + SPL <= s - UP_S:
                    residual(down, 40, "x_ffn", mods[:, 0], [done])
                    done += 1
            residual(down, 40, "x_ffn", mods[:, 0], range(done, KD))
            low.base = MIX1_END
            s5_params(1)
            mixer(1)
            norm(1, "ffn", "g_ffn", 24)
            route()
            with v.Fori(0, NE) as e:
                expert(e, e, None)
            v.wait_ge(sem("down_taken"), KD * (NE + 1))
            most = v.value_load(cnt[0:1, 0:1])
            with v.If(most > CAP):
                with v.Fori(1, PASSES) as a:
                    with v.Fori(0, NE) as e:
                        expert(a * NE + e, e, a)
                v.wait_ge(sem("down_taken"), KD * (PASSES * NE + 1))

            def summed(m):
                return acc[:, m, :], lambda ins: ins.then_inc(sem("fin_x"), 1)

            residual(summed, 40, "x_ffn", mods[:, 1])
            v.wait_ge(sem("end_full"), 1)
            d(mean_root(bank[0], 4, D))
            v.tensor_copy(ini[:, 3:4], ssb[:, 0:1]).then_inc(sem("ss_done"), 1)
            v.wait_ge(sem("root_done"), 5)
            d(v.reciprocal(rstd[:, :], rstd[:, :]))
            for k in range(KD):
                v.scalar_tensor_tensor(hT[:, k, :], xT[:, k, :], col(0, "g_final", k, 1), rstd[:, :],
                                       ALU.mult, ALU.mult).then_inc(sem("y_done"), 1)

        @block.gpsimd
        def _(pool):
            pool.memset(cT[:, :, :], 0.0).then_inc(sem("c_zero"), 1)

            def p(ins):
                then(pool, ins, "p")

            def tables(l):
                pool.wait_ge(sem("rot_done"), l + 1)
                cd, sd, ms, t1, t2 = (pw[:, i, :] for i in range(5))
                p(pool.tensor_copy(cd, sm[:, 5, :]))
                p(pool.tensor_copy(sd, sm[:, 6, :]))
                p(pool.memset(cosT[:, :, 0:1], 1.0))
                p(pool.memset(sinT[:, :, :, 0:1], 0.0))
                n = 1
                while n < HALF:
                    W = [P, JT, n]
                    c, s = cosT[:, :, 0:n], sinT[:, :, 0, 0:n]
                    co, so, x = cosT[:, :, n:2 * n], sinT[:, :, 0, n:2 * n], sinT[:, :, 1, n:2 * n]
                    cb, sbb = cd[:, :, None].broadcast_to(W), sd[:, :, None].broadcast_to(W)
                    p(pool.tensor_tensor(co, c, cb, ALU.mult))
                    p(pool.tensor_tensor(x, s, sbb, ALU.mult))
                    p(pool.tensor_tensor(co, co, x, ALU.subtract))
                    p(pool.tensor_tensor(so, s, cb, ALU.mult))
                    p(pool.tensor_tensor(x, c, sbb, ALU.mult))
                    p(pool.tensor_tensor(so, so, x, ALU.add))
                    p(pool.tensor_tensor(t1, cd, cd, ALU.mult))
                    p(pool.tensor_tensor(t2, sd, sd, ALU.mult))
                    p(pool.tensor_tensor(sd, sd, cd, ALU.mult))
                    p(pool.tensor_tensor(cd, t1, t2, ALU.subtract))
                    p(pool.tensor_scalar(sd, sd, 2.0, None, ALU.mult))
                    n *= 2
                p(pool.tensor_scalar(ms, sd, -1.0, None, ALU.mult))
                pool.tensor_scalar(sinT[:, :, 1, :], sinT[:, :, 0, :], -1.0, None, ALU.mult).then_inc(sem("tab_done"), 1)

            def layer(l):
                if l:
                    pool.wait_ge(sem("x_ffn"), KD)
                pool.memset(raw[:, :, 0:3], 0.0).then_inc(sem("pool_zero"), 1)
                tables(l)
                for j in range(JT):
                    pool.wait_ge(sem("scanned"), JT * l + j + 1)
                    if j >= 8:
                        filled(pool, ("y", l, j // 4 - 2))
                    V = [P, 2, 2, HALF]
                    r4, s4, p4 = (t.rearrange("p c (f t) -> p c f t", f=2) for t in (rrot[j % 2], st[:, j % 8], prot))
                    for c in range(2):
                        cb = cosT[:, j, None, :].broadcast_to([P, 2, HALF])
                        sb_ = sinT[:, j, c, None, :].broadcast_to([P, 2, HALF])
                        p(pool.tensor_tensor(p4[:, c], r4[:, c], cb, ALU.mult))
                        p(pool.tensor_tensor(s4[:, c], r4[:, 1 - c], sb_, ALU.mult))
                    p(pool.tensor_tensor(st[:, j % 8], prot, st[:, j % 8], ALU.subtract))
                    pool.tensor_copy(pw[:, 5:7, j], st[:, j % 8, :, SEQ - 1]).then_inc(sem("s_back"), 1)
                    if j == QT + 1:
                        pool.wait_ge(sem("cvo_done"), l + 1)
                        pool.dma_start(conv_out[l], cvo[:, :, :, :]).then_inc(sem("cv_out"), 16)
                pool.wait_ge(sem("s5o_done"), l + 1)
                pool.dma_start(s5_out[l], s5o[:, :, :, :]).then_inc(sem("s5_out"), 16)
                pool.wait_ge(sem("sp_done"), l + 1)
                pool.dma_start(gdnp_out[l], s_pr).then_inc(sem("sp_out"), 16)
                for i in range(NB):
                    taken(pool, ("so", l, i))
                pool.dma_start(gdns_out[l], s0).then_inc(sem("gs_out"), 16)
                pool.wait_ge(sem("gs_out"), 16 * (l + 1))

            layer(0)
            layer(1)
            for n in ("cv_out", "s5_out", "sp_out"):
                pool.wait_ge(sem(n), 32)


def _blocks(w):
    K, M = w.shape
    return w.reshape(K // P, P, M // P, P).transpose(2, 0, 1, 3)


def _slots(blocks):
    n = blocks.shape[0]
    return blocks.reshape(n // SLOT, SLOT, P, P).transpose(0, 2, 1, 3).reshape(n // SLOT, P, SLOT * P)


def _flat(tiles):
    return tiles.reshape(-1, P, P)


def _pairs(w):
    b = _blocks(w)
    h = b.shape[0] // 2
    return _flat(np.stack([b[:h], b[h:]], axis=1))


def _fm(a):
    r, f = a.shape
    return a.T.reshape(f // P, P, r).transpose(1, 0, 2)


def _const():
    i = np.arange(P)
    r, c = i[:, None], i[None, :]
    m = {"ident": r == c, "upper": r <= c, "strict": r > c}
    m["blk"] = (r > c) & (r // BASE == c // BASE)
    m["blkT"] = m["blk"].T
    for s in range(3):
        b = BASE << s
        m[f"lev{s}"] = (r // (2 * b) == c // (2 * b)) & (r // b % 2 == 0) & (c // b % 2 == 1)
    masks = np.stack([m[n] for n in MASKS], axis=1).astype(np.float32)
    iota = np.broadcast_to(np.arange(PASSES * CAP, dtype=np.float32), (P, PASSES * CAP)).copy()
    sel = np.broadcast_to((np.arange(NE)[None, :] < np.arange(NE)[:, None]).astype(np.float32), (P, NE, NE)).copy()
    return masks, iota, sel


def layouts(i):
    L = range(DEPTH)
    x = np.concatenate([i["x_prompt"][0], i["x_sample"][:, 0]], axis=0)
    c = np.concatenate([i["c_prompt"], i["c_sample"]], axis=0)
    masks, iota, sel = _const()
    feat = lambda v: v.reshape(-1, P).T
    row = lambda v: np.broadcast_to(v[None, :], (P, v.shape[0]))
    cols = []
    for l in L:
        dt = np.repeat(i["s5_log_dt"][l], ST)
        parts = dict(g_mix=feat(i["g_mix"][l]), g_ffn=feat(i["g_ffn"][l]), b_ada=feat(i["b_ada"][l]),
                     s5_d=feat(i["s5_d"][l]), conv_w=feat(i["gdn_conv_w"][l].reshape(-1)),
                     gdn_w=i["gdn_norm_w"][l][:, None], lam_re=feat(i["s5_lambda_re"][l].reshape(-1)),
                     lam_im=feat(i["s5_lambda_im"][l].reshape(-1)), log_dt=feat(dt), a_log=row(i["gdn_a_log"][l]),
                     dt_bias=row(i["gdn_dt_bias"][l]), g_final=feat(i["g_final"]), b_router=row(i["b_router"][0]))
        cols.append(np.concatenate([parts[n] for n in COLS], axis=1))
    cols = np.stack(cols, axis=1)
    bpk = np.zeros((DEPTH, UT, 4, 2, C5, 2, 2, ST), np.float32)
    cpk = np.zeros((DEPTH, 2, ST, JT, 2, 2, C5), np.float32)
    for part, (bn, cn) in enumerate((("s5_b_re", "s5_c_re"), ("s5_b_im", "s5_c_im"))):
        b = i[bn].reshape(DEPTH, UT, 4, 2, ST, C5)
        cc = i[cn].reshape(DEPTH, JT, 2, C5, ST)
        for g in range(2):
            bpk[:, :, :, g, :, part, g, :] = b[:, :, :, g].transpose(0, 1, 2, 4, 3)
            cpk[:, g, :, :, part, g, :] = cc[:, :, g].transpose(0, 3, 1, 2)
    bpk = bpk.reshape(DEPTH, UT, P, 2, P).transpose(0, 2, 1, 3, 4)
    cpk = cpk.reshape(DEPTH, P, JT, 2, 32)
    s5 = np.stack([i["state_s5_re"], i["state_s5_im"]], axis=1).reshape(DEPTH, 2, NB, JT, P).transpose(4, 0, 3, 1, 2)
    gdn = i["state_gdn"].transpose(0, 3, 2, 1, 4).reshape(DEPTH, P, NH * NB, P)
    conv = i["state_conv"].reshape(DEPTH, NB, 3, QT, P).transpose(4, 0, 3, 1, 2)
    ab = S5W + 3 * NH * HD + NH * HD
    wab = np.stack([i["w_in"][l][:, ab:ab + 2 * NH].reshape(KD, P, 2 * NH).transpose(1, 0, 2) for l in L], axis=1)
    wr = i["w_router"][0].reshape(KD, P, NE).transpose(1, 0, 2)
    def ada(l, rd):
        w = i["w_ada"][l][:, 2048 * rd:2048 * rd + 2048]
        return w.reshape(KD, P, 2, 1024).transpose(0, 2, 1, 3).reshape(ADA_S, P, 1024)

    parts = [ada(0, 0)]
    for l in L:
        w = i["w_in"][l]
        w = _slots(_flat(_blocks(np.concatenate([w[:, :ab], w[:, ab + 2 * NH:]], axis=1))))
        glu = _slots(_pairs(i["w_s5_glu"][l]))
        rounds = np.concatenate([ada(*a) for a in ADA_IN[l]], axis=0)
        n = len(ADA_IN[l])
        parts.append(w[:UT])
        for j in range(S5_STEPS):
            parts += [w[UT + j:UT + j + 1], rounds[n * j:n * j + n]]
        parts += [w[UT + S5_STEPS:], glu, _slots(_flat(_blocks(i["w_gdn_out"][l]))), _slots(_flat(_blocks(i["w_out"][l])))]
        if l == 0:
            parts += [_slots(_pairs(i["w_ffn_gate_up"][0])), _slots(_flat(_blocks(i["w_ffn_down"][0])))]
    for e in range(NE):
        parts += [i["w_exp_gate_up"][0, e].reshape(KD, P, 2, NCH, CH).transpose(3, 0, 1, 2, 4).reshape(UP_S, P, 2 * CH),
                  i["w_exp_down"][0, e].reshape(DOWN_S, P, D)]
    w = np.concatenate(parts, axis=0)
    return dict(x=_fm(x), c=_fm(c), cols=cols, masks=masks, iota=iota, sel=sel, bpk=bpk, cpk=cpk, s5s=s5, gdn=gdn,
                conv=conv, wab=wab, wr=wr, w=w)


OUTS = {"y": (P, KD, N), "s5": (DEPTH, P, JT, 2, 1 + NB), "gdnp": (DEPTH, P, NH, P), "gdns": (DEPTH, P, NH * NB, P),
        "convo": (DEPTH, P, QT, 1 + NB, 3)}


def kernel(**inputs):
    import concourse.bacc as bacc
    from concourse.bass_utils import run_bass_kernel_spmd

    nc = bacc.Bacc("TRN2", target_bir_lowering=False, num_devices=1)
    arrays, args = {}, []
    for name, a in layouts({k: np.asarray(v) for k, v in inputs.items()}).items():
        a = np.ascontiguousarray(a)
        arrays[f"in_{name}"] = a
        args.append(nc.dram_tensor(f"in_{name}", a.shape, F32, kind="ExternalInput").ap())
    for name, shape in OUTS.items():
        args.append(nc.dram_tensor(f"out_{name}", shape, F32, kind="ExternalOutput").ap())
    trunk_program(nc, *args)
    r = run_bass_kernel_spmd(nc, [arrays], core_ids=[0]).results[0]
    y = r["out_y"].transpose(2, 1, 0).reshape(N, D)
    s5 = r["out_s5"].transpose(0, 3, 4, 2, 1).reshape(DEPTH, 2, 1 + NB, G5, ST)
    gp = r["out_gdnp"].transpose(0, 2, 1, 3)[:, None]
    gs = r["out_gdns"].reshape(DEPTH, P, NH, NB, P).transpose(0, 3, 2, 1, 4)
    cv = r["out_convo"].transpose(0, 3, 4, 2, 1).reshape(DEPTH, 1 + NB, 3, QT * P)
    out = (y[None, :SEQ], y[SEQ:, None], s5[:, 0, :1], s5[:, 1, :1], gp, cv[:, :1], s5[:, 0, 1:], s5[:, 1, 1:], gs,
           cv[:, 1:])
    return tuple(np.ascontiguousarray(a) for a in out)
```

```python
import math
from contextlib import ExitStack

import numpy as np

import concourse.bass as bass
from concourse import mybir

ALU = mybir.AluOpType
ACT = mybir.ActivationFunctionType
AX = mybir.AxisListType
F32 = mybir.dt.float32
F32R = mybir.dt.float32r
I32 = mybir.dt.int32

P = 128
D = 1024
SEQ = 256
NB = 8
N = SEQ + NB
KD = D // P
DEPTH = 2
S5W = D // 2
G5, C5, ST = 32, 16, 64
UT = S5W // P
JT = G5 * ST // P
HD = 128
NH = 4
QT = 3 * NH
TAPS = 4
HALF = SEQ // 2
NC = SEQ // HALF
FF = 7 * D // 2
FT = FF // P
NE = 8
CAP = 128
PASSES = -(-N // CAP)
EPS = 1e-6

SLOT = 8
RING = 7
SPL = 4
ADA_T = 6 * D // P
ADA_S = KD * 2
S5_STEPS = JT
ADA_IN = ([(0, 1), (0, 2), (1, 0)], [(1, 1), (1, 2)])
MIX_S = UT + 4 * NH + 2 * KD + 2 * KD * UT // SLOT + KD * NH // SLOT + KD * KD // SLOT
UP_S, DOWN_S = 2 * FT * KD // SLOT, FT * KD // SLOT
FFN_S = UP_S + DOWN_S
MIX0_END = ADA_S * (1 + len(ADA_IN[0])) + MIX_S
FFN0_END = MIX0_END + FFN_S
MIX1_END = FFN0_END + ADA_S * len(ADA_IN[1]) + MIX_S
CH = 512
NCH = FF // CH

COLS = {}
_at = 0
for _n, _w in (("g_mix", KD), ("g_ffn", KD), ("b_ada", ADA_T), ("s5_d", UT), ("conv_w", TAPS * QT), ("gdn_w", 1),
               ("lam_re", JT), ("lam_im", JT), ("log_dt", JT), ("a_log", NH), ("dt_bias", NH), ("g_final", KD),
               ("b_router", NE)):
    COLS[_n] = (_at, _w)
    _at += _w
NCOL = _at
MASKS = ["ident", "upper", "strict", "blk", "blkT", "lev0", "lev1", "lev2"]
BASE = 16


def trunk_program(nc, x_in, c_in, cols_in, masks_in, iota_in, sel_in, bpk_in, cpk_in, s5s_in, gdn_in, conv_in,
                  wab_in, wr_in, w_in, y_out, s5_out, gdnp_out, gdns_out, conv_out):
    with ExitStack() as ctx:
        def sb(name, shape, dt=F32):
            return ctx.enter_context(nc.sbuf_tensor(name, shape, dt))

        sems = {}

        def sem(name):
            if name not in sems:
                sems[name] = ctx.enter_context(nc.semaphore(name))
            return sems[name]

        xT = sb("xT", [P, KD, N])
        hT = sb("hT", [P, KD, N])
        slab = sb("slab", [P, QT * (3 + N) + QT * N])
        raw = slab[:, 0:QT * (3 + N)].rearrange("p (a b) -> p a b", b=3 + N)
        cv = slab[:, QT * (3 + N):].rearrange("p (a b) -> p a b", b=N)
        arena = sb("arena", [P, 2 * FT * N])
        ring = sb("ring", [P, RING, SLOT * P])
        bpk = sb("bpk", [P, UT, 2, P])
        cpk = sb("cpk", [P, JT, 2, 32])
        ckk = sb("ckk", [P, JT, 2, 32])
        cols = sb("cols", [P, DEPTH, NCOL])
        masks = sb("masks", [P, len(MASKS), P])
        selw = sb("selw", [P, NE, NE])
        ones = sb("ones", [P, P])
        cT = sb("cT", [P, KD, 32])
        mods = sb("mods", [P, DEPTH, ADA_T, 1 + NB])
        whi = sb("whi", [P, SPL, SLOT * P], F32R)
        wlo = sb("wlo", [P, SPL, SLOT * P], F32R)
        s5s = sb("s5s", [P, DEPTH, JT, 2, NB])
        conv0 = sb("conv0", [P, DEPTH, QT, NB, 3])
        wab = sb("wab", [P, DEPTH, KD, 2 * NH])
        wr = sb("wr", [P, KD, NE])
        s5o = sb("s5o", [P, JT, 2, 1 + NB])
        cvo = sb("cvo", [P, QT, 1 + NB, 3])
        rstd = sb("rstd", [P, N])
        tmp = sb("tmp", [P, 2, N])
        ssb = tmp[:, 1, :]
        sm = sb("sm", [P, 19, JT])
        pw = sb("pw", [P, 7, JT])
        smi = sb("smi", [P, JT], I32)
        sx = sb("sx", [P, 4, JT * NB])
        gd = sb("gd", [P, 12, 3 * NH])
        dg = sb("dg", [NB, 2, NH, NB])
        rowb = sb("rowb", [P, 2, NH * NB])
        ktk = sb("ktk", [NH * NB, P])
        ini = sb("ini", [P, 4])
        rt = sb("rt", [P, 3, NE])
        rtx = sb("rtx", [P, 12, NE])
        pick = sb("pick", [P, 2, 3, NE + 1])
        cnt = sb("cnt", [1, 1], I32)
        bank = [ctx.enter_context(nc.psum_tensor(f"bank{b}", [P, 512], F32)) for b in range(8)]
        where = lambda t: nc.lookup_mls(t).memorylocations[0].addr
        arena_at, slab_at = where(arena), where(slab)

        def over(name, shape, base, at, dt=F32R):
            return nc.alloc_sbuf_tensor_at(name, shape, dt, offset=base + 4 * at)

        gates, adas = over("gates", [P, 2 * KD, N], where(whi), 0, F32), over("adas", [P, 512], where(whi), 2 * KD * N, F32)
        behind = 2 * KD * N + 512
        uT, zs = over("uT", [P, UT, N], where(whi), behind, F32), over("zs", [P, NH, N], where(whi), behind + UT * N, F32)

        ident, upper, strict, blk, blkT = (masks[:, i, :] for i in range(5))

        def ar(at, *shape):
            n = int(np.prod(shape))
            v = arena[:, at:at + n]
            if len(shape) == 2:
                return v.rearrange("p (a b) -> p a b", b=shape[1])
            if len(shape) == 3:
                return v.rearrange("p (a b c) -> p a b c", b=shape[1], c=shape[2])
            return v

        B1 = 1024
        cosT = ar(0, JT, HALF)
        sinT = ar(2 * B1, JT, 2, HALF)
        st = ar(6 * B1, 8, 2, SEQ)
        wrot = ar(10 * B1, 2, SEQ)
        rrot = [ar(10 * B1 + 512, 2, SEQ), ar(11 * B1, 2, SEQ)]
        prot = ar(11 * B1 + 512, 2, SEQ)
        sq = ar(6 * B1, KD, N)
        xsq = cv[:, 0:KD, :]
        nrm = ar(0, KD, N)
        onrm = hT[:, 0:NH, :]
        mats = {}
        for i, names in enumerate(("decT vn", "dec y", "ln vb", "lnT", "att", "e", "eT", "p", "pT", "kbg nwT", "kg", "qg")):
            for n in names.split():
                mats[n] = [ar(i * B1 + c * 512, NH, P) for c in range(NC)]
        s_pr = ar(5 * B1, NH, P)
        s0 = ar(5 * B1, NH * NB, P)
        vm = ar(0, NH * NB, P)
        oT = raw[:, 0:NH, 3:3 + N]
        osq = hT[:, NH:2 * NH, :]
        hh, hl = over("hh", [P, KD, N], slab_at, 0), over("hl", [P, KD, N], slab_at, KD * N)
        ahi, alo = over("ahi", [P, FT, N], arena_at, 0), over("alo", [P, FT, N], arena_at, FT * N)
        sg = tmp
        htok = slab[:, 0:3 * D].rearrange("p (a b) -> p a b", b=D)
        acc = cv[:, 0:KD, :]
        gh, gl = over("gh", [P, KD, CAP], arena_at, 0), over("gl", [P, KD, CAP], arena_at, KD * CAP)
        eh, el = over("eh", [P, FT, CAP], arena_at, 2 * B1), over("el", [P, FT, CAP], arena_at, 2 * B1 + FT * CAP)
        at_e = 2 * B1 + 2 * FT * CAP
        erow = ar(at_e, 2, CH)
        srow = ar(at_e + 2 * CH, 2, CH)
        ye = ar(at_e + 4 * CH, D)
        dcT = ar(at_e + 4 * CH + D, N)
        dsel = ar(at_e + 4 * CH + D + N, 3, CAP)
        dw = ar(at_e + 4 * CH + D + N + 3 * CAP, 3, CAP)
        iota = ar(at_e + 4 * CH + D + N + 6 * CAP, PASSES * CAP)

        def col(l, name, i=0, w=None):
            at, width = COLS[name]
            return cols[:, l, at + i:at + i + (width - i if w is None else w)]

        full = [sem(f"full{b}") for b in range(8)]
        free = [sem(f"free{b}") for b in range(8)]
        group, order, reads = {}, [], [0] * 8
        ROT = 7

        def open_bank(pe, name, readers=1):
            b = len(order) % ROT
            if reads[b]:
                pe.wait_ge(free[b], reads[b])
            reads[b] += readers
            group[name] = (b, len(order) // ROT + 1, reads[b])
            order.append(name)
            return bank[b]

        def filled(eng, name):
            b, n, _ = group[name]
            eng.wait_ge(full[b], n)
            return bank[b]

        def gives(ins, name):
            ins.then_inc(free[group[name][0]], 1)

        def taken(eng, name):
            b, _, n = group[name]
            eng.wait_ge(free[b], n)

        landed = [sem(f"landed{r}") for r in range(RING)]
        used = sem("slots_used")

        class Stream:
            pos, blk, owed = 0, 0, False

        stream = Stream()

        def weights(pe):
            r = stream.pos % RING
            if stream.blk == 0:
                pe.wait_ge(landed[r], 16 * (stream.pos // RING + 1))
            b = stream.blk
            stream.blk += 1
            if stream.blk == SLOT:
                stream.pos, stream.blk = stream.pos + 1, 0
            return ring[:, r, b * P:(b + 1) * P]

        def mm(pe, out, rhs, start, stop):
            first = stream.blk == 0
            w = weights(pe)
            ins = pe.matmul(out, w, rhs, start=start, stop=stop)
            if first and stream.owed:
                ins.then_inc(used, 1)
            if first:
                stream.owed = True
            return ins

        count = {}

        def then(eng, ins, name):
            count[name] = count.get(name, 0) + 1
            ins.then_inc(sem(name), 1)
            eng.wait_ge(sem(name), count[name])

        def takes(eng, ins, name):
            gives(ins, name)
            b, _, n = group[name]
            eng.wait_ge(free[b], n)

        LOADS = ("x", "c", "cols", "masks", "iota", "sel", "s5s", "conv0", "wab", "wr")
        for b in range(8):
            sem(f"full{b}")
        ld = {n: sem(f"in_{n}") for n in LOADS}
        block = ctx.enter_context(nc.Block())

        TURN = 4
        LAG = SPL - 1
        COMBINE = range(2, 6)
        DCT = 8
        GATHER = range(UP_S + 6, UP_S + 10)

        def rounds_of(eng, body):
            body.begin(0, None)
            with eng.Fori(0, NE) as e:
                body(e, e, e, None)
            body.end(NE)
            eng.wait_ge(sem("cnt_done"), 1)
            most = eng.value_load(cnt[0:1, 0:1])
            with eng.If(most > CAP):
                with eng.Fori(1, PASSES) as a:
                    body.begin(a * (NE + 1), a)
                    with eng.Fori(0, NE) as e:
                        body(a * NE + e, a * (NE + 1) + e, e, a)
                    body.end(a * (NE + 1) + NE)

        ADAS = [(0, 0)] + ADA_IN[0] + ADA_IN[1]

        def silu_after(m):
            return [c for c in range(NCH) if m == KD * (c + 1) + SPL - 1]

        def turned_after(m):
            return [c for c in range(NCH) if m == KD * (c + 1) + TURN + SPL]

        UNITS = [4, 1, 4, 2, 2] + [0] * 7 + [1] * 3 + [0] * 4 + [1, 2, 2, 3]
        assert sum(UNITS) == 3 * KD
        Y_AFTER = [6, 10, 14]

        def units(step):
            return range(sum(UNITS[:step]), sum(UNITS[:step + 1]))

        def ada_ends(l):
            n = len(ADA_IN[l])
            return [-(-ADA_S * (i + 1) // n) - 1 for i in range(n)]

        def count_rms(tag):
            return {("mix", 0): 1, ("ffn", 0): 2, ("mix", 1): 3, ("ffn", 1): 4, ("end", 0): 5}[tag]

        @block.tensor
        def _(pe):
            def rms(tag):
                ps = open_bank(pe, ("rms",) + tag)
                for k in range(KD):
                    pe.wait_ge(sem("sq_done"), KD * (count_rms(tag) - 1) + k + 1)
                    ins = pe.matmul(ps[:, 0:N], ones[:, :], xsq[:, k, :], start=k == 0, stop=k == KD - 1)
                    if tag == ("ffn", 0) and k == 0:
                        ins.then_inc(sem("spl_used"), SPL - 1)
                ins.then_inc(full[group[("rms",) + tag][0]], 1)

            def close(ins, name):
                ins.then_inc(full[group[name][0]], 1)

            def project(name, rhs, kt, readers=1):
                ps = open_bank(pe, name, readers)
                for k in range(kt):
                    ins = mm(pe, ps[:, 0:N], rhs(k), k == 0, k == kt - 1)
                close(ins, name)

            def tok_logits(name, w):
                ps = open_bank(pe, name)
                for g in range(3):
                    m = P if g < 2 else NB
                    for k in range(KD):
                        ins = pe.matmul(ps[0:m, 8 * g:8 * g + 8], hT[:, k, P * g:P * g + m], w[:, k, :],
                                        start=k == 0, stop=k == KD - 1)
                close(ins, name)

            def bu(l, j):
                ps = open_bank(pe, ("bu", l, j))
                a = 32 * (j % 4)
                for c in range(2):
                    ins = pe.matmul(ps[:, c * SEQ:(c + 1) * SEQ], bpk[a:a + 32, j // 4, c, :],
                                    uT[a:a + 32, j // 4, 0:SEQ], start=True, stop=True)
                close(ins, ("bu", l, j))

            def batch4(name, fn, readers=1):
                ps = open_bank(pe, name, readers)
                for h in range(NH):
                    ins = fn(ps[:, h * P:(h + 1) * P], h)
                close(ins, name)

            def one(a, b):
                return lambda o, h: pe.matmul(o, a(h), b(h), start=True, stop=True)

            rounds = {"n": 0, "slots": 0}

            def ada_slots(n):
                for _ in range(n):
                    at = rounds["slots"] % ADA_S
                    if at == 0 and rounds["n"]:
                        pe.wait_ge(sem("ada_copied"), rounds["n"])
                    first = True
                    for jj in range(2):
                        j = 2 * (at % 2) + jj
                        w = [weights(pe) for _ in range(4)][0]
                        i = (stream.pos if stream.blk else stream.pos - 1) % RING
                        ins = pe.matmul(bank[7][32 * j:32 * j + 32, :], cT[:, at // 2, :],
                                        ring[:, i, 512 * jj:512 * jj + 512], start=at // 2 == 0, stop=at // 2 == KD - 1,
                                        tile_position=(0, 32 * j))
                        if first and stream.owed:
                            ins.then_inc(used, 1)
                        first, stream.owed = False, True
                    rounds["slots"] += 1
                    if at == ADA_S - 1:
                        ins.then_inc(sem("ada_full"), 1)
                        rounds["n"] += 1

            def ada_turn(l, rd):
                pe.wait_ge(sem("ada_copied"), rounds["n"])
                name = ("adt", l, rd)
                ps = open_bank(pe, name)
                for t in range(4):
                    ins = pe.transpose(ps[:, t * P:(t + 1) * P], adas[:, t * P:(t + 1) * P], ident)
                close(ins, name)

            def mixer(l):
                if l == 0:
                    pe.wait_ge(sem("cs_done"), 1)
                    ada_slots(ADA_S)
                    pe.wait_ge(ld["masks"], 16)
                    pe.wait_ge(sem("ones_done"), 1)
                    ada_turn(0, 0)
                rms(("mix", l))
                pe.wait_ge(sem("h_smp"), 2 * l + 1)

                def h_tile(k):
                    pe.wait_ge(sem("h_act"), KD * 2 * l + k + 1)
                    return hT[:, k, :]

                project(("in", l, 0), h_tile, KD)
                for m in range(1, UT):
                    project(("in", l, m), lambda k: hT[:, k, :], KD)
                if l == 0:
                    pe.wait_ge(ld["wab"], 16)
                tok_logits(("ab", l), wab[:, l])
                pe.wait_ge(sem("b_in"), 16 * (l + 1))
                for m in range(UT):
                    taken(pe, ("in", l, m))
                ps = open_bank(pe, ("bus", l))
                for a in range(4):
                    if a:
                        pe.wait_ge(sem("bus_rows"), 3 * l + a)
                    for j in range(a, JT, 4):
                        for c in range(2):
                            o = NB * (2 * j + c)
                            ins = pe.matmul(ps[:, o:o + NB], bpk[32 * a:32 * a + 32, j // 4, c, :],
                                            uT[32 * a:32 * a + 32, j // 4, SEQ:N], start=True, stop=True)
                    if a < 3:
                        ins.then_inc(sem("bus_rows"), 1)
                close(ins, ("bus", l))
                ends = ada_ends(l)
                for j in range(S5_STEPS):
                    project(("in", l, UT + j), lambda k: hT[:, k, :], KD)
                    bu(l, j)
                    ada_slots(len(ends))
                    if j - 1 in ends:
                        ada_turn(*ADA_IN[l][ends.index(j - 1)])
                    if j in Y_AFTER:
                        s5_y(l, Y_AFTER.index(j))
                def unit(u):
                    if u < 2 * KD:
                        project(("in", l, UT + S5_STEPS + u), lambda k: hT[:, k, :], KD)
                    else:
                        m = u - 2 * KD
                        if m == 0:
                            pe.wait_ge(sem("gelu_done"), UT * (l + 1))
                        for half in range(2):
                            project(("glu", l, 2 * m + half), lambda k: uT[:, k, :], UT)

                def fill(step):
                    for u in units(step):
                        unit(u)

                ada_turn(*ADA_IN[l][-1])
                fill(0)
                s5_y(l, UT - 1)
                pe.wait_ge(sem("qk_sq"), l + 1)
                for i in range(2 * NH):
                    ps = open_bank(pe, ("qkn", l, i))
                    close(pe.matmul(ps[:, 0:N], ones[:, :], sq[:, i, :], start=True, stop=True), ("qkn", l, i))
                fill(1)
                gdn(l, fill)
                gdn_samples(l, fill)
                pe.wait_ge(sem("o_sq"), l + 1)
                for h in range(NH):
                    ps = open_bank(pe, ("on", l, h))
                    close(pe.matmul(ps[:, 0:N], ones[:, :], osq[:, h, :], start=True, stop=True), ("on", l, h))
                fill(22)
                pe.wait_ge(sem("o_done"), l + 1)
                for m in range(KD):
                    project(("go", l, m), lambda k: oT[:, k, :], NH)

                def merged_tile(k):
                    pe.wait_ge(sem("merged"), KD * l + k + 1)
                    return hT[:, k, :]

                project(("wo", l, 0), merged_tile, KD)
                for m in range(1, KD):
                    project(("wo", l, m), lambda k: hT[:, k, :], KD)
                stream.owed = False

            def s5_y(l, i):
                pe.wait_ge(sem("s_back"), JT * l + 4 * i + 4)
                pe.wait_ge(sem("s_smp"), l + 1)
                ps = open_bank(pe, ("y", l, i))
                for jj in range(4):
                    j = 4 * i + jj
                    o = ps[32 * jj:32 * jj + 32, :]
                    for c in range(2):
                        pe.matmul(o[:, 0:SEQ], ckk[:, j, c, :], st[:, j % 8, c, :], start=c == 0, stop=c == 1)
                    for c in range(2):
                        ins = pe.matmul(o[:, SEQ:N], cpk[:, j, c, :], s5s[:, l, j, c, :], start=c == 0, stop=c == 1)
                close(ins, ("y", l, i))

            def gdn(l, fill):
                def q(c):
                    return lambda h: cv[:, h, P * c:P * c + P]

                def k(c):
                    return lambda h: cv[:, NH + h, P * c:P * c + P]

                pe.wait_ge(sem("g_done"), l + 1)
                name = ("gcc", l)
                ps = open_bank(pe, name)
                close(pe.matmul(ps[:, 0:8], upper, gd[:, 0, 0:8], start=True, stop=True), name)
                for c in range(NC):
                    batch4(("gcb", l, c), one(lambda h: gd[:, 0, 4 * c + h:4 * c + h + 1].broadcast_to([P, P]),
                                              lambda h: upper))
                fill(2)
                pe.wait_ge(sem("qk_done"), l + 1)
                for c in range(NC):
                    batch4(("ktok", l, c), lambda o, h: pe.transpose(o, k(c)(h), ident))
                for c in range(NC):
                    batch4(("kk", l, c), one(k(c), k(c)))
                    batch4(("qk", l, c), one(k(c), q(c)))
                fill(3)
                for c in range(NC):
                    pe.wait_ge(sem("ln_done"), NC * l + c + 1)
                    batch4(("lt", l, c), lambda o, h: pe.transpose(o, mats["ln"][c][:, h, :], ident))
                    batch4(("vtok", l, c), lambda o, h: pe.transpose(o, cv[:, 2 * NH + h, P * c:P * c + P], ident))
                at = lambda n, c: (lambda h: mats[n][c][:, h, :])
                fill(4)
                for s in range(3):
                    for c in range(NC):
                        if s == 0:
                            pe.wait_ge(sem("e_done"), NC * l + c + 1)
                        else:
                            taken(pe, ("e", l, s - 1, c))
                            taken(pe, ("eT", l, s - 1, c))
                        batch4(("e", l, s, c), one(at("eT", c), at("e", c)))
                        batch4(("eT", l, s, c), one(at("e", c), at("eT", c)))
                    fill(5 + 2 * s)
                    for c in range(NC):
                        taken(pe, ("e", l, s, c))
                        taken(pe, ("eT", l, s, c))
                        if s:
                            taken(pe, ("pT", l, s - 1, c))
                        batch4(("p", l, s, c), one(at("eT", c), at("p", c)))
                        batch4(("pT", l, s, c), one(at("e", c), at("pT", c)))
                    fill(6 + 2 * s)
                for s in range(3):
                    for c in range(NC):
                        taken(pe, ("pT", l, 2, c) if s == 0 else ("xT", l, s - 1, c))
                        pe.wait_ge(sem("lev_done"), NC * (3 * l + s) + c + 1)
                        batch4(("yl", l, s, c), one(at("eT", c), at("p", c)))
                    fill(11 + 2 * s)
                    for c in range(NC):
                        taken(pe, ("yl", l, s, c))
                        if s < 2:
                            batch4(("x", l, s, c), one(at("pT", c), at("y", c)))
                        batch4(("xT", l, s, c), one(at("y", c), at("pT", c)))
                    fill(12 + 2 * s)
                for c in range(NC):
                    taken(pe, ("xT", l, 2, c))
                    taken(pe, ("ktok", l, c))
                    batch4(("wt", l, c), one(at("kbg", c), at("pT", c)))
                fill(17)
                for c in range(NC):
                    taken(pe, ("vtok", l, c))
                    if c:
                        taken(pe, ("wt", l, c))
                        taken(pe, ("s", l, c - 1))
                    name = ("vn", l, c)
                    ps = open_bank(pe, name)
                    for h in range(NH):
                        o = ps[:, h * P:(h + 1) * P]
                        ins = pe.matmul(o, mats["pT"][c][:, h, :], mats["vb"][c][:, h, :], start=True, stop=c == 0)
                        if c:
                            ins = pe.matmul(o, mats["nwT"][c][:, h, :], s_pr[:, h, :], start=False, stop=True)
                    close(ins, name)
                    fill(18 + c)
                    taken(pe, name)
                    taken(pe, ("qk", l, c))
                    pe.wait_ge(sem("qg_done"), NC * l + c + 1)
                    name = ("o", l, c)
                    ps = open_bank(pe, name)
                    for h in range(NH):
                        o = ps[:, h * P:(h + 1) * P]
                        ins = pe.matmul(o, mats["vn"][c][:, h, :], mats["att"][c][:, h, :], start=True, stop=c == 0)
                        if c:
                            ins = pe.matmul(o, s_pr[:, h, :], mats["qg"][c][:, h, :], start=False, stop=True)
                    close(ins, name)
                    batch4(("s", l, c), one(at("kg", c), at("vn", c)))

            def gdn_samples(l, fill):
                hb = NH * NB
                pe.wait_ge(sem("qkp_done"), l + 1)
                name = ("skt", l)
                ps = open_bank(pe, name)
                close(pe.transpose(ps[0:hb, 0:P], sx[:, 2, 0:hb], ident), name)
                pe.wait_ge(sem("dg_done"), l + 1)
                name = ("sgb", l)
                ps = open_bank(pe, name)
                close(pe.matmul(ps[:, 0:2 * hb], ones[0:NB, :], dg[:, :, :, :].rearrange("p a h b -> p (a h b)"),
                                start=True, stop=True), name)
                name = ("sqk", l)
                ps = open_bank(pe, name)
                close(pe.matmul(ps[:, 0:hb], ones[:, :], sx[:, 0, 0:hb], start=True, stop=True), name)
                fill(20)
                pe.wait_ge(sem("s0_in"), 16 * (l + 1))
                name = ("skq", l)
                ps = open_bank(pe, name)
                for h in range(NH):
                    for b in range(NB):
                        i = h * NB + b
                        ins = pe.matmul(ps[:, 2 * i:2 * i + 2], s0[:, i, :], cv[:, h:h + NH + 1:NH, SEQ + b],
                                        start=True, stop=True)
                close(ins, name)
                pe.wait_ge(sem("svn_done"), l + 1)
                name = ("svt", l)
                ps = open_bank(pe, name)
                close(pe.transpose(ps[0:hb, 0:P], sx[:, 1, 0:hb], ident), name)
                fill(21)
                pe.wait_ge(sem("vm_done"), l + 1)
                for i in range(NB):
                    name = ("so", l, i)
                    ps = open_bank(pe, name)
                    close(pe.matmul(ps[:, :], ktk[:, :], vm[0:hb, 4 * i:4 * i + 4, :].rearrange("p a b -> p (a b)"),
                                    start=True, stop=True), name)

            def drained():
                for b in range(8):
                    if reads[b]:
                        pe.wait_ge(free[b], reads[b])

            def split_product(o, part, xh, xl, first, last, begins):
                wh, wl = part(whi), part(wlo)
                for n, (w, x) in enumerate(((wh, xh), (wl, xh), (wh, xl))):
                    ins = pe.matmul(o, w, x, start=first and n == 0, stop=last and n == 2)
                    if begins and n == 0:
                        ins.then_inc(sem("spl_used"), 1)
                return ins

            def dense():
                drained()
                BODY = 4 * RING
                with pe.Fori(0, UP_S // BODY) as it:
                    for s in range(BODY):
                        f, half = s // 2, s % 2
                        pe.wait_ge(sem("lo_done"), it * BODY + (s + 1))
                        if half == 0:
                            pe.wait_ge(sem("act_done"), it * (BODY // 2) + f if f >= 2 else it * (BODY // 2 - 1 + f) + 1)
                        for k in range(KD):
                            if s == 0 and k % 4 == 0:
                                pe.wait_ge(sem("hl_done"), k // 4 + 1)
                            ins = split_product(bank[2 * (f % 2) + half][:, 0:N],
                                                lambda t: t[:, s % SPL, k * P:(k + 1) * P], hh[:, k, :], hl[:, k, :],
                                                k == 0, k == KD - 1, k == 0)
                        if half:
                            ins.then_inc(sem("up_full"), 1)
                for m in range(KD):
                    if m >= 2:
                        pe.wait_ge(sem("down_taken"), m - 1)
                    for k in range(FT):
                        b = m * FT + k
                        s, i = UP_S + b // SLOT, b % SLOT
                        if i == 0:
                            pe.wait_ge(sem("lo_done"), s + 1)
                        if m == 0 and k % 2 == 0:
                            pe.wait_ge(sem("al_done"), k + 2)
                        ins = split_product(bank[4 + m % 2][:, 0:N], lambda t: t[:, s % SPL, i * P:(i + 1) * P],
                                            ahi[:, k, :], alo[:, k, :], k == 0, k == FT - 1, i == 0)
                    ins.then_inc(sem("down_full"), 1)
                pe.wait_ge(sem("down_taken"), KD)
                stream.pos += FFN_S

            def experts_setup():
                pe.wait_ge(ld["wr"], 16)
                pe.wait_ge(sem("h_act"), 4 * KD)
                pe.wait_ge(sem("h_smp"), 4)
                tok_logits(("rl",), wr)
                for g in range(3):
                    m = P if g < 2 else NB
                    for half in range(2):
                        name = ("ht", g, half)
                        ps = open_bank(pe, name)
                        for k in range(4):
                            ins = pe.transpose(ps[0:m, k * P:(k + 1) * P], hT[:, 4 * half + k, P * g:P * g + m], ident)
                        close(ins, name)
                pe.wait_ge(sem("sel_done"), 1)
                ps = open_bank(pe, ("rank",))
                for g in range(4):
                    m = P if g != 2 else NB
                    o = ps[0:m, 8 * g:8 * g + 8]
                    for a in range(min(g, 3)):
                        ka = P if a < 2 else NB
                        ins = pe.matmul(o, ones[0:ka, 0:m], rt[0:ka, a, :], start=a == 0, stop=g == 3 and a == 2)
                    if g < 3:
                        ins = pe.matmul(o, upper[0:m, 0:m], rt[0:m, g, :], start=g == 0, stop=True)
                close(ins, ("rank",))
                drained()

            class Experts:

                def gather(self, m, g):
                    if m == 0:
                        pe.wait_ge(sem("dsel_done"), g * 1 + 1)
                    for t in range(3):
                        kk = P if t < 2 else NB
                        ins = pe.matmul(bank[m // 4][:, CAP * (m % 4):CAP * (m % 4) + CAP],
                                        htok[0:kk, t, m * P:(m + 1) * P], dsel[0:kk, t, :], start=t == 0, stop=t == 2)
                    if m % 4 == 3:
                        ins.then_inc(sem("gather_full"), 1)

                def combine(self, m, g):
                    if m == 0:
                        pe.wait_ge(sem("ye_done"), g * 2 + 2)
                    pe.wait_ge(sem("down_taken"), g * KD + (KD + m - 1))
                    pe.matmul(bank[4 + m % 2][:, 0:N], ye[0:CAP, m * P:(m + 1) * P], dcT[0:CAP, :],
                              start=True, stop=True).then_inc(sem("down_full"), 1)

                def begin(self, g, a):
                    for m in range(KD):
                        self.gather(m, g)

                def end(self, g):
                    for m in range(KD):
                        self.combine(m, g)

                def __call__(self, q, g, e, a):
                    expert(self, q, g)

            def expert(self, q, g):
                base = FFN_S
                pe.wait_ge(sem("gl_done"), g * 2 + 2)

                def turn(c):
                    pe.wait_ge(sem("act_done"), q * NCH + (FT + 1 + c + 1))
                    if c == 0:
                        pe.wait_ge(sem("dcT_done"), q * 1 + 1)
                    if c >= 2:
                        pe.wait_ge(sem("turned_done"), q * NCH + (c - 1))
                    for t in range(CH // P):
                        ins = pe.transpose(bank[4 + c % 2][:, CAP * t:CAP * t + CAP], erow[0:CAP, c % 2, t * P:(t + 1) * P],
                                           ident[0:CAP, 0:CAP])
                    ins.then_inc(sem("turned_full"), 1)

                for s in range(UP_S):
                    c, k = s // KD, s % KD
                    pe.wait_ge(sem("lo_done"), q * FFN_S + (base + s + 1))
                    if k == 0 and c >= 2:
                        pe.wait_ge(sem("act_done"), q * NCH + (FT + 1 + c - 1))
                    w = [t[:, s % SPL, :] for t in (whi, wlo)]
                    o = [bank[2 * (c % 2) + half][0:CAP, :] for half in range(2)]
                    for n, (x, part) in enumerate(((gh, 0), (gh, 1), (gl, 0))):
                        for half in range(2):
                            ins = pe.matmul(o[half], x[:, k, :], w[part][:, CH * half:CH * half + CH],
                                            start=k == 0 and n == 0, stop=k == KD - 1 and n == 2)
                            if n == 0 and half == 0:
                                ins.then_inc(sem("spl_used"), 1)
                    if k == KD - 1:
                        ins.then_inc(sem("up_full"), 1)
                    if k == TURN and c:
                        turn(c - 1)
                    if s in COMBINE:
                        for m in range(2):
                            self.combine(2 * (s - COMBINE[0]) + m, g)
                    if s == DCT:
                        pe.wait_ge(sem("down_taken"), g * KD + 2 * KD)
                        for t in range(3):
                            m = P if t < 2 else NB
                            ins = pe.transpose(bank[4][0:CAP, P * t:P * t + m], dw[0:m, t, :], ident[0:m, 0:m])
                        ins.then_inc(sem("dcT_full"), 1)
                for s in range(DOWN_S):
                    m = UP_S + s
                    pe.wait_ge(sem("lo_done"), q * FFN_S + (base + m + 1))
                    if s % (CH // P) == 0:
                        pe.wait_ge(sem("turned_done"), q * NCH + (s // (CH // P) + 1))
                    w = [t[:, m % SPL, :] for t in (whi, wlo)]
                    for n, (x, part) in enumerate(((eh, 0), (eh, 1), (el, 0))):
                        for half in range(2):
                            ins = pe.matmul(bank[6 + half][0:CAP, :], x[:, s, :], w[part][:, CH * half:CH * half + CH],
                                            start=s == 0 and n == 0, stop=s == FT - 1 and n == 2)
                            if n == 0 and half == 0:
                                ins.then_inc(sem("spl_used"), 1)
                            if s == FT - 1 and n == 2:
                                ins.then_inc(sem("ye_full"), 1)
                    if s == TURN:
                        turn(NCH - 1)
                    if UP_S + s in GATHER:
                        for m in range(2):
                            self.gather(2 * (UP_S + s - GATHER[0]) + m, g + 1)

            mixer(0)
            rms(("ffn", 0))
            dense()
            mixer(1)
            rms(("ffn", 1))
            experts_setup()
            rounds_of(pe, Experts())
            for k in range(KD):
                pe.wait_ge(sem("sq_done"), KD * (count_rms(("end", 0)) - 1) + k + 1)
                ins = pe.matmul(bank[0][:, 0:N], ones[:, :], xsq[:, k, :], start=k == 0, stop=k == KD - 1)
            ins.then_inc(sem("end_full"), 1)


        @block.sync
        def _(sp):
            def segment(n0, n1, before, gone, each):
                def load(n, at=None):
                    sp.dma_start(ring[:, n % RING, :], w_in[n if at is None else at]).then_inc(landed[n % RING], 16)

                for n in range(n0, n0 + RING):
                    before(n - RING)
                    load(n)
                whole = (n1 - n0 - RING) // RING
                with sp.Fori(0, whole) as i:
                    for r in range(RING):
                        sp.wait_ge(sem(gone), i * RING + (each + r + 1))
                        load(n0 + RING + r, i * RING + (n0 + RING + r))
                for n in range(n0 + RING * (whole + 1), n1):
                    sp.wait_ge(sem(gone), each + n - n0 - RING + 1)
                    load(n)

            def mixer_slot(l, n0, n1):
                def wait(n):
                    if n == n1 - 1:
                        filled(sp, ("wo", l, KD - 1))
                    else:
                        sp.wait_ge(used, (MIX0_END - 1) * l + n - n0 + 1)
                return wait

            segment(0, MIX0_END, lambda n: None, "slots_used", 0)
            segment(MIX0_END, FFN0_END, mixer_slot(0, 0, MIX0_END), "lo_done", 0)
            segment(FFN0_END, MIX1_END, lambda n: sp.wait_ge(sem("lo_done"), n - MIX0_END + 1), "slots_used", MIX0_END - 1)
            m1 = mixer_slot(1, FFN0_END, MIX1_END)
            for n in range(MIX1_END, MIX1_END + RING):
                m1(n - RING)
                sp.dma_start(ring[:, n % RING, :], w_in[n]).then_inc(landed[n % RING], 16)

            def expert_weights(q, e, s0, s1):
                for s in range(s0, s1):
                    sp.wait_ge(sem("lo_done"), q * FFN_S + (FFN_S + s - RING + 1))
                    r = (MIX1_END + s) % RING
                    sp.dma_start(ring[:, r, :], w_in[e * FFN_S + (MIX1_END + s)]).then_inc(landed[r], 16)

            expert_weights(0, 0, RING, FFN_S)
            with sp.Fori(1, NE) as e:
                expert_weights(e, e, 0, FFN_S)
            sp.wait_ge(sem("cnt_done"), 1)
            most = sp.value_load(cnt[0:1, 0:1])
            with sp.If(most > CAP):
                with sp.Fori(1, PASSES) as a:
                    with sp.Fori(0, NE) as e:
                        expert_weights(a * NE + e, e, 0, FFN_S)
            sp.wait_ge(sem("y_done"), KD)
            sp.dma_start(y_out, hT[:, :, :]).then_inc(sem("y_out"), 16)
            sp.wait_ge(sem("y_out"), 16)

        @block.scalar
        def _(act):
            act.wait_ge(sem("c_zero"), 1)
            act.dma_start(cT[:, :, 0:1 + NB], c_in).then_inc(ld["c"], 16)
            act.dma_start(xT[:, :, :], x_in).then_inc(ld["x"], 16)
            act.dma_start(cols[:, :, :], cols_in).then_inc(ld["cols"], 16)
            act.dma_start(masks[:, :, :], masks_in).then_inc(ld["masks"], 16)
            act.dma_start(wab[:, :, :, :], wab_in).then_inc(ld["wab"], 16)
            act.dma_start(bpk[:, :, :, :], bpk_in[0]).then_inc(sem("b_in"), 16)
            act.dma_start(cpk[:, :, :, :], cpk_in[0]).then_inc(sem("c5_in"), 16)
            act.dma_start(s5s[:, :, :, :, :], s5s_in).then_inc(ld["s5s"], 16)
            act.dma_start(conv0[:, :, :, :, :], conv_in).then_inc(ld["conv0"], 16)
            act.dma_start(selw[:, :, :], sel_in).then_inc(ld["sel"], 16)
            act.dma_start(wr[:, :, :], wr_in).then_inc(ld["wr"], 16)
            act.wait_ge(ld["c"], 16)
            act.activation(cT[:, :, :], cT[:, :, :], ACT.Silu).then_inc(sem("cs_done"), 1)
            act.wait_ge(ld["x"], 16)

            def squares(done=None, n=0):
                for k in range(KD):
                    if done:
                        act.wait_ge(sem(done), n + k + 1)
                    act.activation(xsq[:, k, :], xT[:, k, :], ACT.Square).then_inc(sem("sq_done"), 1)

            def root(n):
                act.wait_ge(sem("ss_done"), n)
                act.activation(rstd[:, :], ssb[:, :], ACT.Sqrt).then_inc(sem("root_done"), 1)

            def shift(l, at, n):
                for k in range(KD):
                    act.wait_ge(sem("h_scaled"), KD * n + k + 1)
                    act.activation(hT[:, k, 0:SEQ], hT[:, k, 0:SEQ], ACT.Identity,
                                   bias=mods[:, l, at + k, 0:1]).then_inc(sem("h_act"), 1)

            def ada_copy(n):
                act.wait_ge(sem("ada_full"), n)
                if n > 1:
                    filled(act, ("adt",) + ADAS[n - 2])
                act.activation(adas[:, :], bank[7][:, :], ACT.Copy).then_inc(sem("ada_copied"), 1)

            def unit(l, u):
                if u < 2 * KD:
                    name = ("in", l, UT + S5_STEPS + u)
                    gives(act.activation(gates[:, u, :], filled(act, name)[:, 0:N], ACT.Sigmoid), name)
                else:
                    m = u - 2 * KD
                    name = ("glu", l, 2 * m + 1)
                    ps = filled(act, name)
                    if m >= 2:
                        act.wait_ge(sem("glu_done"), KD * l + m - 1)
                    gives(act.activation(tmp[:, m % 2, :], ps[:, 0:N], ACT.Sigmoid), name)

            def mixer(l):
                def fill(step):
                    for u in units(step):
                        unit(l, u)

                squares("x_ffn" if l else None)
                if l == 0:
                    ada_copy(1)
                root(2 * l + 1)
                shift(l, 0, 2 * l)
                act.wait_ge(ld["cols"], 16)
                for m in range(UT + S5_STEPS):
                    name = ("in", l, m)
                    ps = filled(act, name)[:, 0:N]
                    if m < UT:
                        ins = act.activation(uT[:, m, :], ps, ACT.Copy)
                    elif m < UT + QT:
                        if m == UT:
                            act.wait_ge(sem("pool_zero"), l + 1)
                        ins = act.activation(raw[:, m - UT, 3:3 + N], ps, ACT.Copy)
                    else:
                        ins = act.activation(zs[:, m - UT - QT, :], ps, ACT.Silu)
                    gives(ins, name)
                    if UT <= m < UT + QT:
                        taken(act, name)
                        act.activation(cv[:, m - UT, 0:SEQ], raw[:, m - UT, 0:SEQ], ACT.Copy,
                                       scale=col(l, "conv_w", m - UT, 1)).then_inc(sem("tap_done"), 1)
                    if m >= UT and m - UT in ada_ends(l):
                        ada_copy(ADAS.index(ADA_IN[l][ada_ends(l).index(m - UT)]) + 1)
                for i in range(3):
                    act.wait_ge(sem("conv_done"), l + 1)
                    v = cv[:, NH * i:NH * i + NH, :]
                    then(act, act.activation(v, v, ACT.Silu), "cv_silu")
                for i in range(UT):
                    if i == UT - 1:
                        fill(0)
                    act.wait_ge(sem("y_sum"), UT * l + i + 1)
                    act.activation(uT[:, i, :], uT[:, i, :], ACT.Gelu_apprx_tanh).then_inc(sem("gelu_done"), 1)
                act.activation(sq, cv[:, 0:2 * NH, :], ACT.Square).then_inc(sem("qk_sq"), 1)
                act.wait_ge(sem("ax_done"), l + 1)
                then(act, act.activation(gd[:, 1, :], gd[:, 1, :], ACT.Exp, scale=-1.0), "a_gd")
                act.activation(gd[:, 1, :], gd[:, 1, :], ACT.Ln, bias=1.0).then_inc(sem("a_ln"), 1)
                act.activation(gd[:, 3, 0:NH], col(l, "a_log"), ACT.Exp).then_inc(sem("a_ln"), 1)
                act.activation(gd[:, 4, :], gd[:, 4, :], ACT.Sigmoid).then_inc(sem("a_ln"), 1)
                fill(1)
                act.wait_ge(sem("nrm_ss"), l + 1)
                act.activation(nrm[:, :, :], nrm[:, :, :], ACT.Sqrt).then_inc(sem("nrm_root"), 1)
                fill(2)
                act.wait_ge(sem("gdx_done"), l + 1)
                act.activation(gd[:, 7:10, 0:8], gd[:, 7:10, 0:8], ACT.Exp).then_inc(sem("a_col"), 1)
                act.activation(gd[:, 11, 8:12], gd[:, 0, 8:12], ACT.Exp).then_inc(sem("a_col"), 1)
                for c in range(NC):
                    name = ("gcb", l, c)
                    act.wait_ge(sem("diff_done"), NC * l + c + 1)
                    act.activation(mats["decT"][c], mats["decT"][c], ACT.Exp).then_inc(sem("a_dec"), 1)
                    act.activation(mats["dec"][c], mats["dec"][c], ACT.Exp).then_inc(sem("a_dec"), 1)
                    ps = filled(act, name)
                    gives(act.activation(mats["qg"][c], ps[:, :].rearrange("p (h t) -> p h t", h=NH), ACT.Exp), name)
                fill(3)
                fill(4)
                for s in range(3):
                    if s:
                        fill(4 + 2 * s)
                    for c in range(NC):
                        for n in ("e", "eT"):
                            name = (n, l, s, c)
                            filled(act, ("eT", l, s, c))
                            ps = filled(act, name)
                            gives(act.activation(mats[n][c], ps[:, :].rearrange("p (h t) -> p h t", h=NH), ACT.Copy), name)
                    fill(5 + 2 * s)
                for s in range(3):
                    fill(10 + 2 * s)
                    for c in range(NC):
                        name = ("yl", l, s, c)
                        ps = filled(act, name)
                        gives(act.activation(mats["y"][c], ps[:, :].rearrange("p (h t) -> p h t", h=NH), ACT.Copy), name)
                    fill(11 + 2 * s)
                fill(16)
                for c in range(NC):
                    name = ("wt", l, c)
                    ps = filled(act, name)
                    gives(act.activation(mats["nwT"][c], ps[:, :].rearrange("p (h t) -> p h t", h=NH), ACT.Copy,
                                         scale=-1.0), name)
                fill(17)
                for c in range(NC):
                    name = ("vn", l, c)
                    ps = filled(act, name)
                    gives(act.activation(mats["vn"][c], ps[:, :].rearrange("p (h t) -> p h t", h=NH), ACT.Copy), name)
                    fill(18 + c)
                    name = ("o", l, c)
                    ps = filled(act, name)
                    gives(act.activation(oT[:, :, P * c:P * c + P], ps[:, :].rearrange("p (h t) -> p h t", h=NH),
                                         ACT.Copy), name)
                act.wait_ge(sem("sp_out"), 16 * (l + 1))
                filled(act, ("s", l, NC - 1))
                act.dma_start(s0, gdn_in[l]).then_inc(sem("s0_in"), 16)
                fill(20)
                fill(21)
                act.wait_ge(sem("os_done"), l + 1)
                taken(act, ("o", l, NC - 1))
                act.activation(osq, oT, ACT.Square).then_inc(sem("o_sq"), 1)
                act.wait_ge(sem("on_ss"), l + 1)
                act.activation(onrm, onrm, ACT.Sqrt).then_inc(sem("on_root"), 1)
                fill(22)

            mixer(0)
            def high(r, land, m, count):
                act.wait_ge(landed[r], land)
                act.wait_ge(sem("spl_used"), count)
                act.activation(whi[:, m % SPL, :], ring[:, r, :], ACT.Copy).then_inc(sem("hi_done"), 1)

            squares("x_mix")
            act.wait_ge(sem("gs_out"), 16)
            for s in range(LAG):
                n = MIX0_END + s
                high(n % RING, 16 * (n // RING + 1), s, s + 1)
            root(2)
            shift(0, 24, 1)
            act.wait_ge(sem("h_smp"), 2)
            for half in range(2):
                i = slice(4 * half, 4 * half + 4)
                act.wait_ge(sem("h_act"), KD + 4 * (half + 1))
                act.activation(hh[:, i, :], hT[:, i, :], ACT.Copy).then_inc(sem("hh_done"), 1)
            filled(act, ("y", 0, UT - 1))
            act.dma_start(bpk[:, :, :, :], bpk_in[1]).then_inc(sem("b_in"), 16)
            act.dma_start(cpk[:, :, :, :], cpk_in[1]).then_inc(sem("c5_in"), 16)
            BODY = 4 * RING

            def dense_tile(it, f):
                act.wait_ge(sem("up_full"), it * (BODY // 2) + (f + 1))
                act.wait_ge(sem("act_done"), it * (BODY // 2) + (f + 1))
                act.activation(sg[:, f % 2, :], bank[2 * (f % 2)][:, 0:N], ACT.Silu).then_inc(sem("silu_done"), 1)
                act.wait_ge(sem("act_done"), it * (BODY // 2) + (f + 2))
                act.activation(ahi[:, bass.ds(it * (BODY // 2) + f, 1), :], sg[:, f % 2:f % 2 + 1, :],
                               ACT.Copy).then_inc(sem("ah_done"), 1)

            with act.Fori(0, UP_S // BODY) as it:
                for s in range(BODY):
                    n = MIX0_END + s + LAG
                    high(n % RING, it * (16 * BODY // RING) + 16 * (n // RING + 1), s + LAG, it * BODY + (s + LAG + 1))
                    if s >= 2 and s % 2 == 0:
                        dense_tile(it, s // 2 - 1)
                dense_tile(it, BODY // 2 - 1)
            for s in range(UP_S + LAG, FFN_S):
                n = MIX0_END + s
                high(n % RING, 16 * (n // RING + 1), s, s + 1)
            mixer(1)
            squares("x_mix", KD)
            act.wait_ge(sem("gs_out"), 32)
            act.dma_start(iota, iota_in).then_inc(ld["iota"], 16)
            root(4)
            shift(1, 24, 3)
            for g in range(3):
                m = P if g < 2 else NB
                for half in range(2):
                    name = ("ht", g, half)
                    ps = filled(act, name)
                    gives(act.activation(htok[0:m, g, 512 * half:512 * half + 512], ps[0:m, :], ACT.Copy), name)
            act.wait_ge(sem("sel_done"), 1)
            act.activation(rtx[:, 6:9, :], rtx[:, 6:9, :], ACT.Exp).then_inc(sem("rexp_done"), 1)

            class Experts:
                def gathered(self, half, g):
                    act.wait_ge(sem("gather_full"), g * 2 + (half + 1))
                    act.activation(gh[:, 4 * half:4 * half + 4, :],
                                   bank[half][:, 0:4 * CAP].rearrange("p (a b) -> p a b", b=CAP),
                                   ACT.Copy).then_inc(sem("gh_done"), 1)

                def rows(self, g):
                    for half in range(2):
                        act.wait_ge(sem("ye_full"), g * 2 + (half + 1))
                        act.activation(ye[0:CAP, 512 * half:512 * half + 512], bank[6 + half][0:CAP, :],
                                       ACT.Copy).then_inc(sem("ye_done"), 1)

                def begin(self, g, a):
                    self.gathered(0, g)
                    self.gathered(1, g)

                def end(self, g):
                    self.rows(g)

                def __call__(self, q, g, e, a):
                    expert(self, q, g)

            def expert(self, q, g):
                for m in range(FFN_S):
                    n = MIX1_END + m
                    high(n % RING, q * (16 * FFN_S // RING) + 16 * (n // RING + 1), m, q * FFN_S + (FFN_S + m + 1))
                    for c in silu_after(m):
                        act.wait_ge(sem("up_full"), q * NCH + (FT + c + 1))
                        act.wait_ge(sem("act_done"), q * NCH + (FT + 1 + c - 1))
                        act.activation(srow[0:CAP, c % 2, :], bank[2 * (c % 2)][0:CAP, :],
                                       ACT.Silu).then_inc(sem("silu_done"), 1)
                    for c in turned_after(m):
                        act.wait_ge(sem("turned_full"), q * NCH + (c + 1))
                        act.activation(eh[:, 4 * c:4 * c + 4, :],
                                       bank[4 + c % 2][:, 0:4 * CAP].rearrange("p (a b) -> p a b", b=CAP),
                                       ACT.Copy).then_inc(sem("eh_done"), 1)
                    if m == COMBINE[0]:
                        self.rows(g)
                    if m == DCT + LAG:
                        act.wait_ge(sem("dcT_full"), q * 1 + 1)
                        act.activation(dcT[0:CAP, :], bank[4][0:CAP, 0:N], ACT.Copy).then_inc(sem("dcT_done"), 1)
                    if m - LAG in GATHER and (m - LAG - GATHER[0]) % 2:
                        self.gathered((m - LAG - GATHER[0]) // 2, g + 1)

            rounds_of(act, Experts())
            squares("x_ffn", KD)
            root(5)

        @block.vector
        def _(v):
            def d(ins):
                then(v, ins, "v")

            def bc(ap, shape):
                return ap.broadcast_to(shape)

            def mean_root(ps, n, width):
                return v.tensor_scalar(ssb[:, :], ps[:, 0:N], 1.0 / width, EPS, ALU.mult, ALU.add)

            state = {"norms": 0}

            def norm(l, which, g, at):
                n = state["norms"]
                state["norms"] += 1
                mod = mods[:, l]
                d(v.scalar_tensor_tensor(mod[:, at + 8:at + 16, :], mod[:, at + 8:at + 16, :], 1.0,
                                         bc(col(l, g)[:, :, None], [P, KD, 1 + NB]), ALU.add, ALU.mult))
                name = ("rms", which, l)
                ps = filled(v, name)
                takes(v, mean_root(ps, n, D), name)
                v.tensor_copy(ini[:, 3:4], ssb[:, 0:1]).then_inc(sem("ss_done"), 1)
                v.wait_ge(sem("root_done"), n + 1)
                d(v.reciprocal(rstd[:, :], rstd[:, :]))
                hs = hT[:, :, SEQ:N]
                d(v.tensor_tensor(hs, xT[:, :, SEQ:N], bc(rstd[:, None, SEQ:N], [P, KD, NB]), ALU.mult))
                d(v.tensor_tensor(hs, hs, mod[:, at + 8:at + 16, 1:1 + NB], ALU.mult))
                v.tensor_tensor(hs, hs, mod[:, at:at + 8, 1:1 + NB], ALU.add).then_inc(sem("h_smp"), 1)
                for k in range(KD):
                    v.scalar_tensor_tensor(hT[:, k, 0:SEQ], xT[:, k, 0:SEQ], mod[:, at + 8 + k, 0:1], rstd[:, 0:SEQ],
                                           ALU.mult, ALU.mult).then_inc(sem("h_scaled"), 1)

            def c_(i):
                return sm[:, i, :]

            def tt(o, a, b, op):
                d(v.tensor_tensor(o, a, b, op))

            def ts(o, a, s1, s2, op0, op1=ALU.bypass):
                if s2 is None:
                    d(v.tensor_scalar(o, a, s1, None, op0))
                else:
                    d(v.tensor_scalar(o, a, s1, s2, op0, op1))

            MAGIC = 12582912.0

            def exp_to(o, x, k, r):
                ts(k, x, 1.4426950408889634, None, ALU.mult)
                ts(k, k, 126.0, -126.0, ALU.min, ALU.max)
                ts(k, k, MAGIC, None, ALU.add)
                ts(k, k, -MAGIC, None, ALU.add)
                d(v.scalar_tensor_tensor(r, k, -0.693359375, x, ALU.mult, ALU.add))
                d(v.scalar_tensor_tensor(r, k, 2.12194440e-4, r, ALU.mult, ALU.add))
                ts(o, r, 1.0 / 5040, 1.0 / 720, ALU.mult, ALU.add)
                for a in (1 / 120, 1 / 24, 1 / 6, 0.5, 1.0, 1.0):
                    tt(o, o, r, ALU.mult)
                    ts(o, o, a, None, ALU.add)
                ts(k, k, 127.0, None, ALU.add)
                d(v.tensor_copy(smi[:, :], k))
                d(v.tensor_single_scalar(smi[:, :], smi[:, :], 23, ALU.logical_shift_left))
                tt(o, o, smi[:, :].bitcast(F32), ALU.mult)

            def ada_mod(l, rd):
                name = ("adt", l, rd)
                ps = filled(v, name)[:, :].rearrange("p (t j x) -> p j t x", t=4, j=4)[:, :, :, 0:1 + NB]
                o = mods[:, l, 16 * rd:16 * rd + 16, :].rearrange("p (j t) b -> p j t b", t=4)
                b = col(l, "b_ada", 16 * rd, 16).rearrange("p (j t) -> p j t", t=4)
                takes(v, v.tensor_tensor(o, ps, bc(b[:, :, :, None], [P, 4, 4, 1 + NB]), ALU.add), name)

            dt, mag, th, k, r, co, si = (c_(i) for i in range(7))

            def s5_decay(l):
                lr, li = col(l, "lam_re"), col(l, "lam_im")
                exp_to(dt, col(l, "log_dt"), k, r)
                tt(th, lr, dt, ALU.mult)
                exp_to(mag, th, k, r)
                tt(th, li, dt, ALU.mult)

            def s5_rotation(l):
                ts(k, th, 1.0 / (2 * math.pi), None, ALU.mult)
                ts(k, k, MAGIC, None, ALU.add)
                ts(k, k, -MAGIC, None, ALU.add)
                d(v.scalar_tensor_tensor(r, k, -6.28125, th, ALU.mult, ALU.add))
                d(v.scalar_tensor_tensor(r, k, -1.9350051879882812e-3, r, ALU.mult, ALU.add))
                d(v.scalar_tensor_tensor(r, k, -3.0199159819e-7, r, ALU.mult, ALU.add))
                x, x2, o = sm[:, 7:9, :], sm[:, 9:11, :], sm[:, 11:13, :]
                ts(c_(8), r, 0.5, None, ALU.mult)
                ts(c_(7), r, -0.5, None, ALU.mult)
                tt(c_(7), c_(7), c_(8), ALU.max)
                d(v.tensor_scalar(c_(7), c_(7), -1.0, math.pi / 2, ALU.mult, ALU.add))
                tt(x2, x, x, ALU.mult)
                ts(o, x2, 1.0 / 6227020800, -1.0 / 39916800, ALU.mult, ALU.add)
                for a in (1.0 / 362880, -1.0 / 5040, 1.0 / 120, -1.0 / 6, 1.0):
                    tt(o, o, x2, ALU.mult)
                    ts(o, o, a, None, ALU.add)
                tt(o, o, x, ALU.mult)
                tt(si, c_(11), c_(12), ALU.mult)
                ts(si, si, 2.0, None, ALU.mult)
                tt(co, c_(12), c_(12), ALU.mult)
                d(v.tensor_scalar(co, co, -2.0, 1.0, ALU.mult, ALU.add))
                v.tensor_copy(c_(11), co).then_inc(sem("rot_done"), 1)

            def s5_gain(l):
                lr, li = col(l, "lam_re"), col(l, "lam_im")
                ar_, ai, nr, den, kr, ki = (c_(i) for i in range(12, 18))
                tt(ar_, mag, co, ALU.mult)
                tt(ai, mag, si, ALU.mult)
                ts(nr, ar_, -1.0, None, ALU.add)
                tt(den, lr, lr, ALU.mult)
                tt(c_(18), li, li, ALU.mult)
                tt(den, den, c_(18), ALU.add)
                d(v.reciprocal(den, den))
                tt(kr, nr, lr, ALU.mult)
                tt(c_(18), ai, li, ALU.mult)
                tt(kr, kr, c_(18), ALU.add)
                tt(kr, kr, den, ALU.mult)
                tt(ki, ai, lr, ALU.mult)
                tt(c_(18), nr, li, ALU.mult)
                tt(ki, ki, c_(18), ALU.subtract)
                tt(ki, ki, den, ALU.mult)
                v.wait_ge(sem("c5_in"), 16 * (l + 1))
                W = [P, JT, 32]
                krb, kib = bc(kr[:, :, None], W), bc(ki[:, :, None], W)
                cr, ci, o, o2 = cpk[:, :, 0, :], cpk[:, :, 1, :], ckk[:, :, 0, :], ckk[:, :, 1, :]
                scr = sx[:, :, :].rearrange("p a b -> p (a b)").rearrange("p (a b) -> p a b", b=32)
                tt(o, cr, krb, ALU.mult)
                tt(scr, ci, kib, ALU.mult)
                tt(o, o, scr, ALU.subtract)
                tt(o2, cr, kib, ALU.mult)
                tt(scr, ci, krb, ALU.mult)
                tt(o2, o2, scr, ALU.add)
                ts(o2, o2, -1.0, None, ALU.mult)
                ts(ci, ci, -1.0, None, ALU.mult)

            def s5_samples(l):
                name = ("bus", l)
                ps = filled(v, name)[:, 0:2 * JT * NB].rearrange("p (j c b) -> p j c b", c=2, b=NB)
                if l == 0:
                    v.wait_ge(ld["s5s"], 16)
                W = [P, JT, NB]
                a, b, e = (sx[:, i, :].rearrange("p (j b) -> p j b", b=NB) for i in range(3))
                A = [bc(c_(i)[:, :, None], W) for i in (12, 13, 16, 17)]
                sr, si = s5s[:, l, :, 0, :], s5s[:, l, :, 1, :]
                br, bi = ps[:, :, 0, :], ps[:, :, 1, :]
                tt(a, sr, A[0], ALU.mult)
                tt(e, si, A[1], ALU.mult)
                tt(a, a, e, ALU.subtract)
                tt(e, br, A[2], ALU.mult)
                tt(a, a, e, ALU.add)
                tt(e, bi, A[3], ALU.mult)
                tt(a, a, e, ALU.subtract)
                tt(b, sr, A[1], ALU.mult)
                tt(e, si, A[0], ALU.mult)
                tt(b, b, e, ALU.add)
                tt(e, br, A[3], ALU.mult)
                tt(b, b, e, ALU.add)
                takes(v, v.tensor_tensor(e, bi, A[2], ALU.mult), name)
                tt(si, b, e, ALU.add)
                v.tensor_copy(sr, a).then_inc(sem("s_smp"), 1)
                v.wait_ge(sem("s_smp"), l + 1)
                if l:
                    v.wait_ge(sem("s5_out"), 16)
                d(v.tensor_copy(s5o[:, :, :, 1:1 + NB], s5s[:, l]))

            def s5_tile(l, j):
                name = ("bu", l, j)
                ps = filled(v, name)[:, :].rearrange("p (c f t) -> p c f t", c=2, f=2)
                V = [P, 2, 2, HALF]
                cb = bc(cosT[:, j, None, None, :], V)
                sbn = bc(sinT[:, j, :, None, :], V)
                w4 = wrot.rearrange("p c (f t) -> p c f t", f=2)
                t4 = rrot[j % 2].rearrange("p c (f t) -> p c f t", f=2)
                if j >= 2 or l:
                    v.wait_ge(sem("s_back"), JT * l + j - 1)
                tt(w4, ps, cb, ALU.mult)
                takes(v, v.tensor_tensor(t4, ps[:, ::-1], sbn, ALU.mult), name)
                tt(w4, w4, t4, ALU.add)
                decay = bc(c_(1)[:, j:j + 1], [P, HALF])
                for c in range(2):
                    d(v.tensor_tensor_scan(t4[:, c, 0, :], decay, w4[:, c, 0, :], 0.0, ALU.mult, ALU.add))
                last, start, turned = t4[:, :, 0, HALF - 1], ini[:, 0:2], ini[:, 2:4]
                tt(start, last, bc(pw[:, 0, j:j + 1], [P, 2]), ALU.mult)
                tt(turned, last[:, ::-1], pw[:, 1:3, j], ALU.mult)
                tt(start, start, turned, ALU.add)
                d(v.tensor_tensor_scan(t4[:, 0, 1, :], decay, w4[:, 0, 1, :], ini[:, 0:1], ALU.mult, ALU.add))
                v.tensor_tensor_scan(t4[:, 1, 1, :], decay, w4[:, 1, 1, :], ini[:, 1:2],
                                     ALU.mult, ALU.add).then_inc(sem("scanned"), 1)
                v.wait_ge(sem("scanned"), JT * l + j + 1)

            def s5_last(l):
                v.wait_ge(sem("s_back"), JT * (l + 1))
                fr, fi, e = pw[:, 5, :], pw[:, 6, :], sm[:, 18, :]
                tt(e, fi, c_(17), ALU.mult)
                o = s5o[:, :, :, 0]
                tt(o[:, :, 0], fr, c_(16), ALU.mult)
                tt(o[:, :, 0], o[:, :, 0], e, ALU.subtract)
                tt(e, fi, c_(16), ALU.mult)
                tt(o[:, :, 1], fr, c_(17), ALU.mult)
                v.tensor_tensor(o[:, :, 1], o[:, :, 1], e, ALU.add).then_inc(sem("s5o_done"), 1)

            def conv_tile(l, i):
                taken(v, ("in", l, UT + i))
                w = lambda t: col(l, "conv_w", QT * t + i, 1)
                o = cv[:, i, 0:SEQ]
                v.wait_ge(sem("tap_done"), QT * l + i + 1)
                for t in range(1, TAPS):
                    d(v.scalar_tensor_tensor(o, raw[:, i, t:t + SEQ], w(t), o, ALU.mult, ALU.add))

            def conv_samples(l):
                W = [P, QT, NB]
                wv = lambda t: bc(col(l, "conv_w", QT * t, QT)[:, :, None], W)
                o = cv[:, :, SEQ:N]
                e = sx[:, 0, 0:QT * NB].rearrange("p (i b) -> p i b", b=NB)
                if l == 0:
                    v.wait_ge(ld["conv0"], 16)
                tt(o, conv0[:, l, :, :, 0], wv(0), ALU.mult)
                for t in range(1, TAPS):
                    src = conv0[:, l, :, :, t] if t < 3 else raw[:, :, 3 + SEQ:3 + N]
                    tt(e, src, wv(t), ALU.mult)
                    if t < 3:
                        tt(o, o, e, ALU.add)
                if l:
                    v.wait_ge(sem("cv_out"), 16)
                d(v.tensor_copy(cvo[:, :, 0, :], raw[:, :, SEQ:SEQ + 3]))
                d(v.tensor_copy(cvo[:, :, 1:1 + NB, 0:2], conv0[:, l, :, :, 1:3]))
                v.tensor_copy(cvo[:, :, 1:1 + NB, 2], raw[:, :, 3 + SEQ:3 + N]).then_inc(sem("cvo_done"), 1)
                v.wait_ge(sem("cvo_done"), l + 1)
                v.tensor_tensor(o, o, e, ALU.add).then_inc(sem("conv_done"), 1)

            def gate_logits(l):
                name = ("ab", l)
                ps = filled(v, name)[:, 0:24].rearrange("p (g w) -> p g w", w=8)
                if l == 0:
                    d(v.memset(gd[:, :, :], 0.0))
                x, ax, be = (gd[:, i, :].rearrange("p (g h) -> p g h", h=NH) for i in (2, 1, 4))
                bias = col(l, "dt_bias")
                for g0, g1, m in ((0, 2, P), (2, 3, NB)):
                    tt(x[0:m, g0:g1], ps[0:m, g0:g1, 0:NH], bc(bias[0:m, None, :], [m, g1 - g0, NH]), ALU.add)
                d(v.tensor_copy(be[:, 0:2], ps[:, 0:2, NH:]))
                takes(v, v.tensor_copy(be[0:NB, 2:3], ps[0:NB, 2:3, NH:]), name)
                ts(ax, x, -1.0, None, ALU.mult)
                v.tensor_tensor(ax, ax, x, ALU.max).then_inc(sem("ax_done"), 1)

            def gdn_columns(l):
                g3 = [P, 3, NH]
                r = lambda i: gd[:, i, :].rearrange("p (g h) -> p g h", h=NH)
                v.wait_ge(sem("a_ln"), 3 * (l + 1))
                ts(r(2), r(2), 0.0, None, ALU.max)
                tt(r(2), r(2), r(1), ALU.add)
                ts(gd[:, 3, 0:NH], gd[:, 3, 0:NH], -1.0, None, ALU.mult)
                v.tensor_tensor(r(0), r(2), bc(gd[:, 3, None, 0:NH], g3), ALU.mult).then_inc(sem("g_done"), 1)

            def qk_norms(l):
                v.wait_ge(sem("s5_free"), l + 1)
                for i in range(2 * NH):
                    name = ("qkn", l, i)
                    takes(v, v.tensor_scalar(nrm[:, i, :], filled(v, name)[:, 0:N], EPS, None, ALU.add), name)
                v.tensor_copy(ini[:, 3:4], nrm[:, 0, 0:1]).then_inc(sem("nrm_ss"), 1)
                v.wait_ge(sem("nrm_root"), l + 1)
                d(v.reciprocal(nrm[:, :, :], nrm[:, :, :]))
                q, k = cv[:, 0:NH, :], cv[:, NH:2 * NH, :]
                v.wait_ge(sem("cv_silu"), 3 * (l + 1))
                d(v.scalar_tensor_tensor(q, q, HD ** -0.5, nrm[:, 0:NH, :], ALU.mult, ALU.mult))
                v.tensor_tensor(k, k, nrm[:, NH:2 * NH, :], ALU.mult).then_inc(sem("qk_done"), 1)
                v.wait_ge(sem("qk_done"), l + 1)

            def gdn(l, fill):
                H4 = [P, NH, P]
                name = ("gcc", l)
                gc = gd[:, 5, 0:8]
                takes(v, v.tensor_copy(gc, filled(v, name)[:, 0:8]), name)
                psb = [filled(v, ("gcb", l, c))[:, :].rearrange("p (h t) -> p h t", h=NH) for c in range(NC)]
                c4 = lambda i, c: gd[:, i, 4 * c:4 * c + 4]
                for c in range(NC):
                    d(v.tensor_copy(c4(7, c), c4(5, c)))
                    d(v.tensor_copy(c4(9, c), psb[c][:, :, P - 1]))
                    tt(c4(8, c), c4(9, c), c4(5, c), ALU.subtract)
                v.tensor_copy(ini[:, 3:4], gd[:, 8, 0:1]).then_inc(sem("gdx_done"), 1)
                for c in range(NC):
                    bank_t = psb[c]
                    col_t = bc(c4(5, c)[:, :, None], H4)
                    tt(mats["decT"][c], bank_t, col_t, ALU.subtract)
                    ts(mats["dec"][c], mats["decT"][c], -1.0, 0.0, ALU.mult, ALU.min)
                    v.tensor_scalar(mats["decT"][c], mats["decT"][c], 0.0, None, ALU.min).then_inc(sem("diff_done"), 1)
                v.wait_ge(sem("a_col"), 2 * (l + 1))
                tt(gd[:, 10, 0:8], gd[:, 7, 0:8], gd[:, 4, 0:8], ALU.mult)
                for c in range(NC):
                    v.wait_ge(sem("a_dec"), 2 * NC * l + 2 * c + 2)
                    tt(mats["decT"][c], mats["decT"][c], bc(upper[:, None, :], H4), ALU.mult)
                    tt(mats["dec"][c], mats["dec"][c], bc(strict[:, None, :], H4), ALU.mult)
                    tt(mats["dec"][c], mats["dec"][c], bc(c4(4, c)[:, :, None], H4), ALU.mult)
                    name = ("ktok", l, c)
                    ps = filled(v, name)[:, :].rearrange("p (h t) -> p h t", h=NH)
                    tt(mats["kg"][c], ps, bc(c4(8, c)[:, :, None], H4), ALU.mult)
                    takes(v, v.tensor_tensor(mats["kbg"][c], ps, bc(c4(10, c)[:, :, None], H4), ALU.mult), name)
                    name = ("kk", l, c)
                    ps = filled(v, name)[:, :].rearrange("p (h t) -> p h t", h=NH)
                    takes(v, v.tensor_tensor(mats["ln"][c], ps, mats["dec"][c], ALU.mult), name)
                    v.tensor_scalar(mats["ln"][c], mats["ln"][c], -1.0, None, ALU.mult).then_inc(sem("ln_done"), 1)
                    v.wait_ge(sem("ln_done"), NC * l + c + 1)
                    name = ("qk", l, c)
                    ps = filled(v, name)[:, :].rearrange("p (h t) -> p h t", h=NH)
                    takes(v, v.tensor_tensor(mats["att"][c], ps, mats["decT"][c], ALU.mult), name)
                    taken(v, ("gcb", l, c))
                    v.tensor_tensor(mats["qg"][c], mats["qg"][c], cv[:, 0:NH, P * c:P * c + P],
                                    ALU.mult).then_inc(sem("qg_done"), 1)
                fill(3)
                for c in range(NC):
                    name = ("lt", l, c)
                    ps = filled(v, name)[:, :].rearrange("p (h t) -> p h t", h=NH)
                    tt(mats["e"][c], mats["ln"][c], bc(blk[:, None, :], H4), ALU.mult)
                    takes(v, v.tensor_copy(mats["lnT"][c], ps), name)
                    tt(mats["p"][c], mats["e"][c], bc(ident[:, None, :], H4), ALU.add)
                    tt(mats["eT"][c], mats["lnT"][c], bc(blkT[:, None, :], H4), ALU.mult)
                    v.tensor_tensor(mats["pT"][c], mats["eT"][c], bc(ident[:, None, :], H4),
                                    ALU.add).then_inc(sem("e_done"), 1)
                    v.wait_ge(sem("e_done"), NC * l + c + 1)
                    name = ("vtok", l, c)
                    ps = filled(v, name)[:, :].rearrange("p (h t) -> p h t", h=NH)
                    takes(v, v.tensor_tensor(mats["vb"][c], ps, bc(c4(4, c)[:, :, None], H4), ALU.mult), name)
                fill(4)
                for s in range(3):
                    fill(5 + 2 * s)
                    for c in range(NC):
                        filled(v, ("pT", l, s, c))
                        for n in ("p", "pT"):
                            name = (n, l, s, c)
                            ps = filled(v, name)[:, :].rearrange("p (h t) -> p h t", h=NH)
                            takes(v, v.tensor_tensor(mats[n][c], mats[n][c], ps, ALU.add), name)
                    fill(6 + 2 * s)
                for s in range(3):
                    for c in range(NC):
                        v.tensor_tensor(mats["eT"][c], mats["lnT"][c], bc(masks[:, 5 + s, None, :], H4),
                                        ALU.mult).then_inc(sem("lev_done"), 1)
                    fill(11 + 2 * s)
                    for c in range(NC):
                        filled(v, ("xT", l, s, c))
                        for n, m in (("p", "x"), ("pT", "xT"))[s == 2:]:
                            name = (m, l, s, c)
                            ps = filled(v, name)[:, :].rearrange("p (h t) -> p h t", h=NH)
                            takes(v, v.tensor_tensor(mats[n][c], mats[n][c], ps, ALU.add), name)
                    fill(12 + 2 * s)
                fill(17)
                for c in range(NC):
                    fill(18 + c)
                    name = ("s", l, c)
                    if c == 0:
                        ps = filled(v, name)[:, :].rearrange("p (h t) -> p h t", h=NH)
                        takes(v, v.tensor_copy(s_pr, ps), name)
                    else:
                        ps = filled(v, name)[:, :].rearrange("p (h t) -> p h t", h=NH)
                        tt(s_pr, s_pr, bc(c4(9, c)[:, :, None], H4), ALU.mult)
                        takes(v, v.tensor_tensor(s_pr, s_pr, ps, ALU.add), name)

            def gdn_samples(l, fill):
                hb = NH * NB
                W = [NB, NH, NB]
                v.wait_ge(sem("a_col"), 2 * (l + 1))
                idb = bc(ident[0:NB, None, 0:NB], W)
                tt(dg[:, 0], bc(gd[0:NB, 11, 8:12, None], W), idb, ALU.mult)
                v.tensor_tensor(dg[:, 1], bc(gd[0:NB, 4, 8:12, None], W), idb, ALU.mult).then_inc(sem("dg_done"), 1)
                q, k, vv = (cv[:, NH * i:NH * i + NH, SEQ:N] for i in range(3))
                r = lambda ap: ap.rearrange("p (h b) -> p h b", b=NB)
                d(v.tensor_copy(r(sx[:, 2, 0:hb]), k))
                v.tensor_tensor(r(sx[:, 0, 0:hb]), q, k, ALU.mult).then_inc(sem("qkp_done"), 1)
                name = ("skt", l)
                takes(v, v.tensor_copy(ktk[:, :], filled(v, name)[0:hb, 0:P]), name)
                name = ("sgb", l)
                takes(v, v.tensor_copy(rowb[:, :, :].rearrange("p a b -> p (a b)"), filled(v, name)[:, 0:2 * hb]), name)
                eg, be = rowb[:, 0, :], rowb[:, 1, :]
                fill(20)
                name = ("skq", l)
                ps = filled(v, name)[:, 0:2 * hb].rearrange("p (i c) -> p i c", c=2)
                vn, t, o = sx[:, 1, 0:hb], sx[:, 2, 0:hb], sx[:, 3, 0:hb]
                tt(t, ps[:, :, 1], eg, ALU.mult)
                takes(v, v.tensor_tensor(o, ps[:, :, 0], eg, ALU.mult), name)
                tt(r(vn), vv, r(t), ALU.subtract)
                v.tensor_tensor(vn, vn, be, ALU.mult).then_inc(sem("svn_done"), 1)
                v.wait_ge(sem("svn_done"), l + 1)
                name = ("sqk", l)
                takes(v, v.tensor_tensor(t, filled(v, name)[:, 0:hb], vn, ALU.mult), name)
                v.tensor_tensor(oT[:, :, SEQ:N], r(o), r(t), ALU.add).then_inc(sem("os_done"), 1)
                name = ("svt", l)
                ps = filled(v, name)[0:hb, None, 0:P]
                gives(v.tensor_tensor(vm[0:hb], bc(ps, [hb, hb, P]), bc(ident[0:hb, 0:hb, None], [hb, hb, P]),
                                      ALU.mult), name)
                taken(v, name)
                v.tensor_copy(ini[:, 3:4], eg[:, 0:1]).then_inc(sem("vm_done"), 1)
                d(v.tensor_tensor(s0, s0, bc(eg[:, :, None], [P, hb, P]), ALU.mult))
                fill(21)
                for i in range(NB):
                    name = ("so", l, i)
                    ps = filled(v, name)[:, :].rearrange("p (a b) -> p a b", b=P)
                    gives(v.tensor_tensor(s0[:, 4 * i:4 * i + 4, :], s0[:, 4 * i:4 * i + 4, :], ps, ALU.add), name)

            def gdn_output(l, fill):
                for h in range(NH):
                    name = ("on", l, h)
                    takes(v, v.tensor_scalar(onrm[:, h, :], filled(v, name)[:, 0:N], 1.0 / HD, EPS, ALU.mult, ALU.add),
                          name)
                v.tensor_copy(ini[:, 3:4], onrm[:, 0, 0:1]).then_inc(sem("on_ss"), 1)
                v.wait_ge(sem("on_root"), l + 1)
                n4 = onrm
                d(v.reciprocal(n4, n4))
                d(v.scalar_tensor_tensor(oT, oT, col(l, "gdn_w"), n4, ALU.mult, ALU.mult))
                v.tensor_tensor(oT, oT, zs[:, :, :], ALU.mult).then_inc(sem("o_done"), 1)
                fill(22)

            def unit(l, u):
                if u < 2 * KD:
                    return
                m = u - 2 * KD
                taken(v, ("glu", l, 2 * m + 1))
                name = ("glu", l, 2 * m)
                ga = gates[:, m, :]
                takes(v, v.tensor_tensor(ga, ga, filled(v, name)[:, 0:N], ALU.mult), name)
                v.tensor_tensor(ga, ga, tmp[:, m % 2, :], ALU.mult).then_inc(sem("glu_done"), 1)

            def mixer(l):
                def fill(step):
                    for u in units(step):
                        unit(l, u)

                if l == 0:
                    v.wait_ge(ld["cols"], 16)
                    v.wait_ge(ld["x"], 16)
                    s5_decay(0)
                    s5_rotation(0)
                    s5_gain(0)
                    ada_mod(0, 0)
                norm(l, "mix", "g_mix", 0)
                gate_logits(l)
                v.wait_ge(sem("tab_done"), l + 1)
                s5_samples(l)
                ends = ada_ends(l)
                for j in range(S5_STEPS):
                    s5_tile(l, j)
                    if j < QT:
                        conv_tile(l, j)
                    elif j == QT:
                        conv_samples(l)
                    if j - 1 in ends:
                        ada_mod(*ADA_IN[l][ends.index(j - 1)])
                    if j in Y_AFTER:
                        s5_output(l, Y_AFTER.index(j))
                ada_mod(*ADA_IN[l][-1])
                s5_output(l, UT - 1)
                s5_last(l)
                v.tensor_copy(ini[:, 3:4], s5o[:, 0, 0, 0:1]).then_inc(sem("s5_free"), 1)
                gdn_columns(l)
                fill(0)
                fill(1)
                qk_norms(l)
                fill(2)
                gdn(l, fill)
                v.tensor_copy(ini[:, 3:4], s_pr[:, 0, 0:1]).then_inc(sem("sp_done"), 1)
                gdn_samples(l, fill)
                gdn_output(l, fill)
                v.wait_ge(sem("glu_done"), KD * (l + 1))
                for m in range(KD):
                    name = ("go", l, m)
                    takes(v, v.tensor_tensor(hT[:, m, :], gates[:, KD + m, :], filled(v, name)[:, 0:N], ALU.mult), name)
                    v.tensor_tensor(hT[:, m, :], hT[:, m, :], gates[:, m, :], ALU.add).then_inc(sem("merged"), 1)
                residual(lambda m: (filled(v, ("wo", l, m)), lambda ins: gives(ins, ("wo", l, m))), 16, "x_mix", mods[:, l])

            def residual(src, at, done, mod, tiles=range(KD)):
                for m in tiles:
                    ps, mark = src(m)
                    e = tmp[:, 0, 0:NB]
                    d(v.tensor_tensor(e, ps[:, SEQ:N], mod[:, at + m, 1:1 + NB], ALU.mult))
                    d(v.tensor_tensor(xT[:, m, SEQ:N], xT[:, m, SEQ:N], e, ALU.add))
                    ins = v.scalar_tensor_tensor(xT[:, m, 0:SEQ], ps[:, 0:SEQ], mod[:, at + m, 0:1], xT[:, m, 0:SEQ],
                                                 ALU.mult, ALU.add)
                    mark(ins)
                    v.tensor_copy(ini[:, 3:4], mod[:, at + m, 0:1]).then_inc(sem(done), 1)

            def s5_output(l, i):
                name = ("y", l, i)
                ps = filled(v, name)[:, 0:N]
                gives(v.scalar_tensor_tensor(uT[:, i, :], uT[:, i, :], col(l, "s5_d", i, 1), ps, ALU.mult, ALU.add), name)
                taken(v, name)
                v.tensor_copy(ini[:, 3:4], uT[:, i, 0:1]).then_inc(sem("y_sum"), 1)

            def route():
                lg = rtx[:, 0:3, :]
                d(v.memset(rtx[:, :, :], 0.0))
                d(v.memset(pick[:, :, :, :], -1.0))
                d(v.memset(dcT, 0.0))
                d(v.memset(acc, 0.0))
                name = ("rl",)
                ps = filled(v, name)[:, 0:24].rearrange("p (g e) -> p g e", e=NE)
                br = col(1, "b_router")
                tt(lg[:, 0:2], ps[:, 0:2], bc(br[:, None, :], [P, 2, NE]), ALU.add)
                takes(v, v.tensor_tensor(lg[0:NB, 2:3], ps[0:NB, 2:3], bc(br[0:NB, None, :], [NB, 1, NE]), ALU.add), name)
                v.wait_ge(ld["sel"], 16)
                W = [P, 3, NE, NE]
                before, same = ar(at_e, 3, NE, NE), ar(at_e + CH, 3, NE, NE)
                mine, other = bc(lg[:, :, :, None], W), bc(lg[:, :, None, :], W)
                tt(before, other, mine, ALU.is_gt)
                tt(same, other, mine, ALU.is_equal)
                tt(same, same, bc(selw[:, None, :, :], W), ALU.mult)
                tt(before, before, same, ALU.add)
                d(v.tensor_reduce(rtx[:, 3:6, :], before, AX.X, ALU.add))
                d(v.tensor_scalar(rt[:, :, :], rtx[:, 3:6, :], 2.0, None, ALU.is_lt))
                d(v.tensor_reduce(rtx[:, 9, 0:3], lg, AX.X, ALU.max))
                v.tensor_tensor(rtx[:, 6:9, :], lg, bc(rtx[:, 9, 0:3, None], [P, 3, NE]),
                                ALU.subtract).then_inc(sem("sel_done"), 1)
                v.wait_ge(sem("rexp_done"), 1)
                cw = rtx[:, 6:9, :]
                tt(cw, cw, rt[:, :, :], ALU.mult)
                d(v.tensor_reduce(rtx[:, 9, 0:3], cw, AX.X, ALU.add))
                d(v.reciprocal(rtx[:, 9, 0:3], rtx[:, 9, 0:3]))
                tt(cw, cw, bc(rtx[:, 9, 0:3, None], [P, 3, NE]), ALU.mult)
                name = ("rank",)
                ps = filled(v, name)[:, 0:32].rearrange("p (g e) -> p g e", e=NE)
                pos = rtx[:, 3:6, :]
                tt(pos[:, 0:2], ps[:, 0:2], rt[:, 0:2, :], ALU.mult)
                tt(pos[0:NB, 2], ps[0:NB, 2], rt[0:NB, 2, :], ALU.mult)
                ts(pos, pos, -1.0, None, ALU.add)
                d(v.tensor_reduce(rtx[:, 10, 0:1], ps[:, 3], AX.X, ALU.max))
                takes(v, v.tensor_copy(cnt[:, :], rtx[0:1, 10, 0:1]), name)
                d(v.tensor_copy(pick[:, 0, :, 0:NE], pos))
                v.tensor_copy(pick[:, 1, :, 0:NE], cw).then_inc(sem("cnt_done"), 1)
                v.wait_ge(ld["iota"], 16)
                v.wait_ge(sem("cnt_done"), 1)

            class Experts:
                def choose(self, e, a):
                    for t in range(3):
                        m = P if t < 2 else NB
                        p1, c1 = pick[0:m, 0, t, bass.ds(e, 1)], pick[0:m, 1, t, bass.ds(e, 1)]
                        columns = iota[0:m, 0:CAP] if a is None else iota[0:m, bass.ds(a * CAP, CAP)]
                        v.tensor_scalar(dw[0:m, t, :], columns, p1, c1, ALU.is_equal, ALU.mult)
                        ins = v.tensor_scalar(dsel[0:m, t, :], columns, p1, None, ALU.is_equal)
                    ins.then_inc(sem("dsel_done"), 1)

                def gathered(self, half, g):
                    v.wait_ge(sem("gh_done"), g * 2 + (half + 1))
                    i = slice(4 * half, 4 * half + 4)
                    v.tensor_tensor(gl[:, i, :], four(bank[half]), gh[:, i, :].bitcast(F32),
                                    ALU.subtract).then_inc(sem("gl_done"), 1)

                def add(self, m, g):
                    v.wait_ge(sem("down_full"), g * KD + (KD + m + 1))
                    v.tensor_tensor(acc[:, m, :], acc[:, m, :], bank[4 + m % 2][:, 0:N],
                                    ALU.add).then_inc(sem("down_taken"), 1)

                def begin(self, g, a):
                    for half in range(2):
                        v.memset(bank[6 + half][0:CAP, :], 0.0).then_inc(sem("ye_full"), 1)
                    self.choose(0, a)
                    self.gathered(0, g)
                    self.gathered(1, g)

                def end(self, g):
                    for m in range(KD):
                        self.add(m, g)
                    v.wait_ge(sem("down_taken"), g * KD + 2 * KD)

                def __call__(self, q, g, e, a):
                    expert(self, q, g, e, a)

            four = lambda b: b[:, 0:4 * CAP].rearrange("p (a b) -> p a b", b=CAP)

            def expert(self, q, g, e, a):
                for m in range(FFN_S):
                    low(m, q * FFN_S + (FFN_S + m + 1))
                    for c in silu_after(m):
                        v.wait_ge(sem("silu_done"), q * NCH + (FT + c + 1))
                        v.tensor_tensor(erow[0:CAP, c % 2, :], srow[0:CAP, c % 2, :], bank[2 * (c % 2) + 1][0:CAP, :],
                                        ALU.mult).then_inc(sem("act_done"), 1)
                    for c in turned_after(m):
                        v.wait_ge(sem("eh_done"), q * NCH + (c + 1))
                        i = slice(4 * c, 4 * c + 4)
                        v.tensor_tensor(el[:, i, :], four(bank[4 + c % 2]), eh[:, i, :].bitcast(F32),
                                        ALU.subtract).then_inc(sem("turned_done"), 1)
                    if m - LAG in COMBINE:
                        for t in range(2):
                            self.add(2 * (m - LAG - COMBINE[0]) + t, g)
                    if m == UP_S:
                        self.choose(e + 1, a)
                    if m - LAG in GATHER and (m - LAG - GATHER[0]) % 2:
                        self.gathered((m - LAG - GATHER[0]) // 2, g + 1)

            v.memset(ones[:, :], 1.0).then_inc(sem("ones_done"), 1)
            v.wait_ge(ld["masks"], 16)
            mixer(0)
            norm(0, "ffn", "g_ffn", 24)
            v.tensor_copy(ini[:, 3:4], rstd[:, 0:1]).then_inc(sem("act_done"), 1)
            def low(m, count):
                v.wait_ge(sem("hi_done"), count)
                v.tensor_tensor(wlo[:, m % SPL, :], ring[:, (low.base + m) % RING, :], whi[:, m % SPL, :].bitcast(F32),
                                ALU.subtract).then_inc(sem("lo_done"), 1)

            low.base = MIX0_END
            low(0, 1)
            for half in range(2):
                v.wait_ge(sem("hh_done"), half + 1)
                i = slice(4 * half, 4 * half + 4)
                v.tensor_tensor(hl[:, i, :], hT[:, i, :], hh[:, i, :].bitcast(F32),
                                ALU.subtract).then_inc(sem("hl_done"), 1)
            for s in range(1, LAG):
                low(s, s + 1)
            BODY = 4 * RING

            def dense_tile(it, f):
                v.wait_ge(sem("silu_done"), it * (BODY // 2) + (f + 1))
                v.tensor_tensor(sg[:, f % 2, :], sg[:, f % 2, :], bank[2 * (f % 2) + 1][:, 0:N],
                                ALU.mult).then_inc(sem("act_done"), 1)
                v.wait_ge(sem("ah_done"), it * (BODY // 2) + (f + 1))
                i = bass.ds(it * (BODY // 2) + f, 1)
                v.tensor_tensor(alo[:, i, :], sg[:, f % 2:f % 2 + 1, :], ahi[:, i, :].bitcast(F32),
                                ALU.subtract).then_inc(sem("al_done"), 1)

            with v.Fori(0, UP_S // BODY) as it:
                for s in range(BODY):
                    low(s + LAG, it * BODY + (s + LAG + 1))
                    if s >= 2 and s % 2 == 0:
                        dense_tile(it, s // 2 - 1)
                dense_tile(it, BODY // 2 - 1)

            def down(m):
                v.wait_ge(sem("down_full"), m + 1)
                return bank[4 + m % 2], lambda ins: ins.then_inc(sem("down_taken"), 1)

            done = 0
            for s in range(UP_S + LAG, FFN_S):
                low(s, s + 1)
                if s == UP_S + 6:
                    s5_decay(1)
                if s == UP_S + 13:
                    s5_rotation(1)
                if s == UP_S + 20:
                    s5_gain(1)
                while done < KD and (FT * (done + 1) - 1) // SLOT + SPL <= s - UP_S:
                    residual(down, 40, "x_ffn", mods[:, 0], [done])
                    done += 1
            residual(down, 40, "x_ffn", mods[:, 0], range(done, KD))
            low.base = MIX1_END
            mixer(1)
            norm(1, "ffn", "g_ffn", 24)
            route()
            rounds_of(v, Experts())

            def summed(m):
                return acc[:, m, :], lambda ins: None

            residual(summed, 40, "x_ffn", mods[:, 1])
            v.wait_ge(sem("end_full"), 1)
            d(mean_root(bank[0], 4, D))
            v.tensor_copy(ini[:, 3:4], ssb[:, 0:1]).then_inc(sem("ss_done"), 1)
            v.wait_ge(sem("root_done"), 5)
            d(v.reciprocal(rstd[:, :], rstd[:, :]))
            for k in range(KD):
                v.scalar_tensor_tensor(hT[:, k, :], xT[:, k, :], col(0, "g_final", k, 1), rstd[:, :],
                                       ALU.mult, ALU.mult).then_inc(sem("y_done"), 1)

        @block.gpsimd
        def _(pool):
            pool.memset(cT[:, :, :], 0.0).then_inc(sem("c_zero"), 1)

            def p(ins):
                then(pool, ins, "p")

            def tables(l):
                pool.wait_ge(sem("rot_done"), l + 1)
                cd, ms, sd, t1, t2 = (pw[:, i, :] for i in range(5))
                p(pool.tensor_copy(cd, sm[:, 5, :]))
                p(pool.tensor_copy(sd, sm[:, 6, :]))
                p(pool.memset(cosT[:, :, 0:1], 1.0))
                p(pool.memset(sinT[:, :, :, 0:1], 0.0))
                n = 1
                while n < HALF:
                    W = [P, JT, n]
                    c, s = cosT[:, :, 0:n], sinT[:, :, 0, 0:n]
                    co, so, x = cosT[:, :, n:2 * n], sinT[:, :, 0, n:2 * n], sinT[:, :, 1, n:2 * n]
                    cb, sbb = cd[:, :, None].broadcast_to(W), sd[:, :, None].broadcast_to(W)
                    p(pool.tensor_tensor(co, c, cb, ALU.mult))
                    p(pool.tensor_tensor(x, s, sbb, ALU.mult))
                    p(pool.tensor_tensor(co, co, x, ALU.subtract))
                    p(pool.tensor_tensor(so, s, cb, ALU.mult))
                    p(pool.tensor_tensor(x, c, sbb, ALU.mult))
                    p(pool.tensor_tensor(so, so, x, ALU.add))
                    p(pool.tensor_tensor(t1, cd, cd, ALU.mult))
                    p(pool.tensor_tensor(t2, sd, sd, ALU.mult))
                    p(pool.tensor_tensor(sd, sd, cd, ALU.mult))
                    p(pool.tensor_tensor(cd, t1, t2, ALU.subtract))
                    p(pool.tensor_scalar(sd, sd, 2.0, None, ALU.mult))
                    n *= 2
                p(pool.tensor_scalar(ms, sd, -1.0, None, ALU.mult))
                pool.tensor_scalar(sinT[:, :, 1, :], sinT[:, :, 0, :], -1.0, None, ALU.mult).then_inc(sem("tab_done"), 1)

            def layer(l):
                if l:
                    pool.wait_ge(sem("x_ffn"), KD)
                pool.memset(raw[:, :, 0:3], 0.0).then_inc(sem("pool_zero"), 1)
                tables(l)
                for j in range(JT):
                    pool.wait_ge(sem("scanned"), JT * l + j + 1)
                    if j >= 8:
                        filled(pool, ("y", l, j // 4 - 2))
                    V = [P, 2, 2, HALF]
                    r4, s4, p4 = (t.rearrange("p c (f t) -> p c f t", f=2) for t in (rrot[j % 2], st[:, j % 8], prot))
                    for c in range(2):
                        cb = cosT[:, j, None, :].broadcast_to([P, 2, HALF])
                        sb_ = sinT[:, j, c, None, :].broadcast_to([P, 2, HALF])
                        p(pool.tensor_tensor(p4[:, c], r4[:, c], cb, ALU.mult))
                        p(pool.tensor_tensor(s4[:, c], r4[:, 1 - c], sb_, ALU.mult))
                    p(pool.tensor_tensor(st[:, j % 8], prot, st[:, j % 8], ALU.subtract))
                    pool.tensor_copy(pw[:, 5:7, j], st[:, j % 8, :, SEQ - 1]).then_inc(sem("s_back"), 1)
                    if j == QT + 1:
                        pool.wait_ge(sem("cvo_done"), l + 1)
                        pool.dma_start(conv_out[l], cvo[:, :, :, :]).then_inc(sem("cv_out"), 16)
                pool.wait_ge(sem("s5o_done"), l + 1)
                pool.dma_start(s5_out[l], s5o[:, :, :, :]).then_inc(sem("s5_out"), 16)
                pool.wait_ge(sem("sp_done"), l + 1)
                pool.dma_start(gdnp_out[l], s_pr).then_inc(sem("sp_out"), 16)
                for i in range(NB):
                    taken(pool, ("so", l, i))
                pool.dma_start(gdns_out[l], s0).then_inc(sem("gs_out"), 16)
                pool.wait_ge(sem("gs_out"), 16 * (l + 1))

            layer(0)
            layer(1)
            for n in ("cv_out", "s5_out", "sp_out"):
                pool.wait_ge(sem(n), 32)


def _blocks(w):
    K, M = w.shape
    return w.reshape(K // P, P, M // P, P).transpose(2, 0, 1, 3)


def _slots(blocks):
    n = blocks.shape[0]
    return blocks.reshape(n // SLOT, SLOT, P, P).transpose(0, 2, 1, 3).reshape(n // SLOT, P, SLOT * P)


def _flat(tiles):
    return tiles.reshape(-1, P, P)


def _pairs(w):
    b = _blocks(w)
    h = b.shape[0] // 2
    return _flat(np.stack([b[:h], b[h:]], axis=1))


def _fm(a):
    r, f = a.shape
    return a.T.reshape(f // P, P, r).transpose(1, 0, 2)


def _const():
    i = np.arange(P)
    r, c = i[:, None], i[None, :]
    m = {"ident": r == c, "upper": r <= c, "strict": r > c}
    m["blk"] = (r > c) & (r // BASE == c // BASE)
    m["blkT"] = m["blk"].T
    for s in range(3):
        b = BASE << s
        m[f"lev{s}"] = (r // (2 * b) == c // (2 * b)) & (r // b % 2 == 0) & (c // b % 2 == 1)
    masks = np.stack([m[n] for n in MASKS], axis=1).astype(np.float32)
    iota = np.broadcast_to(np.arange(PASSES * CAP, dtype=np.float32), (P, PASSES * CAP)).copy()
    sel = np.broadcast_to((np.arange(NE)[None, :] < np.arange(NE)[:, None]).astype(np.float32), (P, NE, NE)).copy()
    return masks, iota, sel


def layouts(i):
    L = range(DEPTH)
    x = np.concatenate([i["x_prompt"][0], i["x_sample"][:, 0]], axis=0)
    c = np.concatenate([i["c_prompt"], i["c_sample"]], axis=0)
    masks, iota, sel = _const()
    feat = lambda v: v.reshape(-1, P).T
    row = lambda v: np.broadcast_to(v[None, :], (P, v.shape[0]))
    cols = []
    for l in L:
        dt = np.repeat(i["s5_log_dt"][l], ST)
        parts = dict(g_mix=feat(i["g_mix"][l]), g_ffn=feat(i["g_ffn"][l]), b_ada=feat(i["b_ada"][l]),
                     s5_d=feat(i["s5_d"][l]), conv_w=feat(i["gdn_conv_w"][l].reshape(-1)),
                     gdn_w=i["gdn_norm_w"][l][:, None], lam_re=feat(i["s5_lambda_re"][l].reshape(-1)),
                     lam_im=feat(i["s5_lambda_im"][l].reshape(-1)), log_dt=feat(dt), a_log=row(i["gdn_a_log"][l]),
                     dt_bias=row(i["gdn_dt_bias"][l]), g_final=feat(i["g_final"]), b_router=row(i["b_router"][0]))
        cols.append(np.concatenate([parts[n] for n in COLS], axis=1))
    cols = np.stack(cols, axis=1)
    bpk = np.zeros((DEPTH, UT, 4, 2, C5, 2, 2, ST), np.float32)
    cpk = np.zeros((DEPTH, 2, ST, JT, 2, 2, C5), np.float32)
    for part, (bn, cn) in enumerate((("s5_b_re", "s5_c_re"), ("s5_b_im", "s5_c_im"))):
        b = i[bn].reshape(DEPTH, UT, 4, 2, ST, C5)
        cc = i[cn].reshape(DEPTH, JT, 2, C5, ST)
        for g in range(2):
            bpk[:, :, :, g, :, part, g, :] = b[:, :, :, g].transpose(0, 1, 2, 4, 3)
            cpk[:, g, :, :, part, g, :] = cc[:, :, g].transpose(0, 3, 1, 2)
    bpk = bpk.reshape(DEPTH, UT, P, 2, P).transpose(0, 2, 1, 3, 4)
    cpk = cpk.reshape(DEPTH, P, JT, 2, 32)
    s5 = np.stack([i["state_s5_re"], i["state_s5_im"]], axis=1).reshape(DEPTH, 2, NB, JT, P).transpose(4, 0, 3, 1, 2)
    gdn = i["state_gdn"].transpose(0, 3, 2, 1, 4).reshape(DEPTH, P, NH * NB, P)
    conv = i["state_conv"].reshape(DEPTH, NB, 3, QT, P).transpose(4, 0, 3, 1, 2)
    ab = S5W + 3 * NH * HD + NH * HD
    wab = np.stack([i["w_in"][l][:, ab:ab + 2 * NH].reshape(KD, P, 2 * NH).transpose(1, 0, 2) for l in L], axis=1)
    wr = i["w_router"][0].reshape(KD, P, NE).transpose(1, 0, 2)
    def ada(l, rd):
        w = i["w_ada"][l][:, 2048 * rd:2048 * rd + 2048]
        return w.reshape(KD, P, 2, 1024).transpose(0, 2, 1, 3).reshape(ADA_S, P, 1024)

    parts = [ada(0, 0)]
    for l in L:
        w = i["w_in"][l]
        w = _slots(_flat(_blocks(np.concatenate([w[:, :ab], w[:, ab + 2 * NH:]], axis=1))))
        glu = _slots(_pairs(i["w_s5_glu"][l]))
        rounds = np.concatenate([ada(*a) for a in ADA_IN[l]], axis=0)
        n = len(ADA_IN[l])
        parts.append(w[:UT])
        for j in range(S5_STEPS):
            parts += [w[UT + j:UT + j + 1], rounds[n * j:n * j + n]]
        parts += [w[UT + S5_STEPS:], glu, _slots(_flat(_blocks(i["w_gdn_out"][l]))), _slots(_flat(_blocks(i["w_out"][l])))]
        if l == 0:
            parts += [_slots(_pairs(i["w_ffn_gate_up"][0])), _slots(_flat(_blocks(i["w_ffn_down"][0])))]
    for e in range(NE):
        parts += [i["w_exp_gate_up"][0, e].reshape(KD, P, 2, NCH, CH).transpose(3, 0, 1, 2, 4).reshape(UP_S, P, 2 * CH),
                  i["w_exp_down"][0, e].reshape(DOWN_S, P, D)]
    w = np.concatenate(parts, axis=0)
    return dict(x=_fm(x), c=_fm(c), cols=cols, masks=masks, iota=iota, sel=sel, bpk=bpk, cpk=cpk, s5s=s5, gdn=gdn,
                conv=conv, wab=wab, wr=wr, w=w)


OUTS = {"y": (P, KD, N), "s5": (DEPTH, P, JT, 2, 1 + NB), "gdnp": (DEPTH, P, NH, P), "gdns": (DEPTH, P, NH * NB, P),
        "convo": (DEPTH, P, QT, 1 + NB, 3)}


def kernel(**inputs):
    import concourse.bacc as bacc
    from concourse.bass_utils import run_bass_kernel_spmd

    nc = bacc.Bacc("TRN2", target_bir_lowering=False, num_devices=1)
    arrays, args = {}, []
    for name, a in layouts({k: np.asarray(v) for k, v in inputs.items()}).items():
        a = np.ascontiguousarray(a)
        arrays[f"in_{name}"] = a
        args.append(nc.dram_tensor(f"in_{name}", a.shape, F32, kind="ExternalInput").ap())
    for name, shape in OUTS.items():
        args.append(nc.dram_tensor(f"out_{name}", shape, F32, kind="ExternalOutput").ap())
    trunk_program(nc, *args)
    r = run_bass_kernel_spmd(nc, [arrays], core_ids=[0]).results[0]
    y = r["out_y"].transpose(2, 1, 0).reshape(N, D)
    s5 = r["out_s5"].transpose(0, 3, 4, 2, 1).reshape(DEPTH, 2, 1 + NB, G5, ST)
    gp = r["out_gdnp"].transpose(0, 2, 1, 3)[:, None]
    gs = r["out_gdns"].reshape(DEPTH, P, NH, NB, P).transpose(0, 3, 2, 1, 4)
    cv = r["out_convo"].transpose(0, 3, 4, 2, 1).reshape(DEPTH, 1 + NB, 3, QT * P)
    out = (y[None, :SEQ], y[SEQ:, None], s5[:, 0, :1], s5[:, 1, :1], gp, cv[:, :1], s5[:, 0, 1:], s5[:, 1, 1:], gs,
           cv[:, 1:])
    return tuple(np.ascontiguousarray(a) for a in out)
```
